# Optimizing a Trainium2 kernel written in Bass

```python
import math
import jax, jax.numpy as jnp
from jax import lax
import numpy as np

D_MODEL = 1024
BATCH = 1
SEQ = 2048
DEPTH = 1
DEC_BATCH = 8
DEC_SEQ = 8
PAST_LEN = 16384
PAGE_SIZE = 128

MIX_WIDTH = D_MODEL
CONV_DIM = MIX_WIDTH // 2
CONV_GROUPS = 8
CONV_W = 3
HGRN_DIM = MIX_WIDTH - CONV_DIM
HGRN_HEAD_DIM = 128
HGRN_HEADS = HGRN_DIM // HGRN_HEAD_DIM
HGRN_CHUNK = 64
IN_PROJ_DIM = 3 * CONV_DIM + 4 * HGRN_DIM
N_GROUPS = 4
EXPERTS_PER_GROUP = 8
N_EXPERTS = N_GROUPS * EXPERTS_PER_GROUP
TOP_K = 2
D_EXPERT = D_MODEL // 4
MOE_BLOCK = 128
LN_EPS = 1e-5
RMS_EPS = 1e-6
DEEPNORM_ALPHA = (2 * DEPTH) ** 0.25
DEEPNORM_BETA = (8 * DEPTH) ** -0.25

kernel_name = "hymba_conv_hgrn2_hmoe_deepnorm_step"

def _layer_norm(x, g, b):
    xf = x.astype(jnp.float32)
    mu = jnp.mean(xf, axis=-1, keepdims=True)
    var = jnp.mean(jnp.square(xf - mu), axis=-1, keepdims=True)
    return ((xf - mu) * lax.rsqrt(var + LN_EPS)).astype(x.dtype) * g + b

def _short_conv_mixer(xb, xc, xv, buf, conv_w):
    L = xv.shape[1]
    v = xc * xv
    vp = jnp.concatenate([buf.astype(v.dtype), v], axis=1)
    y = sum(conv_w[j] * vp[:, j:j + L] for j in range(CONV_W))
    return xb * y, vp[:, L:]

def _gla_chunked(q, k, v, log_f, s0):
    B, L, H, K = q.shape
    V = v.shape[-1]
    C = math.gcd(L, HGRN_CHUNK)
    n = L // C

    def to_chunks(t):
        return t.reshape(B, n, C, H, t.shape[-1]).transpose(1, 0, 3, 2, 4)

    causal = jnp.tril(jnp.ones((C, C), dtype=bool))[:, :, None]

    def step(s, inp):
        qc, kc, vc, gc = inp
        b = jnp.cumsum(gc, axis=2)
        diff = b[:, :, :, None, :] - b[:, :, None, :, :]
        decay = jnp.where(causal, jnp.exp(jnp.where(causal, diff, 0.0)), 0.0)
        a = jnp.einsum("bhtk,bhtsk,bhsk->bhts", qc, decay, kc)
        o = jnp.einsum("bhts,bhsv->bhtv", a, vc) + jnp.einsum("bhtk,bhkv->bhtv", qc * jnp.exp(b), s)
        b_end = b[:, :, -1:, :]
        s = jnp.exp(b_end[:, :, 0, :, None]) * s + jnp.einsum("bhsk,bhsv->bhkv", kc * jnp.exp(b_end - b), vc)
        return s, o

    s, o = lax.scan(step, s0, (to_chunks(q), to_chunks(k), to_chunks(v), to_chunks(log_f)))
    return o.transpose(1, 0, 3, 2, 4).reshape(B, L, H, V), s

def _hgrn2_mixer(q, f, i, g, s0, lb, gnorm_w):
    B, L, _ = q.shape
    H, K = HGRN_HEADS, HGRN_HEAD_DIM
    qh = (jax.nn.silu(q.astype(jnp.float32)) * K ** -0.5).reshape(B, L, H, K)
    zf = f.astype(jnp.float32).reshape(B, L, H, K)
    lbh = lb.astype(jnp.float32).reshape(H, K)
    f_gate = lbh + (1.0 - lbh) * jax.nn.sigmoid(zf)
    log_f = jnp.log(f_gate)
    kh = (1.0 - lbh) * jax.nn.sigmoid(-zf)
    vh = i.astype(jnp.float32).reshape(B, L, H, K)
    o, s = _gla_chunked(qh, kh, vh, log_f, s0.astype(jnp.float32))
    o = o * lax.rsqrt(jnp.mean(jnp.square(o), axis=-1, keepdims=True) + RMS_EPS)
    o = o * gnorm_w.astype(jnp.float32) * jax.nn.silu(g.astype(jnp.float32)).reshape(B, L, H, K)
    return o.reshape(B, L, HGRN_DIM).astype(q.dtype), s.astype(s0.dtype)

def _grouped_experts(xt, eid, wts, w_gate, w_up, w_down):
    T, D = xt.shape
    S = T * TOP_K
    e = eid.reshape(-1)
    tok = jnp.arange(S, dtype=jnp.int32) // TOP_K
    order = jnp.argsort(e)
    e_sorted = e[order]
    counts = jnp.zeros((N_EXPERTS,), jnp.int32).at[e].add(1)
    padded = (counts + MOE_BLOCK - 1) // MOE_BLOCK * MOE_BLOCK
    start = jnp.cumsum(counts) - counts
    pad_end = jnp.cumsum(padded)
    pad_start = pad_end - padded
    dest = pad_start[e_sorted] + jnp.arange(S, dtype=jnp.int32) - start[e_sorted]
    n_blk = -(-(S + N_EXPERTS * (MOE_BLOCK - 1)) // MOE_BLOCK)
    P = n_blk * MOE_BLOCK
    buf_tok = jnp.full((P,), T, jnp.int32).at[dest].set(tok[order])
    xb = jnp.concatenate([xt, jnp.zeros((1, D), xt.dtype)], axis=0)[buf_tok].reshape(n_blk, MOE_BLOCK, D)
    blk_start = jnp.arange(n_blk, dtype=jnp.int32) * MOE_BLOCK
    blk_e = jnp.minimum(jnp.sum(pad_end[None, :] <= blk_start[:, None], axis=1), N_EXPERTS - 1)

    def expert_block(args):
        xblk, ex = args
        h = jax.nn.silu(xblk @ w_gate[ex]) * (xblk @ w_up[ex])
        return h @ w_down[ex]

    yb = lax.map(expert_block, (xb, blk_e)).reshape(P, D)
    y_slot = jnp.zeros((S, D), yb.dtype).at[order].set(yb[dest])
    return jnp.einsum("tkd,tk->td", y_slot.reshape(T, TOP_K, D), wts.astype(y_slot.dtype))

def _hier_moe(u, w_rg, w_re, w_e_gate, w_e_up, w_e_down):
    B, L, D = u.shape
    xt = u.reshape(B * L, D)
    T = xt.shape[0]
    p_group = jax.nn.softmax((xt @ w_rg).astype(jnp.float32), axis=-1)
    grp = jnp.argmax(p_group, axis=-1).astype(jnp.int32)
    p_sel = jnp.take_along_axis(p_group, grp[:, None], axis=-1)
    logit_e = (xt @ w_re).astype(jnp.float32).reshape(T, N_GROUPS, EXPERTS_PER_GROUP)
    le = jnp.take_along_axis(logit_e, grp[:, None, None], axis=1)[:, 0]
    top_p, top_i = lax.top_k(jax.nn.softmax(le, axis=-1), TOP_K)
    wts = p_sel * top_p / jnp.sum(top_p, axis=-1, keepdims=True)
    eid = grp[:, None] * EXPERTS_PER_GROUP + top_i.astype(jnp.int32)
    return _grouped_experts(xt, eid, wts, w_e_gate, w_e_up, w_e_down).reshape(B, L, D)

def _trunk_layer(x, mod, conv_buf, s0, lb, w_in, conv_w, gnorm_w, w_out, ln_g, ln_b,
                 w_rg, w_re, w_e_gate, w_e_up, w_e_down):
    shift1, scale1, gate1, shift2, scale2, gate2 = jnp.split(mod[:, None, :], 6, axis=-1)
    u = x * (1.0 + scale1) + shift1
    p = u @ w_in
    cuts = [CONV_DIM, 2 * CONV_DIM, 3 * CONV_DIM, 3 * CONV_DIM + HGRN_DIM,
            3 * CONV_DIM + 2 * HGRN_DIM, 3 * CONV_DIM + 3 * HGRN_DIM]
    cb, cc, cv, q, f, i, g = jnp.split(p, cuts, axis=-1)
    y_conv, new_buf = _short_conv_mixer(cb, cc, cv, conv_buf, conv_w)
    y_rec, new_s = _hgrn2_mixer(q, f, i, g, s0, lb, gnorm_w)
    mix = jnp.concatenate([y_conv, y_rec], axis=-1) @ w_out
    x = _layer_norm(DEEPNORM_ALPHA * x + gate1 * mix, ln_g[0], ln_b[0])
    u = x * (1.0 + scale2) + shift2
    y_moe = _hier_moe(u, w_rg, w_re, w_e_gate, w_e_up, w_e_down)
    x = _layer_norm(DEEPNORM_ALPHA * x + gate2 * y_moe, ln_g[1], ln_b[1])
    return x, new_buf, new_s

def setup_inputs(seed: int = 0) -> dict:
    key = jax.random.key(seed)
    ks = jax.random.split(key, 20)
    f32 = jnp.float32
    nrm = lambda k, shape, s: jax.random.normal(k, shape, f32) * s
    return {
        "x_prompt": nrm(ks[0], (BATCH, SEQ, D_MODEL), 1.0),
        "x_sample": nrm(ks[1], (DEC_BATCH, DEC_SEQ, D_MODEL), 1.0),
        "state_conv": nrm(ks[2], (DEPTH, DEC_BATCH, CONV_W - 1, CONV_DIM), 1.0),
        "state_hgrn": nrm(ks[3], (DEPTH, DEC_BATCH, HGRN_HEADS, HGRN_HEAD_DIM, HGRN_HEAD_DIM), 0.5),
        "c_prompt": nrm(ks[4], (BATCH, D_MODEL), 1.0),
        "c_sample": nrm(ks[5], (DEC_BATCH, D_MODEL), 1.0),
        "hgrn_lb_logits": nrm(ks[6], (DEPTH, HGRN_DIM), 0.5),
        "w_mod": nrm(ks[7], (DEPTH, D_MODEL, 6 * D_MODEL), 0.5 * D_MODEL ** -0.5),
        "b_mod": nrm(ks[8], (DEPTH, 6 * D_MODEL), 0.02),
        "w_in": nrm(ks[9], (DEPTH, D_MODEL, IN_PROJ_DIM), D_MODEL ** -0.5),
        "conv_w": nrm(ks[10], (DEPTH, CONV_W, CONV_DIM), CONV_W ** -0.5),
        "gnorm_w": 1.0 + nrm(ks[11], (DEPTH, HGRN_HEAD_DIM), 0.02),
        "w_out": nrm(ks[12], (DEPTH, MIX_WIDTH, D_MODEL), DEEPNORM_BETA * MIX_WIDTH ** -0.5),
        "ln_g": 1.0 + nrm(ks[13], (DEPTH, 2, D_MODEL), 0.02),
        "ln_b": nrm(ks[14], (DEPTH, 2, D_MODEL), 0.02),
        "w_router_group": nrm(ks[15], (DEPTH, D_MODEL, N_GROUPS), D_MODEL ** -0.5),
        "w_router_expert": nrm(ks[16], (DEPTH, D_MODEL, N_EXPERTS), D_MODEL ** -0.5),
        "w_e_gate": nrm(ks[17], (DEPTH, N_EXPERTS, D_MODEL, D_EXPERT), D_MODEL ** -0.5),
        "w_e_up": nrm(ks[18], (DEPTH, N_EXPERTS, D_MODEL, D_EXPERT), D_MODEL ** -0.5),
        "w_e_down": nrm(ks[19], (DEPTH, N_EXPERTS, D_EXPERT, D_MODEL), DEEPNORM_BETA * D_EXPERT ** -0.5),
    }

def reference(x_prompt, x_sample, state_conv, state_hgrn, c_prompt, c_sample, hgrn_lb_logits,
              w_mod, b_mod, w_in, conv_w, gnorm_w, w_out, ln_g, ln_b,
              w_router_group, w_router_expert, w_e_gate, w_e_up, w_e_down):
    lb_p = jax.nn.softmax(hgrn_lb_logits.astype(jnp.float32), axis=0)
    lower_bounds = jnp.cumsum(lb_p, axis=0) - lb_p[0:1]
    yp, ys = x_prompt, x_sample
    conv_p, hgrn_p, conv_s, hgrn_s = [], [], [], []
    for l in range(DEPTH):
        params = (w_in[l], conv_w[l], gnorm_w[l], w_out[l], ln_g[l], ln_b[l],
                  w_router_group[l], w_router_expert[l], w_e_gate[l], w_e_up[l], w_e_down[l])
        mod_p = jax.nn.silu(c_prompt) @ w_mod[l] + b_mod[l]
        mod_s = jax.nn.silu(c_sample) @ w_mod[l] + b_mod[l]
        zb = jnp.zeros((yp.shape[0], CONV_W - 1, CONV_DIM), yp.dtype)
        zs = jnp.zeros((yp.shape[0], HGRN_HEADS, HGRN_HEAD_DIM, HGRN_HEAD_DIM), yp.dtype)
        yp, cb, sb = _trunk_layer(yp, mod_p, zb, zs, lower_bounds[l], *params)
        ys, cs, ss = _trunk_layer(ys, mod_s, state_conv[l], state_hgrn[l], lower_bounds[l], *params)
        conv_p.append(cb)
        hgrn_p.append(sb)
        conv_s.append(cs)
        hgrn_s.append(ss)
    return (yp, ys, jnp.stack(conv_p), jnp.stack(hgrn_p), jnp.stack(conv_s), jnp.stack(hgrn_s))


_drawn_inputs = setup_inputs


def setup_inputs(seed=0):
    import zlib

    import numpy as np

    out = dict(_drawn_inputs(seed))
    spreads = {}
    factors = {'state_hgrn': 6.848, 'gnorm_w': 112.337, 'state_conv': 4.267}
    for name, (base, spread) in spreads.items():
        noise = np.random.default_rng([zlib.crc32(name.encode()), seed]).standard_normal(out[name].shape)
        drawn = base * np.exp(spread * noise) if base else spread * noise
        out[name] = __import__('jax').numpy.asarray(drawn.astype(out[name].dtype))
    for name, factor in factors.items():
        out[name] = (out[name] * factor).astype(out[name].dtype)
    return out
```

```python
from contextlib import ExitStack

import numpy as np

import concourse.bass as bass
from concourse import mybir

P = 128
D = 1024
KT = D // P
SEQ = 2048
DEC_B = 8
DEC_L = 8
NSAMP = DEC_B * DEC_L
NTOK = SEQ + NSAMP
CONV_DIM = 512
HEADS = 4
CONV_W = 3
SEGS = 4
SP_TOK = SEQ // SEGS
SS_TOK = NSAMP // SEGS
SB = DEC_B // SEGS
TS = SP_TOK + SS_TOK
HALF = TS // 2
CH = 128
NCH = SP_TOK // CH
LEVELS = 7
SLEVELS = 3
XT = SP_TOK // P
NE = 32
NG = 4
EPG = NE // NG
DE = 256
TILES = SEQ // P + 1
CAP = (TILES) * P
RAW = 3
LN_EPS = 1e-5
RMS_EPS = 1e-6
ALPHA = 2.0 ** 0.25
QSCALE = float(P) ** -0.5
BIG = 3.0e38
F32 = mybir.dt.float32
F32R = mybir.dt.float32r
I32 = mybir.dt.int32
ALU = mybir.AluOpType
ACT = mybir.ActivationFunctionType
AX = mybir.AxisListType

COL_F, COL_Q, COL_I, COL_G, COL_CB, COL_CC, COL_CV = (
    CONV_DIM * 4, CONV_DIM * 3, CONV_DIM * 5, CONV_DIM * 6, 0, CONV_DIM, 2 * CONV_DIM)
UNIT_COLS = (COL_F, COL_Q, COL_I, COL_G, COL_CB, COL_CC, COL_CV)
NT = len(UNIT_COLS)
WS = 4

OUTS = [((1, SEQ, D), "float32"), ((DEC_B, DEC_L, D), "float32"), ((1, 1, 2, CONV_DIM), "float32"),
        ((1, 1, HEADS, P, P), "float32"), ((1, DEC_B, 2, CONV_DIM), "float32"),
        ((1, DEC_B, HEADS, P, P), "float32")]


def wait_apart(eng, sem, value, tick):
    eng.wait_ge(sem, value)
    eng.sem_inc(tick, 1)


def row_bcast(row, parts):
    return row.partition_broadcast(parts)


def modulation_phase(nc, io, keep, scr):
    NROW = 1 + DEC_B
    NCHUNK = 6 * D // 512
    ident, modT, sel_p, sel_s = keep["ident"], keep["modT"], keep["sel_p"], keep["sel_s"]
    head_par = keep["head_par"]
    with ExitStack() as ctx:
        sb = lambda name, shape, dt=F32: ctx.enter_context(nc.sbuf_tensor(name, shape, dt))
        ps = lambda name, shape: ctx.enter_context(nc.psum_tensor(name, shape, F32))
        sem = lambda name: ctx.enter_context(nc.semaphore(name))
        c_rows = sb("c_rows", [NROW, D])
        c_sig = sb("c_sig", [NROW, D])
        c_silu = sb("c_silu", [NROW, D])
        cT = sb("cT", [P, KT, NROW])
        b_rows = sb("b_rows", [NROW, 6 * D])
        mod = sb("mod", [NROW, 6 * D])
        w_ring = sb("w_ring", [P, 2, KT, 512])
        conv_rows = sb("conv_rows", [2 * DEC_B, CONV_DIM])
        lbt = sb("lbt", [P, 8, HEADS])
        blk_idx = sb("blk_idx", [P, NCH * CH // 2], I32)
        part_idx = sb("part_idx", [P, 1], I32)
        part_blk = sb("part_blk", [P, LEVELS], I32)
        part_blkf = sb("part_blkf", [P, LEVELS])
        blk_f = sb("blk_f", [P, NCH * CH // 2])
        ps_t = ps("ps_mt", [P, 512])
        ps_m = [ps("ps_m0", [P, 512]), ps("ps_m1", [P, 512])]
        ps_x = ps("ps_mx", [P, 512])
        c_in, b_in, small_in, conv_in = sem("c_in"), sem("b_in"), sem("small_in"), sem("conv_in")
        w_in = [sem("w_mod_in0"), sem("w_mod_in1")]
        c_sigd, c_silud, ident_rdy, cT_ps, cT_rdy = (sem("c_sigd"), sem("c_silud"), sem("ident_rdy"),
                                                     sem("cT_ps"), sem("cT_rdy"))
        prod, evac = sem("mod_prod"), sem("mod_evac")
        modT_ps, lb_d, lb_s, idx_rdy = sem("modT_ps"), sem("lb_d"), sem("lb_s"), sem("idx_rdy")
        mod_out = sem("mod_out")
        wv = io["w_mod"][0].rearrange("(k p) n -> p k n", p=P)

        with nc.Block() as block:
            @block.sync
            def _(sp):
                sp.dma_start(c_rows[0:1, :], io["c_prompt"]).then_inc(c_in, 16)
                sp.dma_start(c_rows[1:NROW, :], io["c_sample"]).then_inc(c_in, 16)
                for s in range(2):
                    sp.dma_start(w_ring[:, s], wv[:, :, bass.ds(s * 512, 512)]).then_inc(w_in[s], 16)
                with sp.Fori(1, NCHUNK // 2) as i:
                    for s in range(2):
                        sp.wait_ge(prod, 2 * i + s - 1)
                        sp.dma_start(w_ring[:, s], wv[:, :, bass.ds(i * 1024 + s * 512, 512)]).then_inc(w_in[s], 16)
                sp.wait_ge(evac, NCHUNK + 2)
                sp.dma_start(scr["mod"], mod[:, :]).then_inc(mod_out, 16)
                sp.wait_ge(mod_out, 16)

            @block.scalar
            def _(act):
                act.dma_start(b_rows[:, :], row_bcast(io["b_mod"][0], NROW)).then_inc(b_in, 16)
                act.dma_start(conv_rows[:, :], io["state_conv"][0].rearrange("b r c -> (b r) c")).then_inc(conv_in, 16)
                with nc.allow_non_contiguous_dma(reason="a few short parameter vectors"):
                    act.dma_start(lbt[:, 0, :], io["hgrn_lb_logits"][0].rearrange("(h p) -> p h", p=P)).then_inc(small_in, 16)
                    for j in range(CONV_W):
                        act.dma_start(head_par[:, :, 2 + j], io["conv_w"][0, j].rearrange("(h p) -> p h", p=P)).then_inc(small_in, 16)
                    for h in range(HEADS):
                        act.dma_start(head_par[:, h, 5:6], io["gnorm_w"][0].rearrange("(p a) -> p a", a=1)).then_inc(small_in, 16)
                act.wait_ge(c_in, 32)
                act.activation(c_sig[:, :], c_rows[:, :], ACT.Sigmoid).then_inc(c_sigd, 1)
                act.wait_ge(lb_d, 1)
                act.activation(lbt[:, 2, :], lbt[:, 1, :], ACT.Sigmoid)
                act.activation(lbt[:, 3, :], lbt[:, 1, :], ACT.Sigmoid, scale=-1.0).then_inc(lb_s, 1)

            @block.gpsimd
            def _(pool):
                pool.memset(ident[:, :], 0.0)
                pool.memset(sel_p[:, :], 0.0)
                pool.memset(sel_s[:, :], 1.0)
                pool.drain()
                pool.affine_select(out=ident[:, :], in_=ident[:, :], compare_op=ALU.not_equal, fill=1.0,
                                   base=0, pattern=[[-1, P]], channel_multiplier=1)
                pool.affine_select(out=sel_p[:, :], in_=sel_p[:, :], compare_op=ALU.not_equal, fill=1.0,
                                   base=0, pattern=[[0, P]], channel_multiplier=1)
                pool.affine_select(out=sel_s[:, :], in_=sel_s[:, :], compare_op=ALU.is_ge, fill=0.0,
                                   base=DEC_L, pattern=[[1, NSAMP]], channel_multiplier=-DEC_L)
                pool.drain()
                pool.affine_select(out=sel_s[:, :], in_=sel_s[:, :], compare_op=ALU.is_ge, fill=0.0,
                                   base=-1, pattern=[[-1, NSAMP]], channel_multiplier=DEC_L)
                pool.drain()
                pool.tensor_copy(keep["ident_i"][:, :], ident[:, :]).then_inc(ident_rdy, 1)
                pool.memset(keep["bmask"][:, :], 1.0)
                pool.memset(keep["neg_half"][:, :], -0.5)
                pool.memset(keep["ones"][:, :], 1.0)
                pool.memset(keep["tri"][:, :], 1.0)
                pool.drain()
                pool.affine_select(out=keep["bmask"][:, :], in_=keep["bmask"][:, :], compare_op=ALU.is_ge, fill=0.0,
                                   base=0, pattern=[[-DEC_L, SB]], channel_multiplier=1)
                pool.affine_select(out=keep["tri"][:, :], in_=keep["tri"][:, :], compare_op=ALU.is_ge, fill=0.0,
                                   base=-1, pattern=[[1, P]], channel_multiplier=-1)
                pool.iota(part_idx[:, :], pattern=[[0, 1]], base=0, channel_multiplier=1)
                pool.drain()
                pool.affine_select(out=keep["bmask"][:, :], in_=keep["bmask"][:, :], compare_op=ALU.is_ge, fill=0.0,
                                   base=DEC_L - 1, pattern=[[DEC_L, SB]], channel_multiplier=-1).then_inc(idx_rdy, 1)
                for l in range(LEVELS):
                    h, nb = 1 << l, CH >> (l + 1)
                    if l:
                        pool.wait_ge(modT_ps, l + 1)
                    pool.iota(blk_idx[:, :].rearrange("p (c b h) -> p c b h", c=NCH, b=nb),
                              pattern=[[0, NCH], [2, nb], [0, h]], base=0, channel_multiplier=0).then_inc(idx_rdy, 1)

            @block.tensor
            def _(pe):
                pe.wait_ge(ident_rdy, 1)
                pe.wait_ge(c_silud, 1)
                for k in range(KT):
                    last = pe.transpose(ps_t[:, k * NROW:(k + 1) * NROW], c_silu[:, k * P:(k + 1) * P], ident[0:NROW, 0:NROW])
                last.then_inc(cT_ps, 1)
                pe.wait_ge(conv_in, 16)
                for h in range(HEADS):
                    last = pe.transpose(ps_x[:, h * 16:(h + 1) * 16], conv_rows[:, h * P:(h + 1) * P], ident[0:16, 0:16])
                last.then_inc(cT_ps, 1)
                pe.wait_ge(cT_rdy, 1)
                with pe.Fori(0, NCHUNK // 2) as i:
                    for s in range(2):
                        pe.wait_ge(w_in[s], 16 * i + 16)
                        pe.wait_ge(evac, 2 * i + s + 1)
                        for k in range(KT):
                            last = pe.matmul(ps_m[s][0:NROW, :], cT[:, k, :], w_ring[:, s, k, :],
                                             start=(k == 0), stop=(k == KT - 1))
                        last.then_inc(prod, 1)
                pe.wait_ge(evac, NCHUNK + 2)
                pe.wait_ge(cT_rdy, 2)
                for k in range(2 * KT):
                    last = pe.transpose(ps_t[:, k * NROW:(k + 1) * NROW], mod[:, k * P:(k + 1) * P], ident[0:NROW, 0:NROW])
                last.then_inc(cT_ps, 1)

            @block.vector
            def _(dve):
                dve.sem_inc(evac, 2)
                dve.wait_ge(c_sigd, 1)
                dve.tensor_tensor(c_silu[:, :], c_rows[:, :], c_sig[:, :], ALU.mult).then_inc(c_silud, 1)
                dve.wait_ge(cT_ps, 1)
                dve.tensor_copy(cT[:, :, :], ps_t[:, 0:KT * NROW].rearrange("p (k r) -> p k r", k=KT)).then_inc(cT_rdy, 1)
                dve.wait_ge(cT_ps, 2)
                dve.tensor_copy(keep["conv_state_s"][:, :, :], ps_x[:, 0:HEADS * 16].rearrange("p (h r) -> p h r", h=HEADS)).then_inc(cT_rdy, 1)
                dve.wait_ge(small_in, 16 * (1 + CONV_W + HEADS))
                dve.tensor_tensor(lbt[:, 1, :], lbt[:, 0, :], lbt[:, 0, :], ALU.subtract).then_inc(lb_d, 1)
                dve.wait_ge(lb_s, 1)
                dve.reciprocal(lbt[:, 4, :], lbt[:, 3, :])
                dve.drain()
                dve.tensor_tensor(lbt[:, 5, :], lbt[:, 2, :], lbt[:, 4, :], ALU.mult)
                dve.drain()
                dve.reciprocal(lbt[:, 6, :], lbt[:, 5, :])
                dve.drain()
                dve.tensor_tensor(lbt[:, 7, :], lbt[:, 5, :], lbt[:, 6, :], ALU.mult)
                dve.drain()
                dve.tensor_tensor(head_par[:, :, 0], lbt[:, 7, :], lbt[:, 7, :], ALU.subtract)
                dve.drain()
                dve.tensor_scalar(head_par[:, :, 1], head_par[:, :, 0], -1.0, 1.0, ALU.mult, ALU.add)
                dve.wait_ge(idx_rdy, 1)
                for l in range(LEVELS):
                    dve.tensor_scalar(part_blk[:, l:l + 1], part_idx[:, :], l, None, ALU.logical_shift_right)
                dve.drain()
                dve.tensor_copy(part_blkf[:, :], part_blk[:, :]).then_inc(modT_ps, 1)
                for l in range(LEVELS):
                    dve.wait_ge(idx_rdy, l + 2)
                    dve.tensor_copy(blk_f[:, :], blk_idx[:, :])
                    dve.drain()
                    dve.tensor_scalar(keep["lmask"][:, l, :], blk_f[:, :], part_blkf[:, l:l + 1], None, ALU.is_equal)
                    dve.drain().then_inc(modT_ps, 1)
                dve.memset(keep["A"][:, :, :], 0.0)
                dve.memset(keep["A_s"][:, :], 0.0)
                dve.memset(keep["state"][:, :, :], 0.0)
                dve.memset(keep["conv_carry"][:, :, :], 0.0)
                dve.wait_ge(b_in, 16)
                with dve.Fori(0, NCHUNK // 2) as i:
                    for s in range(2):
                        dve.wait_ge(prod, 2 * i + s + 1)
                        dve.tensor_tensor(mod[:, bass.ds(i * 1024 + s * 512, 512)], ps_m[s][0:NROW, :],
                                          b_rows[:, bass.ds(i * 1024 + s * 512, 512)], ALU.add).then_inc(evac, 1)
                dve.wait_ge(cT_ps, 3)
                dve.tensor_copy(modT[:, 0:KT, :], ps_t[:, 0:KT * NROW].rearrange("p (k r) -> p k r", k=KT))
                dve.tensor_scalar(modT[:, KT:2 * KT, :], ps_t[:, KT * NROW:2 * KT * NROW].rearrange("p (k r) -> p k r", k=KT),
                                  1.0, None, ALU.add)


def mixer_phase(nc, io, keep, scr, outs):
    ident, modT, head_par = keep["ident"], keep["modT"], keep["head_par"]
    lmask, ident_i, A, A_s = keep["lmask"], keep["ident_i"], keep["A"], keep["A_s"]
    state, conv_carry, conv_state_s, bmask = keep["state"], keep["conv_carry"], keep["conv_state_s"], keep["bmask"]
    with ExitStack() as ctx:
        sb = lambda name, shape, dt=F32: ctx.enter_context(nc.sbuf_tensor(name, shape, dt))
        ps = lambda name, shape: ctx.enter_context(nc.psum_tensor(name, shape, F32))
        sem = lambda name: ctx.enter_context(nc.semaphore(name))
        x_rows = sb("x_rows", [P, XT, D])
        xs_rows = sb("xs_rows", [SS_TOK, D])
        seg_mod = sb("seg_mod", [P, 2 * KT, SB])
        u_f = sb("u_f", [P, 2, TS])
        u_hi = sb("u_hi", [P, KT, TS], F32R)
        u_lo = sb("u_lo", [P, KT, TS], F32R)
        w_raw = sb("w_raw", [P, WS, KT, P])
        w_hi = sb("w_hi", [P, WS, KT, P], F32R)
        w_lo = sb("w_lo", [P, WS, KT, P], F32R)
        par = sb("par", [P, 6])
        f_sig = sb("f_sig", [P, TS])
        k_sig = sb("k_sig", [P, TS])
        q_sig = sb("q_sig", [P, TS])
        g_sig = sb("g_sig", [P, TS])
        vT = sb("vT", [P, TS])
        cbs = sb("cbs", [P, TS])
        ccs = sb("ccs", [P, TS])
        q0 = sb("q0", [P, TS])
        ql = sb("ql", [P, LEVELS + 1, TS])
        kl = sb("kl", [P, LEVELS + 1, TS])
        wl0 = sb("wl0", [P, TS])
        wl = sb("wl", [P, TS])
        gg = sb("gg", [P, TS])
        v_tok = sb("v_tok", [P, NCH, P])
        k_tok = sb("k_tok", [P, NCH, P])
        vs_tok = sb("vs_tok", [SS_TOK, P])
        ks_tok = sb("ks_tok", [SS_TOK, P])
        vs_msk = sb("vs_msk", [SS_TOK, SB, P])
        qs_msk = sb("qs_msk", [P, SB * (SS_TOK + DEC_L)])
        s_chain = sb("s_chain", [P, NCH + 1, P])
        s0 = sb("s0", [P, SB, P])
        s1 = sb("s1", [P, SB, P])
        o_tok = sb("o_tok", [P, NCH + 1, P])
        o_sq = sb("o_sq", [P, NCH + 1, P])
        o_n = sb("o_n", [P, NCH + 1, P])
        o_ss = sb("o_ss", [P, NCH + 1])
        o_ms = sb("o_ms", [P, NCH + 1])
        o_r = sb("o_r", [P, NCH + 1])
        cvv = sb("cvv", [P, 2 + SP_TOK + SB * (2 + DEC_L)])
        cy = sb("cy", [P, 2, TS])
        y_conv = sb("y_conv", [P, TS])
        y_rec = sb("y_rec", [P, TS])
        pr = [ps("pr0", [P, 1024]), ps("pr1", [P, 1024])]
        pa = [ps("pa0", [P, 512]), ps("pa1", [P, 512])]
        pt = ps("pt", [P, 512])
        po = ps("po", [P, 512])

        tick = sem("tick")
        x_in = sem("x_in")
        raw_in = [sem("raw_in%d" % s) for s in range(WS)]
        s0_in = sem("s0_in")
        hi_done, lo_done, proj_done = sem("hi_done"), sem("lo_done"), sem("proj_done")
        pr_free = [sem("pr_free0"), sem("pr_free1")]
        pa_free = [sem("pa_free0"), sem("pa_free1")]
        pt_free, po_free = sem("pt_free"), sem("po_free")
        xT_ps, u_act, u_rdy = sem("xT_ps"), sem("u_act"), sem("u_rdy")
        ev = sem("act_evac")
        gates = sem("gates")
        q_lev, k_lev = sem("q_lev"), sem("k_lev")
        hg = sem("hg_ps")
        tok_rdy = sem("tok_rdy")
        a_rdy = sem("a_rdy")
        s_rdy = sem("s_rdy")
        smsk = sem("smsk")
        o_evac = sem("o_evac")
        o_mean, o_rs, o_nrm = sem("o_mean"), sem("o_rs"), sem("o_nrm")
        yc_rdy, yr_rdy, s1_rdy = sem("yc_rdy"), sem("yr_rdy"), sem("s1_rdy")
        stored, os_evac = sem("stored"), sem("os_evac")
        yc_out, yr_out, s1_out = sem("yc_out"), sem("yr_out"), sem("s1_out")
        fin, fin_ps, fin_sb, fin_out = sem("fin"), sem("fin_ps"), sem("fin_sb"), sem("fin_out")
        wv = io["w_in"][0].rearrange("(k p) n -> p k n", p=P)
        HG = 13
        (VT_, DIAG, L01, KT_, L23, L45, L6, SA, DS, DSS, O_, OT, OST) = range(1, HG + 1)
        lag = [j - 3 if j >= WS else (j - 2 if j < NT - WS else -3) for j in range(NT)]
        RC = 4

        def raw_count(j, u):
            s = j % WS
            uses = len([t for t in range(NT) if t % WS == s])
            return 16 * uses * u + 16 * (j // WS + 1)

        wl_n = [TS >> l if l <= SLEVELS else SP_TOK >> l for l in range(LEVELS + 1)]
        wl_at = [0, 0]
        for l in range(2, LEVELS + 1):
            wl_at.append(wl_at[-1] + wl_n[l - 1])
        assert wl_at[-1] + wl_n[-1] <= TS

        def decay(l, n):
            return wl0[:, 0:n] if l == 0 else wl[:, wl_at[l]:wl_at[l] + n]

        def blocks(ap, h):
            return ap.rearrange("p (b two h) -> p b two h", two=2, h=h)

        with nc.Block() as block:
            @block.sync
            def _(sp):
                def load_tile(u, h, j):
                    wait_apart(sp, lo_done, NT * u + (lag[j] + RC), tick)
                    sp.dma_start(w_raw[:, j % WS], wv[:, :, bass.ds(h * P + UNIT_COLS[j], P)]).then_inc(raw_in[j % WS], 16)

                load_tile(0, 0, 0)
                load_tile(0, 0, 1)
                with sp.Fori(0, SEGS) as seg:
                    with sp.Fori(0, HEADS) as h:
                        u = sp.snap(seg * HEADS + h)
                        h_next = sp.snap((h + 1) % HEADS)
                        for j in range(2, NT):
                            load_tile(u, h, j)
                        wait_apart(sp, s1_rdy, u + 1, tick)
                        sp.dma_start(s0[:, :, :], io["state_hgrn"][0, bass.ds(seg * SB, SB), bass.ds(h, 1), :, :]
                                     .rearrange("b a k v -> k (b a) v")).then_inc(s0_in, 16)
                        load_tile(u + 1, h_next, 0)
                        load_tile(u + 1, h_next, 1)
                sp.wait_ge(fin_sb, 1)
                for b in range(1):
                    sp.dma_start(outs[2][0, 0], cy[0:2, 0, 0:CONV_DIM]).then_inc(fin_out, 16)
                    sp.dma_start(outs[4][0].rearrange("b r c -> (b r) c"), cy[0:16, 1, 0:CONV_DIM]).then_inc(fin_out, 16)
                    sp.dma_start(outs[3][0, 0].rearrange("h k v -> k h v"), state[:, :, :]).then_inc(fin_out, 16)
                sp.wait_ge(fin_out, 48)

            @block.scalar
            def _(act):
                def split_hi(u, j, j_count):
                    act.wait_ge(raw_in[j % WS], j_count)
                    act.wait_ge(proj_done, NT * u + (lag[j] + RC))
                    act.activation(w_hi[:, j % WS], w_raw[:, j % WS], ACT.Copy).then_inc(hi_done, 1)

                def split_next(u, j):
                    if j + 2 < NT:
                        split_hi(u, j + 2, raw_count(j + 2, u))
                    else:
                        split_hi(u + 1, j + 2 - NT, raw_count(j + 2 - NT, u + 1))

                def proj(j):
                    return pr[j % 2][:, :].rearrange("p (a n) -> p a n", a=2)[:, :, 0:HALF]

                def two(ap):
                    return ap.rearrange("p (a n) -> p a n", a=2)

                act.sem_inc(u_rdy, 2)
                split_hi(0, 0, 16)
                split_hi(0, 1, 16)
                with act.Fori(0, SEGS) as seg:
                    act.activation(seg_mod[:, :, :], modT[:, :, bass.ds(seg * SB + 1, SB)], ACT.Copy)
                    act.drain()
                    for k in range(KT):
                        act.wait_ge(xT_ps, KT * seg + (k + 1))
                        act.wait_ge(u_rdy, KT * seg + (k + 1))
                        act.activation(u_f[:, k % 2, 0:SP_TOK], pr[k % 2][:, 0:SP_TOK], ACT.Identity,
                                       bias=modT[:, k, 0:1], scale=modT[:, KT + k, 0:1])
                        for b in range(SB):
                            last = act.activation(u_f[:, k % 2, SP_TOK + b * DEC_L:SP_TOK + (b + 1) * DEC_L],
                                                  pr[k % 2][:, SP_TOK + b * DEC_L:SP_TOK + (b + 1) * DEC_L], ACT.Identity,
                                                  bias=seg_mod[:, k, b:b + 1], scale=seg_mod[:, KT + k, b:b + 1])
                        act.drain().then_inc(u_act, 1)
                    with act.Fori(0, HEADS) as h:
                        u = act.snap(seg * HEADS + h)
                        split_next(u, 0)
                        act.wait_ge(proj_done, NT * u + (0 + 1 + RC))
                        act.wait_ge(gates, 8 * u + 1)
                        act.activation(two(f_sig[:, :]), proj(0), ACT.Sigmoid)
                        act.activation(two(k_sig[:, :]), proj(0), ACT.Sigmoid, scale=-1.0)
                        act.drain().then_inc(ev, 1)
                        split_next(u, 1)
                        act.wait_ge(proj_done, NT * u + (1 + 1 + RC))
                        act.activation(two(q_sig[:, :]), proj(1), ACT.Sigmoid).then_inc(ev, 1)
                        split_next(u, 2)
                        act.wait_ge(proj_done, NT * u + (2 + 1 + RC))
                        act.activation(two(vT[:, :]), proj(2), ACT.Copy).then_inc(ev, 1)
                        split_next(u, 3)
                        act.wait_ge(hg, HG * u + VT_)
                        act.activation(v_tok[:, :, :], pt[:, :].rearrange("p (c v) -> p c v", c=NCH), ACT.Copy).then_inc(tok_rdy, 1)
                        act.wait_ge(proj_done, NT * u + (3 + 1 + RC))
                        act.activation(two(g_sig[:, :]), proj(3), ACT.Sigmoid).then_inc(ev, 1)
                        split_next(u, 4)
                        act.wait_ge(hg, HG * u + KT_)
                        act.activation(k_tok[:, :, :], pt[:, :].rearrange("p (c v) -> p c v", c=NCH), ACT.Copy).then_inc(tok_rdy, 1)
                        act.wait_ge(proj_done, NT * u + (4 + 1 + RC))
                        act.wait_ge(yc_rdy, u + 1)
                        act.activation(two(cbs[:, :]), proj(4), ACT.Copy).then_inc(ev, 1)
                        split_next(u, 5)
                        act.wait_ge(hg, HG * u + SA)
                        act.activation(vs_tok[:, :], pa[1][0:SS_TOK, 64:64 + P], ACT.Copy)
                        act.activation(ks_tok[:, :], pa[1][0:SS_TOK, 192:192 + P], ACT.Copy)
                        act.drain().then_inc(tok_rdy, 1)
                        act.wait_ge(proj_done, NT * u + (5 + 1 + RC))
                        act.activation(two(ccs[:, :]), proj(5), ACT.Copy).then_inc(ev, 1)
                        split_next(u, 6)
                        act.wait_ge(hg, HG * u + DSS)
                        act.activation(o_tok[0:SS_TOK, NCH, :], pa[0][0:SS_TOK, 2 * P:3 * P], ACT.Copy)
                        act.activation(o_sq[0:SS_TOK, NCH, :], pa[0][0:SS_TOK, 2 * P:3 * P], ACT.Square).then_inc(os_evac, 1)
                        act.wait_ge(hg, HG * u + O_)
                        act.activation(o_tok[:, 0:NCH, :], po[:, :].rearrange("p (c v) -> p c v", c=NCH), ACT.Copy)
                        act.activation(o_sq[:, 0:NCH, :], po[:, :].rearrange("p (c v) -> p c v", c=NCH), ACT.Square)
                        act.drain().then_inc(o_evac, 1)

            @block.gpsimd
            def _(pool):
                def load_x(seg):
                    pool.dma_start(x_rows[:, :, :], io["x_prompt"][0, bass.ds(seg * SP_TOK, SP_TOK), :]
                                 .rearrange("(t p) d -> p t d", p=P)).then_inc(x_in, 16)
                    pool.dma_start(xs_rows[:, :], io["x_sample"].rearrange("b l d -> (b l) d")[bass.ds(seg * SS_TOK, SS_TOK), :]).then_inc(x_in, 16)

                pool.sem_inc(yc_rdy, 1)
                pool.sem_inc(s1_rdy, 1)
                pool.sem_inc(yr_rdy, 1)
                pool.sem_inc(stored, 1)
                ss_off = SEQ
                load_x(0)

                def segment(seg):
                    with pool.Fori(0, HEADS) as h:
                        u = pool.snap(seg * HEADS + h)
                        for l in range(LEVELS):
                            n = TS if l < SLEVELS else SP_TOK
                            hh = 1 << l
                            pool.wait_ge(gates, 8 * u + (l + 2))
                            src, dst = blocks(kl[:, l, 0:n], hh), blocks(kl[:, l + 1, 0:n], hh)
                            wsrc = decay(l, n // hh)
                            wr = wsrc.rearrange("p (b two) -> p b two", two=2)[:, :, 1:2].broadcast_to([P, n // (2 * hh), hh])
                            pool.tensor_tensor(dst[:, :, 0, :], src[:, :, 0, :], wr, ALU.mult)
                            pool.tensor_copy(dst[:, :, 1, :], src[:, :, 1, :])
                            pool.drain().then_inc(k_lev, 1)
                        pool.wait_ge(o_mean, u + 1)
                        pool.tensor_tensor(o_r[:, :], o_ms[:, :], keep["neg_half"][:, 0:NCH + 1], ALU.pow).then_inc(o_rs, 1)
                        pool.wait_ge(yc_rdy, u + 2)
                        pool.dma_start(scr["y"][bass.ds(h, 1), :, bass.ds(seg * SP_TOK, SP_TOK)].rearrange("a p n -> (a p) n"),
                                       y_conv[:, 0:SP_TOK]).then_inc(yc_out, 16)
                        pool.dma_start(scr["y"][bass.ds(h, 1), :, bass.ds(seg * SS_TOK + ss_off, SS_TOK)].rearrange("a p n -> (a p) n"),
                                       y_conv[:, SP_TOK:TS]).then_inc(yc_out, 16)
                        pool.wait_ge(s1_rdy, u + 2)
                        pool.dma_start(outs[5][0, bass.ds(seg * SB, SB), bass.ds(h, 1), :, :].rearrange("b a k v -> k (b a) v"),
                                       s1[:, :, :]).then_inc(s1_out, 16)
                        pool.wait_ge(yr_rdy, u + 2)
                        pool.dma_start(scr["y"][bass.ds(h + HEADS, 1), :, bass.ds(seg * SP_TOK, SP_TOK)].rearrange("a p n -> (a p) n"),
                                       y_rec[:, 0:SP_TOK]).then_inc(yr_out, 16)
                        pool.dma_start(scr["y"][bass.ds(h + HEADS, 1), :, bass.ds(seg * SS_TOK + ss_off, SS_TOK)].rearrange("a p n -> (a p) n"),
                                       y_rec[:, SP_TOK:TS]).then_inc(yr_out, 16)
                        pool.wait_ge(yc_out, 32 * u + 32)
                        pool.wait_ge(s1_out, 16 * u + 16)
                        pool.wait_ge(yr_out, 32 * u + 32)
                        pool.sem_inc(stored, 1)

                with pool.Fori(0, SEGS - 1) as seg:
                    pool.wait_ge(xT_ps, KT * seg + KT)
                    load_x(seg + 1)
                    segment(seg)
                segment(SEGS - 1)

            @block.tensor
            def _(pe):
                for s in range(2):
                    pe.sem_inc(pr_free[s], 1)
                    pe.sem_inc(pa_free[s], 1)
                pe.sem_inc(pt_free, 1)
                pe.sem_inc(po_free, 1)
                pe.sem_inc(proj_done, RC)
                with pe.Fori(0, SEGS) as seg:
                    pe.wait_ge(x_in, 32 * seg + 32)
                    for k in range(KT):
                        uses = 20 if k % 2 == 0 else 16
                        pe.wait_ge(pr_free[k % 2], uses * seg + (k // 2 + 1))
                        for t in range(XT):
                            pe.transpose(pr[k % 2][:, t * P:(t + 1) * P], x_rows[:, t, k * P:(k + 1) * P], ident[:, :])
                        pe.transpose(pr[k % 2][:, SP_TOK:TS], xs_rows[:, k * P:(k + 1) * P],
                                     ident[0:SS_TOK, 0:SS_TOK]).then_inc(xT_ps, 1)
                    wait_apart(pe, u_rdy, KT * seg + (KT + 2), tick)
                    with pe.Fori(0, HEADS) as h:
                        u = pe.snap(seg * HEADS + h)
                        f0 = pe.snap(seg * 20 + h * 4)
                        f1 = pe.snap(seg * 16 + h * 3)

                        def project(j, mid=None):
                            s = j % WS
                            pe.wait_ge(lo_done, NT * u + (j + 1 + RC))
                            if j % 2 == 0:
                                pe.wait_ge(pr_free[0], f0 + (5 + j // 2))
                            else:
                                pe.wait_ge(pr_free[1], f1 + (5 + j // 2))
                            for k in range(KT):
                                for n, (w, x) in enumerate(((w_hi, u_hi), (w_hi, u_lo), (w_lo, u_hi))):
                                    for a in range(2):
                                        last = pe.matmul(pr[j % 2][:, a * 512:a * 512 + HALF], w[:, s, k, :],
                                                         x[:, k, a * HALF:(a + 1) * HALF],
                                                         start=(k == 0 and n == 0), stop=(k == KT - 1 and n == 2))
                                if k == 3 and mid:
                                    mid()
                            last.then_inc(proj_done, 1)

                        def level(l, out, col, tok=P, nch=NCH, base=0):
                            hh = 1 << l
                            for c in range(nch):
                                t0 = base + c * tok
                                right = blocks(ql[:, l, t0:t0 + tok], hh)[:, :, 1, :]
                                last = pe.matmul(out[0:tok, col + c * tok // 2:col + (c + 1) * tok // 2],
                                                 kl[:, l, t0:t0 + tok], right, start=True, stop=True)
                            return last

                        def v_transposes():
                            pe.wait_ge(ev, 6 * u + 3)
                            pe.wait_ge(pt_free, 4 * u + 1)
                            for c in range(NCH):
                                last = pe.transpose(pt[:, c * P:(c + 1) * P], vT[:, c * P:(c + 1) * P], ident[:, :])
                            last.then_inc(hg, 1)

                        def first_scores():
                            pe.wait_ge(q_lev, 9 * u + 1)
                            pe.wait_ge(pa_free[0], 4 * u + 1)
                            for c in range(NCH):
                                last = pe.matmul(pa[0][:, c * P:(c + 1) * P], kl[:, 0, c * P:(c + 1) * P],
                                                 q0[:, c * P:(c + 1) * P], start=True, stop=True)
                            last.then_inc(hg, 1)
                            pe.wait_ge(q_lev, 9 * u + 3)
                            pe.wait_ge(k_lev, 7 * u + 1)
                            pe.wait_ge(pa_free[1], 4 * u + 1)
                            level(0, pa[1], 0)
                            level(1, pa[1], 256).then_inc(hg, 1)
                            pe.wait_ge(k_lev, 7 * u + 7)
                            pe.wait_ge(pt_free, 4 * u + 2)
                            for c in range(NCH):
                                last = pe.transpose(pt[:, c * P:(c + 1) * P], kl[:, LEVELS, c * P:(c + 1) * P], ident[:, :])
                            last.then_inc(hg, 1)

                        def mid_scores():
                            pe.wait_ge(q_lev, 9 * u + 7)
                            pe.wait_ge(pa_free[0], 4 * u + 2)
                            level(2, pa[0], 0)
                            level(3, pa[0], 256).then_inc(hg, 1)
                            pe.wait_ge(pa_free[1], 4 * u + 2)
                            level(4, pa[1], 0)
                            level(5, pa[1], 256).then_inc(hg, 1)

                        def last_scores():
                            pe.wait_ge(q_lev, 9 * u + 9)
                            pe.wait_ge(pa_free[0], 4 * u + 3)
                            level(6, pa[0], 0).then_inc(hg, 1)
                            pe.wait_ge(pa_free[1], 4 * u + 3)
                            pe.matmul(pa[1][0:SS_TOK, 0:SS_TOK], kl[:, 0, SP_TOK:TS], q0[:, SP_TOK:TS], start=True, stop=True)
                            for l in range(SLEVELS):
                                level(l, pa[1], SS_TOK + l * SS_TOK // 2, tok=SS_TOK, nch=1, base=SP_TOK)
                            pe.transpose(pa[1][0:SS_TOK, 64:64 + P], vT[:, SP_TOK:TS], ident[:, :])
                            pe.transpose(pa[1][0:SS_TOK, 192:192 + P], kl[:, SLEVELS, SP_TOK:TS], ident[:, :]).then_inc(hg, 1)
                            pe.wait_ge(tok_rdy, 3 * u + 2)
                            pe.wait_ge(pt_free, 4 * u + 3)
                            for c in range(NCH):
                                last = pe.matmul(pt[:, c * P:(c + 1) * P], k_tok[:, c, :], v_tok[:, c, :], start=True, stop=True)
                            last.then_inc(hg, 1)

                        def outputs():
                            pe.wait_ge(tok_rdy, 3 * u + 3)
                            pe.wait_ge(smsk, 2 * u + 2)
                            pe.wait_ge(a_rdy, 2 * u + 2)
                            pe.wait_ge(s0_in, 16 * u + 16)
                            pe.wait_ge(pa_free[0], 4 * u + 4)
                            pe.matmul(pa[0][:, 0:SB * P], ks_tok[:, :], vs_msk[:, :, :].rearrange("s b v -> s (b v)"), start=True, stop=True)
                            pe.matmul(pa[0][0:SS_TOK, SB * P:(SB + 1) * P], A_s[:, :], vs_tok[:, :], start=True, stop=False)
                            for b in range(SB):
                                last = pe.matmul(pa[0][0:SS_TOK, SB * P:(SB + 1) * P], qs_msk[:, b * SS_TOK:(b + 1) * SS_TOK],
                                                 s0[:, b, :], start=False, stop=(b == SB - 1))
                            last.then_inc(hg, 1)
                            pe.wait_ge(s_rdy, u + 1)
                            pe.wait_ge(po_free, u + 1)
                            for c in range(NCH):
                                pe.matmul(po[:, c * P:(c + 1) * P], A[:, c, :], v_tok[:, c, :], start=True, stop=False)
                                last = pe.matmul(po[:, c * P:(c + 1) * P], ql[:, LEVELS, c * P:(c + 1) * P], s_chain[:, c, :],
                                                 start=False, stop=True)
                            last.then_inc(hg, 1)

                        project(0)
                        project(1)
                        project(2)
                        v_transposes()
                        project(3)
                        first_scores()
                        project(4, mid_scores)
                        last_scores()
                        project(5)
                        outputs()
                        project(6)
                        pe.wait_ge(o_nrm, u + 1)
                        pe.wait_ge(pt_free, 4 * u + 4)
                        for c in range(NCH):
                            last = pe.transpose(pt[:, c * P:(c + 1) * P], o_n[:, c, :], ident[:, :])
                        last.then_inc(hg, 1)
                        wait_apart(pe, pa_free[1], 4 * u + 4, tick)
                        pe.transpose(pa[1][:, 0:SS_TOK], o_n[0:SS_TOK, NCH, :], ident[0:SS_TOK, 0:SS_TOK]).then_inc(hg, 1)
                pe.wait_ge(fin, 1)
                for h in range(HEADS):
                    pe.transpose(pa[0][0:2, h * P:(h + 1) * P], conv_carry[:, h, :], ident[:, :])
                    last = pe.transpose(po[0:16, h * P:(h + 1) * P], conv_state_s[:, h, :], ident[:, :])
                last.then_inc(fin_ps, 1)

            @block.vector
            def _(dve):
                def split_lo(u, j):
                    dve.wait_ge(hi_done, NT * u + (j + 1))
                    dve.tensor_tensor(w_lo[:, j % WS], w_raw[:, j % WS], w_hi[:, j % WS].bitcast(F32), ALU.subtract).then_inc(lo_done, 1)

                def split_next(u, j):
                    if j + 2 < NT:
                        split_lo(u, j + 2)
                    else:
                        split_lo(u + 1, j + 2 - NT)

                def proj(j):
                    return pr[j % 2][:, :].rearrange("p (a n) -> p a n", a=2)[:, :, 0:HALF]

                def two(ap):
                    return ap.rearrange("p (a n) -> p a n", a=2)

                def place(l, src, col, free=None):
                    hh = 1 << l
                    out = blocks(A[:, :, :].rearrange("p c t -> p (c t)"), hh)[:, :, 1, :]
                    ins = dve.copy_predicated(out, lmask[:, l, :].rearrange("p (b h) -> p b h", h=hh),
                                              src[:, col:col + NCH * P // 2].rearrange("p (b h) -> p b h", h=hh))
                    return ins

                dve.sem_inc(lo_done, RC)
                dve.sem_inc(gates, 1)
                dve.memset(qs_msk[:, :], 0.0)
                dve.memset(o_tok[:, NCH, :], 0.0)
                dve.memset(o_sq[:, NCH, :], 0.0)
                split_lo(0, 0)
                split_lo(0, 1)
                with dve.Fori(0, SEGS) as seg:
                    for k in range(KT):
                        dve.wait_ge(u_act, KT * seg + (k + 1))
                        dve.wait_ge(proj_done, seg * HEADS * NT + RC)
                        dve.tensor_copy(u_hi[:, k, :], u_f[:, k % 2, :]).then_inc(pr_free[k % 2], 1)
                        dve.drain()
                        dve.tensor_tensor(u_lo[:, k, :], u_f[:, k % 2, :], u_hi[:, k, :].bitcast(F32), ALU.subtract).then_inc(u_rdy, 1)
                    with dve.Fori(0, HEADS) as h:
                        u = dve.snap(seg * HEADS + h)
                        dve.tensor_copy(par[:, :], head_par[:, bass.ds(h, 1), :].rearrange("p a c -> p (a c)"))
                        split_next(u, 0)
                        dve.drain()
                        dve.wait_ge(ev, 6 * u + 1)
                        dve.tensor_scalar(wl0[:, :], f_sig[:, :], par[:, 1:2], par[:, 0:1], ALU.mult, ALU.add).then_inc(pr_free[0], 1)
                        dve.tensor_scalar(kl[:, 0, :], k_sig[:, :], par[:, 1:2], None, ALU.mult)
                        dve.drain().then_inc(gates, 1)
                        for l in range(LEVELS):
                            n = (TS if l < SLEVELS else SP_TOK) >> l
                            src = decay(l, n).rearrange("p (b two) -> p b two", two=2)
                            dve.tensor_tensor(decay(l + 1, n // 2), src[:, :, 0], src[:, :, 1], ALU.mult)
                            dve.drain().then_inc(gates, 1)
                        split_next(u, 1)
                        dve.wait_ge(ev, 6 * u + 2)
                        dve.scalar_tensor_tensor(two(q0[:, :]), proj(1), QSCALE, two(q_sig[:, :]), ALU.mult, ALU.mult)
                        dve.drain().then_inc(q_lev, 1)
                        dve.tensor_tensor(ql[:, 0, :], q0[:, :], wl0[:, :], ALU.mult).then_inc(pr_free[1], 1)
                        dve.drain().then_inc(q_lev, 1)
                        for l in range(LEVELS):
                            n = TS if l < SLEVELS else SP_TOK
                            hh = 1 << l
                            src, dst = blocks(ql[:, l, 0:n], hh), blocks(ql[:, l + 1, 0:n], hh)
                            wsrc = decay(l, n // hh)
                            wleft = wsrc.rearrange("p (b two) -> p b two", two=2)[:, :, 0:1].broadcast_to([P, n // (2 * hh), hh])
                            dve.tensor_tensor(dst[:, :, 1, :], src[:, :, 1, :], wleft, ALU.mult)
                            dve.tensor_copy(dst[:, :, 0, :], src[:, :, 0, :])
                            dve.drain().then_inc(q_lev, 1)
                        dve.tensor_copy(qs_msk[:, :].rearrange("p (b t) -> p b t", b=SB)[:, :, 0:DEC_L],
                                        ql[:, SLEVELS, SP_TOK:TS].rearrange("p (b t) -> p b t", b=SB)).then_inc(smsk, 1)
                        split_next(u, 2)
                        split_next(u, 3)
                        dve.wait_ge(tok_rdy, 3 * u + 1)
                        dve.sem_inc(pt_free, 1)
                        dve.wait_ge(ev, 6 * u + 4)
                        dve.sem_inc(pr_free[0], 1)
                        dve.scalar_tensor_tensor(two(gg[:, :]), proj(3), par[:, 5:6], two(g_sig[:, :]), ALU.mult, ALU.mult).then_inc(pr_free[1], 1)
                        wait_apart(dve, hg, HG * u + DIAG, tick)
                        dve.copy_predicated(A[:, :, :], ident_i[:, :].rearrange("p (a t) -> p a t", a=1).broadcast_to([P, NCH, P]),
                                            pa[0][:, :].rearrange("p (c t) -> p c t", c=NCH)).then_inc(pa_free[0], 1)
                        dve.drain()
                        wait_apart(dve, hg, HG * u + L01, tick)
                        place(0, pa[1], 0)
                        dve.drain()
                        place(1, pa[1], 256).then_inc(pa_free[1], 1)
                        split_next(u, 4)
                        dve.drain()
                        wait_apart(dve, hg, HG * u + L23, tick)
                        place(2, pa[0], 0)
                        dve.drain()
                        place(3, pa[0], 256).then_inc(pa_free[0], 1)
                        dve.drain()
                        wait_apart(dve, hg, HG * u + L45, tick)
                        place(4, pa[1], 0)
                        dve.drain()
                        place(5, pa[1], 256).then_inc(pa_free[1], 1)
                        dve.wait_ge(tok_rdy, 3 * u + 2)
                        dve.sem_inc(pt_free, 1)
                        split_next(u, 5)
                        dve.wait_ge(ev, 6 * u + 5)
                        dve.sem_inc(pr_free[0], 1)
                        dve.drain()
                        wait_apart(dve, hg, HG * u + L6, tick)
                        place(6, pa[0], 0)
                        dve.drain().then_inc(pa_free[0], 1)
                        dve.sem_inc(a_rdy, 1)
                        wait_apart(dve, tok_rdy, 3 * u + 3, tick)
                        dve.copy_predicated(A_s[:, :], ident_i[0:SS_TOK, 0:SS_TOK], pa[1][0:SS_TOK, 0:SS_TOK])
                        for l in range(SLEVELS):
                            hh, n = 1 << l, SS_TOK // 2
                            dve.drain()
                            dve.copy_predicated(blocks(A_s[:, :], hh)[:, :, 1, :],
                                                lmask[0:SS_TOK, l, 0:n].rearrange("p (b h) -> p b h", h=hh),
                                                pa[1][0:SS_TOK, SS_TOK + l * n:SS_TOK + (l + 1) * n].rearrange("p (b h) -> p b h", h=hh))
                        dve.drain().then_inc(a_rdy, 1)
                        dve.sem_inc(pa_free[1], 1)
                        dve.tensor_tensor(vs_msk[:, :, :], vs_tok[:, :].rearrange("s (a v) -> s a v", a=1).broadcast_to([SS_TOK, SB, P]),
                                          bmask[:, :].rearrange("s (b a) -> s b a", a=1).broadcast_to([SS_TOK, SB, P]), ALU.mult).then_inc(smsk, 1)
                        dve.tensor_copy(s_chain[:, 0, :], state[:, bass.ds(h, 1), :].rearrange("p a v -> p (a v)"))
                        dve.drain()
                        dve.wait_ge(hg, HG * u + DS)
                        for c in range(NCH):
                            dve.scalar_tensor_tensor(s_chain[:, c + 1, :], s_chain[:, c, :], decay(LEVELS, NCH)[:, c:c + 1],
                                                     pt[:, c * P:(c + 1) * P], ALU.mult, ALU.add)
                            dve.drain()
                        dve.sem_inc(s_rdy, 1)
                        dve.tensor_copy(state[:, bass.ds(h, 1), :].rearrange("p a v -> p (a v)"), s_chain[:, NCH, :]).then_inc(pt_free, 1)
                        split_next(u, 6)
                        dve.tensor_copy(cvv[:, 0:2], conv_carry[:, bass.ds(h, 1), :].rearrange("p a r -> p (a r)"))
                        samp = cvv[:, 2 + SP_TOK:].rearrange("p (b t) -> p b t", b=SB)
                        cst = conv_state_s[:, bass.ds(h, 1), bass.ds(seg * (2 * SB), 2 * SB)].rearrange("p a (b r) -> p (a b) r", r=2)
                        dve.tensor_copy(samp[:, :, 0:2], cst)
                        dve.wait_ge(os_evac, u + 1)
                        dve.wait_ge(stored, u + 1)
                        for b in range(SB):
                            last = dve.scalar_tensor_tensor(s1[:, b, :], s0[:, b, :], decay(SLEVELS, TS // DEC_L)[:, SP_TOK // DEC_L + b:SP_TOK // DEC_L + b + 1],
                                                            pa[0][:, b * P:(b + 1) * P], ALU.mult, ALU.add)
                        dve.drain().then_inc(s1_rdy, 1)
                        dve.wait_ge(o_evac, u + 1)
                        dve.sem_inc(pa_free[0], 1)
                        dve.sem_inc(po_free, 1)
                        dve.tensor_reduce(o_ss[:, :], o_sq[:, :, :], axis=AX.X, op=ALU.add)
                        dve.drain()
                        dve.tensor_scalar(o_ms[:, :], o_ss[:, :], 1.0 / P, RMS_EPS, ALU.mult, ALU.add).then_inc(o_mean, 1)
                        dve.wait_ge(o_rs, u + 1)
                        dve.tensor_tensor(o_n[:, :, :], o_tok[:, :, :],
                                          o_r[:, :].rearrange("p (c a) -> p c a", a=1).broadcast_to([P, NCH + 1, P]), ALU.mult).then_inc(o_nrm, 1)
                        dve.wait_ge(ev, 6 * u + 6)
                        dve.sem_inc(pr_free[1], 1)
                        dve.wait_ge(proj_done, NT * u + (6 + 1 + RC))
                        dve.tensor_tensor(cvv[:, 2:2 + HALF], pr[0][:, 0:HALF], ccs[:, 0:HALF], ALU.mult)
                        dve.tensor_tensor(cvv[:, 2 + HALF:2 + SP_TOK], pr[0][:, 512:512 + SP_TOK - HALF], ccs[:, HALF:SP_TOK], ALU.mult)
                        dve.tensor_tensor(samp[:, :, 2:2 + DEC_L],
                                          pr[0][:, 512 + SP_TOK - HALF:512 + HALF].rearrange("p (b t) -> p b t", b=SB),
                                          ccs[:, SP_TOK:TS].rearrange("p (b t) -> p b t", b=SB), ALU.mult)
                        dve.drain().then_inc(pr_free[0], 1)
                        cys = [cy[:, n, SP_TOK:TS].rearrange("p (b t) -> p b t", b=SB) for n in range(2)]
                        dve.tensor_scalar(cy[:, 0, 0:SP_TOK], cvv[:, 0:SP_TOK], par[:, 2:3], None, ALU.mult)
                        dve.tensor_scalar(cys[0], samp[:, :, 0:DEC_L], par[:, 2:3], None, ALU.mult)
                        dve.drain()
                        for n in range(1, CONV_W):
                            dve.scalar_tensor_tensor(cy[:, n % 2, 0:SP_TOK], cvv[:, n:n + SP_TOK], par[:, 2 + n:3 + n],
                                                     cy[:, (n + 1) % 2, 0:SP_TOK], ALU.mult, ALU.add)
                            dve.scalar_tensor_tensor(cys[n % 2], samp[:, :, n:n + DEC_L], par[:, 2 + n:3 + n],
                                                     cys[(n + 1) % 2], ALU.mult, ALU.add)
                            dve.drain()
                        dve.tensor_copy(conv_carry[:, bass.ds(h, 1), :].rearrange("p a r -> p (a r)"), cvv[:, SP_TOK:SP_TOK + 2])
                        dve.tensor_copy(cst, samp[:, :, DEC_L:DEC_L + 2])
                        dve.tensor_tensor(y_conv[:, :], cy[:, 0, :], cbs[:, :], ALU.mult).then_inc(yc_rdy, 1)
                        dve.wait_ge(hg, HG * u + OST)
                        dve.tensor_tensor(y_rec[:, 0:SP_TOK], pt[:, :], gg[:, 0:SP_TOK], ALU.mult).then_inc(pt_free, 1)
                        dve.tensor_tensor(y_rec[:, SP_TOK:TS], pa[1][:, 0:SS_TOK], gg[:, SP_TOK:TS], ALU.mult).then_inc(pa_free[1], 1)
                        dve.drain().then_inc(yr_rdy, 1)
                dve.sem_inc(fin, 1)
                dve.wait_ge(fin_ps, 1)
                dve.tensor_copy(cy[0:2, 0, 0:CONV_DIM], pa[0][0:2, :])
                dve.tensor_copy(cy[0:16, 1, 0:CONV_DIM], po[0:16, :])
                dve.drain().then_inc(fin_sb, 1)


def output_phase(nc, io, keep, scr):
    ident, neg_half, logits = keep["ident"], keep["neg_half"], keep["logits"]
    T = TILES
    LAST = T - 1
    with ExitStack() as ctx:
        sb = lambda name, shape, dt=F32: ctx.enter_context(nc.sbuf_tensor(name, shape, dt))
        ps = lambda name, shape: ctx.enter_context(nc.psum_tensor(name, shape, F32))
        sem = lambda name: ctx.enter_context(nc.semaphore(name))
        mod_rows = sb("mod_rows", [1 + DEC_B, 3 * D])
        mod_p = sb("mod_p", [P, 3, D])
        mod_s = sb("mod_s", [NSAMP, 3, D])
        ln1 = sb("ln1", [P, 2, D])
        wo_raw = sb("wo_raw", [P, 2, D])
        wo_hi = sb("wo_hi", [P, KT, D], F32R)
        wo_lo = sb("wo_lo", [P, KT, D], F32R)
        w_rt = sb("w_rt", [P, KT, NG + NE])
        y_raw = sb("y_raw", [P, 2, KT, P])
        y_hi = sb("y_hi", [P, 2, KT, P], F32R)
        y_lo = sb("y_lo", [P, 2, KT, P], F32R)
        x_t = sb("x_t", [P, 2, D])
        z = sb("z", [P, D])
        z2 = sb("z2", [P, D])
        zn = sb("zn", [P, D])
        x1 = sb("x1", [P, D])
        u2m = sb("u2m", [P, D])
        u2 = sb("u2", [P, D])
        u2T = sb("u2T", [P, KT, P])
        stats = sb("stats", [P, 2, 6])
        mv = sb("mv", [P, 2])
        ve = sb("ve", [P, 1])
        rstd = sb("rstd", [P, 1])
        zero_row = sb("zero_row", [1, D])
        NLIST = (NE + 1) * CAP // P
        slot_i = sb("slot_i", [P, NLIST], I32)
        fill = sb("fill", [P, NLIST, 4], I32)
        pm = [ps("pm0", [P, 1024]), ps("pm1", [P, 1024])]
        px = ps("px", [P, 1024])
        pl = ps("pl", [P, 512])

        mod_in, ln_in, rt_in = sem("mod2_in"), sem("ln_in"), sem("rt_in")
        wo_in = [sem("wo_in0"), sem("wo_in1")]
        y_in = [sem("y_in0"), sem("y_in1")]
        x_in = [sem("x2_in0"), sem("x2_in1")]
        wo_h, wo_l, y_h, y_l = sem("wo_h"), sem("wo_l"), sem("y_h"), sem("y_l")
        bc_ps, bc_ev = sem("bc_ps"), sem("bc_ev")
        prod, z_rdy, var_rdy, rs_rdy, x1_rdy, u2_rdy = (sem(n) for n in ("prod2", "z_rdy", "var_rdy", "rs_rdy", "x1_rdy", "u2_rdy"))
        uT_ps, uT_sb, lg_ps, lg_sb = sem("uT_ps"), sem("uT_sb"), sem("lg_ps"), sem("lg_sb")
        x1_out, u2_out, st_done = sem("x1_out"), sem("u2_out"), sem("st_done")
        consts, fill_rdy, fill_out, zr_rdy, zr_out = (sem(n) for n in ("consts2", "fill_rdy", "fill_out", "zr_rdy", "zr_out"))
        tick = sem("tick2")
        wov = io["w_out"][0].rearrange("(k p) n -> p k n", p=P)
        xp = io["x_prompt"][0]
        xs = io["x_sample"].rearrange("b l d -> (b l) d")
        yv = scr["y"].rearrange("k p t -> p k t")

        def rows_of(t):
            return NSAMP if isinstance(t, int) and t == LAST else P

        with nc.Block() as block:
            @block.sync
            def _(sp):
                sp.dma_start(mod_rows[:, :], scr["mod"][:, 2 * D:5 * D]).then_inc(mod_in, 16)
                for k in range(2):
                    sp.dma_start(wo_raw[:, k], wov[:, k]).then_inc(wo_in[k], 16)

                def load(t, s):
                    n = rows_of(t)
                    sp.dma_start(y_raw[:, s, :, 0:n], yv[:, :, bass.ds(t * P, n)]).then_inc(y_in[s], 16)
                    src = xs if n < P else xp[bass.ds(t * P, n), :]
                    sp.dma_start(x_t[0:n, s, :], src).then_inc(x_in[s], 16)

                load(0, 0)
                load(1, 1)
                for k in range(2, KT):
                    sp.wait_ge(wo_l, k - 1)
                    sp.dma_start(wo_raw[:, k % 2], wov[:, k]).then_inc(wo_in[k % 2], 16)

                def again(t, s):
                    sp.wait_ge(y_l, t - 1)
                    wait_apart(sp, z_rdy, t - 1, tick)
                    load(t, s)
                with sp.Fori(1, LAST // 2) as i:
                    for s in range(2):
                        again(i * 2 + s, s)
                again(LAST, 0)

            @block.scalar
            def _(act):
                act.dma_start(w_rt[:, :, 0:NG], io["w_router_group"][0].rearrange("(k p) n -> p k n", p=P)).then_inc(rt_in, 16)
                act.dma_start(w_rt[:, :, NG:NG + NE], io["w_router_expert"][0].rearrange("(k p) n -> p k n", p=P)).then_inc(rt_in, 16)
                act.dma_start(ln1[:, 0, :], row_bcast(io["ln_g"][0, 0], P)).then_inc(ln_in, 16)
                act.dma_start(ln1[:, 1, :], row_bcast(io["ln_b"][0, 0], P)).then_inc(ln_in, 16)

                def hi(t, s, n_in):
                    n = rows_of(t)
                    act.wait_ge(y_in[s], n_in)
                    act.activation(y_hi[:, s, :, 0:n], y_raw[:, s, :, 0:n], ACT.Copy).then_inc(y_h, 1)

                def to_sb(t):
                    n = rows_of(t)
                    act.wait_ge(uT_ps, t + 1)
                    act.activation(u2T[:, :, 0:n], px[:, :].rearrange("p (k t) -> p k t", k=KT)[:, :, 0:n], ACT.Copy).then_inc(uT_sb, 1)

                hi(0, 0, 16)
                hi(1, 1, 16)
                for k in range(KT):
                    act.wait_ge(wo_in[k % 2], 16 * (k // 2) + 16)
                    act.activation(wo_hi[:, k], wo_raw[:, k % 2], ACT.Copy).then_inc(wo_h, 1)
                for n in range(12):
                    act.wait_ge(bc_ps, n + 1)
                    v, hf, p_ = n // 2 % 3, n % 2, n < 6
                    dst = (mod_p if p_ else mod_s)[:, v, hf * 512:(hf + 1) * 512]
                    act.activation(dst, pm[n % 2][0:(P if p_ else NSAMP), 0:512], ACT.Identity, bias=0.0 if v != 2 else 1.0).then_inc(bc_ev, 1)
                with act.Fori(0, (LAST - 2) // 2) as i:
                    for s in range(2):
                        act.wait_ge(prod, 2 * i + s + 1)
                        hi(2 * i + s + 2, s, 16 * i + 32)
                        to_sb(2 * i + s)
                act.wait_ge(prod, LAST - 1)
                hi(LAST, 0, 16 * (LAST // 2) + 16)
                for t in range(LAST - 2, T):
                    to_sb(t)

            @block.gpsimd
            def _(pool):
                pool.memset(zero_row[:, :], 0.0).then_inc(zr_rdy, 1)
                pool.iota(slot_i[:, :], pattern=[[1, NLIST]], base=0, channel_multiplier=NLIST)
                pool.iota(fill[:, :, 0], pattern=[[0, NLIST]], base=NTOK, channel_multiplier=0)
                pool.memset(fill[:, :, 2:4], 0)
                pool.memset(logits[:, LAST, :], 0.0)
                pool.drain().then_inc(consts, 1)
                pool.wait_ge(zr_rdy, 1)
                pool.dma_start(scr["u2"][NTOK:NTOK + 1, :], zero_row[:, :]).then_inc(zr_out, 16)
                pool.wait_ge(fill_rdy, 1)
                pool.dma_start(scr["list"].rearrange("(p s) c -> p (s c)", p=P), fill[:, :, :].rearrange("p s c -> p (s c)")).then_inc(fill_out, 16)
                pool.wait_ge(ln_in, 32)
                pool.wait_ge(bc_ev, 12)

                pool.sem_inc(st_done, 1)

                def tile(t):
                    n = rows_of(t)
                    m = mod_s if n < P else mod_p
                    pool.wait_ge(var_rdy, t + 1)
                    pool.tensor_tensor(rstd[0:n, :], ve[0:n, :], neg_half[0:n, 0:1], ALU.pow).then_inc(rs_rdy, 1)
                    pool.wait_ge(x1_rdy, t + 1)
                    pool.dma_start(scr["x1"][bass.ds(t * P, n), :], x1[0:n, :]).then_inc(x1_out, 16)
                    pool.tensor_tensor(u2m[0:n, :], x1[0:n, :], m[0:n, 2, :], ALU.mult)
                    pool.drain()
                    pool.tensor_tensor(u2[0:n, :], u2m[0:n, :], m[0:n, 1, :], ALU.add)
                    pool.drain().then_inc(u2_rdy, 1)
                    pool.dma_start(scr["u2"][bass.ds(t * P, n), :], u2[0:n, :]).then_inc(u2_out, 16)
                    wait_apart(pool, x1_out, 16 * t + 16, tick)
                    wait_apart(pool, u2_out, 16 * t + 16, tick)
                    wait_apart(pool, uT_ps, t + 1, tick)
                    pool.sem_inc(st_done, 1)
                with pool.Fori(0, LAST) as t:
                    tile(t)
                tile(LAST)
                pool.wait_ge(zr_out, 16)
                pool.wait_ge(fill_out, 16)

            @block.tensor
            def _(pe):
                pe.wait_ge(mod_in, 16)
                for n in range(12):
                    v, hf, p_ = n // 2 % 3, n % 2, n < 6
                    if n >= 2:
                        pe.wait_ge(bc_ev, n - 1)
                    sel = keep["sel_p"] if p_ else keep["sel_s"]
                    pe.matmul(pm[n % 2][0:(P if p_ else NSAMP), 0:512], sel[:, :],
                              mod_rows[:, v * D + hf * 512:v * D + (hf + 1) * 512], start=True, stop=True).then_inc(bc_ps, 1)
                pe.wait_ge(wo_l, KT)
                pe.wait_ge(bc_ev, 12)
                pe.wait_ge(rt_in, 32)

                def project(t, s):
                    n = rows_of(t)
                    pe.wait_ge(y_l, t + 1)
                    if not (isinstance(t, int) and t < 2):
                        pe.wait_ge(z_rdy, t - 1)
                    for k in range(KT):
                        for m, (a, w) in enumerate(((y_hi, wo_hi), (y_hi, wo_lo), (y_lo, wo_hi))):
                            for hf in range(2):
                                last = pe.matmul(pm[s][0:n, hf * 512:(hf + 1) * 512], a[:, s, k, 0:n],
                                                 w[:, k, hf * 512:(hf + 1) * 512],
                                                 start=(k == 0 and m == 0), stop=(k == KT - 1 and m == 2))
                    last.then_inc(prod, 1)

                def route(t):
                    n = rows_of(t)
                    pe.wait_ge(u2_rdy, t + 1)
                    if not (isinstance(t, int) and t < 1):
                        pe.wait_ge(uT_sb, t)
                    for k in range(KT):
                        last = pe.transpose(px[:, k * P:k * P + n], u2[0:n, k * P:(k + 1) * P], ident[0:n, 0:n])
                    last.then_inc(uT_ps, 1)
                    pe.wait_ge(uT_sb, t + 1)
                    if not (isinstance(t, int) and t < 1):
                        pe.wait_ge(lg_sb, t)
                    for k in range(KT):
                        last = pe.matmul(pl[0:n, 0:NG + NE], u2T[:, k, 0:n], w_rt[:, k, :], start=(k == 0), stop=(k == KT - 1))
                    last.then_inc(lg_ps, 1)

                project(0, 0)
                project(1, 1)
                route(0)
                with pe.Fori(1, LAST // 2) as i:
                    project(2 * i, 0)
                    route(2 * i - 1)
                    project(2 * i + 1, 1)
                    route(2 * i)
                project(LAST, 0)
                route(LAST - 1)
                route(LAST)

            @block.vector
            def _(dve):
                def lo(t, s):
                    n = rows_of(t)
                    dve.wait_ge(y_h, t + 1)
                    dve.tensor_tensor(y_lo[:, s, :, 0:n], y_raw[:, s, :, 0:n], y_hi[:, s, :, 0:n].bitcast(F32), ALU.subtract).then_inc(y_l, 1)

                def norm(t, s, x_n):
                    n = rows_of(t)
                    m = mod_s if n < P else mod_p
                    dve.wait_ge(prod, t + 1)
                    dve.tensor_tensor(z[0:n, :], pm[s][0:n, :], m[0:n, 0, :], ALU.mult)
                    dve.drain()
                    dve.wait_ge(x_in[s], x_n)
                    dve.scalar_tensor_tensor(z2[0:n, :], x_t[0:n, s, :], ALPHA, z[0:n, :], ALU.mult, ALU.add)
                    dve.drain().then_inc(z_rdy, 1)
                    for a in range(2):
                        dve.bn_stats(stats[0:n, a, :], z2[0:n, a * 512:(a + 1) * 512])
                    dve.drain()
                    dve.bn_aggr(mv[0:n, :], stats[0:n, :, :])
                    dve.drain()
                    dve.tensor_scalar(ve[0:n, :], mv[0:n, 1:2], LN_EPS, None, ALU.add).then_inc(var_rdy, 1)
                    dve.wait_ge(rs_rdy, t + 1)
                    dve.tensor_scalar(zn[0:n, :], z2[0:n, :], mv[0:n, 0:1], rstd[0:n, :], ALU.subtract, ALU.mult)
                    dve.drain()
                    dve.tensor_tensor(z[0:n, :], zn[0:n, :], ln1[0:n, 0, :], ALU.mult)
                    dve.drain()
                    if not (isinstance(t, int) and t < 1):
                        dve.wait_ge(st_done, t + 1)
                    dve.tensor_tensor(x1[0:n, :], z[0:n, :], ln1[0:n, 1, :], ALU.add).then_inc(x1_rdy, 1)

                def keep_logits(t):
                    n = rows_of(t)
                    dve.wait_ge(lg_ps, t + 1)
                    dst = logits[0:n, bass.ds(t, 1), :].rearrange("p a c -> p (a c)")
                    dve.tensor_copy(dst, pl[0:n, 0:NG + NE]).then_inc(lg_sb, 1)

                dve.wait_ge(consts, 1)
                dve.tensor_scalar(slot_i[:, :], slot_i[:, :], P - 1, None, ALU.bitwise_and)
                dve.drain()
                dve.tensor_scalar(fill[:, :, 1], slot_i[:, :], 2 * NTOK, None, ALU.add)
                dve.drain().then_inc(fill_rdy, 1)
                lo(0, 0)
                lo(1, 1)
                for k in range(KT):
                    dve.wait_ge(wo_h, k + 1)
                    dve.tensor_tensor(wo_lo[:, k], wo_raw[:, k % 2], wo_hi[:, k].bitcast(F32), ALU.subtract).then_inc(wo_l, 1)
                dve.wait_ge(bc_ev, 12)
                dve.wait_ge(ln_in, 32)
                with dve.Fori(0, (LAST - 2) // 2) as i:
                    for s in range(2):
                        norm(2 * i + s, s, 16 * i + 16)
                        lo(2 * i + s + 2, s)
                        keep_logits(2 * i + s)
                norm(LAST - 2, 0, 16 * (LAST // 2))
                lo(LAST, 0)
                keep_logits(LAST - 2)
                norm(LAST - 1, 1, 16 * (LAST // 2))
                keep_logits(LAST - 1)
                norm(LAST, 0, 16 * (LAST // 2) + 16)
                keep_logits(LAST)


def gate_up_w(buf, s):
    return buf[:, bass.ds(s, 1), 0:KT * 2 * DE].rearrange("p a (k c f) -> p (a k) c f", k=KT, c=2)


def load_gate_up(eng, io, keep, e, s):
    for c, (w, landed) in enumerate((("w_e_gate", "wg_in"), ("w_e_up", "wu_in"))):
        eng.dma_start(gate_up_w(keep["gu_raw"], s)[:, :, c, :],
                      io[w][0, bass.ds(e, 1)].rearrange("e (k p) f -> p (e k) f", p=P)).then_inc(keep[landed], 16)


def load_down(eng, io, keep, e, s):
    eng.dma_start(keep["dn_w"][:, bass.ds(s, 1), :].rearrange("p a (k n) -> p (a k) n", k=DE // P),
                  io["w_e_down"][0, bass.ds(e, 1)].rearrange("e (k p) n -> p (e k) n", p=P)).then_inc(keep["wd_in"], 16)


def routing_phase(nc, io, keep, scr):
    ones, tri, logits = keep["ones"], keep["tri"], keep["logits"]
    blk_tab, exp_tab = keep["blk_tab"], keep["exp_tab"]
    T = TILES
    LAST = T - 1
    with ExitStack() as ctx:
        sb = lambda name, shape, dt=F32: ctx.enter_context(nc.sbuf_tensor(name, shape, dt))
        ps = lambda name, shape: ctx.enter_context(nc.psum_tensor(name, shape, F32))
        sem = lambda name: ctx.enter_context(nc.semaphore(name))
        gmax, gsum, psel, gidx = (sb(n, [P, T]) for n in ("gmax", "gsum", "psel", "gidx"))
        gd, gs1, gs2, gr, ge, gq = (sb(n, [P, T, NG]) for n in ("gd", "gs1", "gs2", "gr", "ge", "gq"))
        lem, lem2, eq1, oh1, oh2, posf, tmp = (sb(n, [P, T, NE]) for n in ("lem", "lem2", "eq1", "oh1", "oh2", "posf", "tmp"))
        mm = sb("mm", [P, T, NE])
        m1, m2, e1, dm, w1, w2 = (sb(n, [P, T]) for n in ("m1", "m2", "e1", "dm", "w1", "w2"))
        valid = sb("valid", [P, T])
        base = sb("base", [P, T + 1, NE])
        dest_f = sb("dest_f", [P, T, 2])
        dest = sb("dest", [P, T, 2], I32)
        rows = sb("rows", [P, T, 2, 4], I32)
        cj_g = sb("cj_g", [P, NG])
        cj_e = sb("cj_e", [P, NE])
        ecap = sb("ecap", [P, NE])
        pidx = sb("pidx", [P, 1])
        cnt = sb("cnt", [P, NE])
        cnt_i = sb("cnt_i", [P, NE], I32)
        nb_i = sb("nb_i", [P, NE], I32)
        nb = sb("nb", [P, NE])
        cum = sb("cum", [P, 2, NE])
        cmp_, cmp2 = sb("cmp_", [P, NE]), sb("cmp2", [P, NE])
        eg, gst = sb("eg", [P, 1]), sb("gst", [P, 1])
        odd = sb("odd", [1, 1], I32)
        tab_f = sb("tab_f", [P, 2])
        tab_i = sb("tab_i", [P, 2], I32)
        pm = [ps("pr_rank", [P, 1024]), ps("pr_total", [P, 1024])]
        consts = sem("consts_r")
        r_dve, r_act, r_pe, rows_rdy = sem("r_dve"), sem("r_act"), sem("r_pe"), sem("rows_rdy")
        sc_out, tab_rdy, tab_out, tab_in = sem("sc_out"), sem("tab_rdy"), sem("tab_out"), sem("tab_in")

        def rows_of(t):
            return NSAMP if t == LAST else P

        with nc.Block() as block:
            @block.sync
            def _(sp):
                load_gate_up(sp, io, keep, 0, 0)
                load_down(sp, io, keep, 0, 0)
                sp.wait_ge(keep["wg_in"], 16)
                sp.wait_ge(keep["wu_in"], 16)
                load_gate_up(sp, io, keep, 1, 1)
                sp.wait_ge(tab_rdy, 1)
                sp.dma_start(scr["tab"], tab_i[:, :]).then_inc(tab_out, 16)
                sp.wait_ge(tab_out, 16)
                sp.dma_start(blk_tab[:, :], scr["tab"].rearrange("(a g) c -> a (g c)", a=1)).then_inc(tab_in, 16)
                sp.wait_ge(tab_in, 16)

            @block.scalar
            def _(act):
                act.wait_ge(r_dve, 1)
                act.activation(gs1[:, :, :], gd[:, :, :], ACT.Sigmoid)
                act.activation(gs2[:, :, :], gd[:, :, :], ACT.Sigmoid, scale=-1.0).then_inc(r_act, 1)
                act.wait_ge(r_dve, 2)
                act.activation(w1[:, :], dm[:, :], ACT.Sigmoid)
                act.activation(w2[:, :], dm[:, :], ACT.Sigmoid, scale=-1.0).then_inc(r_act, 1)

            @block.gpsimd
            def _(pool):
                pool.iota(rows[:, :, 0, 0], pattern=[[P, T]], base=0, channel_multiplier=1)
                pool.iota(rows[:, :, 1, 0], pattern=[[P, T]], base=0, channel_multiplier=1)
                pool.iota(rows[:, :, 0, 1], pattern=[[2 * P, T]], base=0, channel_multiplier=2)
                pool.iota(rows[:, :, 1, 1], pattern=[[2 * P, T]], base=1, channel_multiplier=2)
                pool.memset(rows[:, :, :, 3], 0)
                pool.iota(cj_g[:, :], pattern=[[1, NG]], base=-NG, channel_multiplier=0, allow_small_or_imprecise_dtypes=True)
                pool.iota(cj_e[:, :], pattern=[[1, NE]], base=-NE, channel_multiplier=0, allow_small_or_imprecise_dtypes=True)
                pool.iota(ecap[:, :], pattern=[[CAP, NE]], base=0, channel_multiplier=0, allow_small_or_imprecise_dtypes=True)
                pool.iota(pidx[:, :], pattern=[[0, 1]], base=0, channel_multiplier=1, allow_small_or_imprecise_dtypes=True)
                pool.memset(valid[:, :], 1.0)
                pool.drain()
                pool.memset(valid[NSAMP:P, LAST:T], 0.0)
                pool.drain().then_inc(consts, 1)
                pool.wait_ge(rows_rdy, 1)
                for t in range(T):
                    n = rows_of(t)
                    for k in range(2):
                        pool.indirect_dma_start(scr["list"], bass.IndirectOffsetOnAxis(ap=dest[0:n, t, k:k + 1], axis=0),
                                                rows[0:n, t, k, :], None).then_inc(sc_out, 16)
                pool.wait_ge(sc_out, 16 * 2 * T)

            @block.tensor
            def _(pe):
                pe.wait_ge(r_dve, 3)
                mf = mm[:, :, :].rearrange("p t e -> p (t e)")
                n1 = 512
                n2 = T * NE - n1
                pe.matmul(pm[0][:, 0:n1], tri[:, :], mf[:, 0:n1], start=True, stop=True)
                pe.matmul(pm[0][:, 512:512 + n2], tri[:, :], mf[:, n1:n1 + n2], start=True, stop=True)
                pe.matmul(pm[1][:, 0:n1], ones[:, :], mf[:, 0:n1], start=True, stop=True)
                pe.matmul(pm[1][:, 512:512 + n2], ones[:, :], mf[:, n1:n1 + n2], start=True, stop=True).then_inc(r_pe, 1)

            @block.vector
            def _(dve):
                dve.wait_ge(consts, 1)
                def over(ap, n):
                    return ap.rearrange("p (t a) -> p t a", a=1).broadcast_to([P, T, n])

                def const(ap, n):
                    return ap.rearrange("p (a j) -> p a j", a=1).broadcast_to([P, T, n])

                lg, le = logits[:, :, 0:NG], logits[:, :, NG:NG + NE]
                dve.tensor_reduce(gmax[:, :], lg, axis=AX.X, op=ALU.max)
                dve.drain()
                dve.tensor_tensor(gd[:, :, :], lg, over(gmax[:, :], NG), ALU.subtract)
                dve.drain().then_inc(r_dve, 1)
                dve.tensor_scalar(gq[:, :, :], gd[:, :, :], 0.0, None, ALU.is_equal)
                dve.drain()
                dve.tensor_tensor(ge[:, :, :], gq[:, :, :], const(cj_g[:, :], NG), ALU.mult)
                dve.drain()
                dve.tensor_reduce(gidx[:, :], ge[:, :, :], axis=AX.X, op=ALU.min)
                dve.drain()
                dve.tensor_tensor(gq[:, :, :], const(cj_g[:, :], NG), over(gidx[:, :], NG), ALU.is_equal)
                dve.drain()
                dve.tensor_scalar(gq[:, :, :], gq[:, :, :], -1.0, BIG, ALU.add, ALU.mult)
                dve.drain()
                pen = gq[:, :, :].rearrange("p t (g a) -> p (t g) a", a=1).broadcast_to([P, T * NG, EPG])
                dve.tensor_copy(tmp[:, :, :], le)
                dve.drain()
                dve.tensor_tensor(lem[:, :, :].rearrange("p t (g e) -> p (t g) e", e=EPG),
                                  tmp[:, :, :].rearrange("p t (g e) -> p (t g) e", e=EPG), pen, ALU.add)
                dve.wait_ge(r_act, 1)
                dve.reciprocal(gr[:, :, :], gs2[:, :, :])
                dve.drain()
                dve.tensor_tensor(ge[:, :, :], gs1[:, :, :], gr[:, :, :], ALU.mult)
                dve.drain()
                dve.tensor_reduce(gsum[:, :], ge[:, :, :], axis=AX.X, op=ALU.add)
                dve.drain()
                dve.reciprocal(psel[:, :], gsum[:, :])

                def top(src, val, onehot):
                    dve.tensor_reduce(val[:, :], src[:, :, :], axis=AX.X, op=ALU.max)
                    dve.drain()
                    dve.tensor_tensor(eq1[:, :, :], src[:, :, :], over(val[:, :], NE), ALU.is_equal)
                    dve.drain()
                    dve.tensor_tensor(tmp[:, :, :], eq1[:, :, :], const(cj_e[:, :], NE), ALU.mult)
                    dve.drain()
                    dve.tensor_reduce(e1[:, :], tmp[:, :, :], axis=AX.X, op=ALU.min)
                    dve.drain()
                    dve.tensor_tensor(onehot[:, :, :], const(cj_e[:, :], NE), over(e1[:, :], NE), ALU.is_equal)
                    dve.drain()

                top(lem, m1, oh1)
                dve.scalar_tensor_tensor(lem2[:, :, :], oh1[:, :, :], -BIG, lem[:, :, :], ALU.mult, ALU.add)
                dve.drain()
                top(lem2, m2, oh2)
                dve.tensor_tensor(dm[:, :], m1[:, :], m2[:, :], ALU.subtract)
                dve.drain().then_inc(r_dve, 1)
                dve.tensor_tensor(tmp[:, :, :], oh1[:, :, :], oh2[:, :, :], ALU.add)
                dve.drain()
                dve.tensor_tensor(mm[:, :, :], tmp[:, :, :], over(valid[:, :], NE), ALU.mult)
                dve.drain().then_inc(r_dve, 1)
                dve.wait_ge(r_act, 2)
                dve.tensor_tensor(rows[:, :, 0, 2].bitcast(F32), psel[:, :], w1[:, :], ALU.mult)
                dve.tensor_tensor(rows[:, :, 1, 2].bitcast(F32), psel[:, :], w2[:, :], ALU.mult)
                dve.tensor_copy(base[:, 0, :], ecap[:, :])
                dve.drain()
                dve.wait_ge(r_pe, 1)
                for t in range(T):
                    dve.tensor_tensor(base[:, t + 1, :], base[:, t, :], pm[1][:, t * NE:(t + 1) * NE], ALU.add)
                    dve.drain()
                dve.tensor_tensor(posf[:, :, :].rearrange("p t e -> p (t e)"), pm[0][:, 0:T * NE],
                                  base[:, 0:T, :].rearrange("p t e -> p (t e)"), ALU.add)
                dve.drain()
                for k, oh in enumerate((oh1, oh2)):
                    dve.tensor_tensor(tmp[:, :, :], posf[:, :, :], oh[:, :, :], ALU.mult)
                    dve.drain()
                    dve.tensor_reduce(dest_f[:, :, k], tmp[:, :, :], axis=AX.X, op=ALU.add)
                    dve.drain()
                dve.tensor_copy(dest[:, :, :], dest_f[:, :, :])
                dve.drain().then_inc(rows_rdy, 1)
                dve.tensor_tensor(cnt[:, :], base[:, T, :], ecap[:, :], ALU.subtract)
                dve.drain()
                dve.tensor_scalar(cnt[:, :], cnt[:, :], float(P - 1), None, ALU.add)
                dve.drain()
                dve.tensor_copy(cnt_i[:, :], cnt[:, :])
                dve.drain()
                dve.tensor_scalar(nb_i[:, :], cnt_i[:, :], 7, None, ALU.logical_shift_right)
                dve.drain()
                dve.tensor_copy(nb[:, :], nb_i[:, :])
                dve.drain()
                dve.tensor_scalar(nb[:, :], nb[:, :], 1.0, None, ALU.max)
                dve.drain()
                dve.tensor_copy(cum[:, 0, :], nb[:, :])
                dve.drain()
                src = 0
                step = 1
                while step < NE:
                    dve.tensor_copy(cum[:, 1 - src, 0:step], cum[:, src, 0:step])
                    dve.tensor_tensor(cum[:, 1 - src, step:NE], cum[:, src, step:NE], cum[:, src, 0:NE - step], ALU.add)
                    dve.drain()
                    src, step = 1 - src, step * 2
                dve.memset(exp_tab[:, 0:1], 0)
                dve.tensor_copy(exp_tab[:, 1:NE + 1], cum[0:1, src, :])
                dve.drain()
                dve.tensor_scalar(odd[:, :], exp_tab[:, NE:NE + 1], 1, None, ALU.bitwise_and)
                dve.drain()
                dve.tensor_tensor(exp_tab[:, NE:NE + 1], exp_tab[:, NE:NE + 1], odd[:, :], ALU.add)
                dve.tensor_scalar(cmp_[:, :], cum[:, src, :], pidx[:, :], None, ALU.is_le)
                dve.drain()
                dve.tensor_reduce(eg[:, :], cmp_[:, :], axis=AX.X, op=ALU.add)
                dve.tensor_tensor(cmp2[:, :], cmp_[:, :], nb[:, :], ALU.mult)
                dve.drain()
                dve.tensor_reduce(gst[:, :], cmp2[:, :], axis=AX.X, op=ALU.add)
                dve.tensor_scalar(tab_f[:, 0:1], eg[:, :], float(NE - 1), None, ALU.min)
                dve.drain()
                dve.tensor_tensor(gst[:, :], pidx[:, :], gst[:, :], ALU.subtract)
                dve.tensor_scalar(eg[:, :], eg[:, :], float(CAP // P), None, ALU.mult)
                dve.drain()
                dve.tensor_tensor(tab_f[:, 1:2], eg[:, :], gst[:, :], ALU.add)
                dve.drain()
                dve.tensor_copy(tab_i[:, :], tab_f[:, :])
                dve.drain().then_inc(tab_rdy, 1)


def expert_phase(nc, io, keep, scr):
    ident, blk_tab, exp_tab = keep["ident"], keep["blk_tab"], keep["exp_tab"]
    gu_raw, gu_hi, gu_lo, dn_w = keep["gu_raw"], keep["gu_hi"], keep["gu_lo"], keep["dn_w"]
    wg_in, wu_in, wd_in = keep["wg_in"], keep["wu_in"], keep["wd_in"]
    KD = DE // P
    GU = 2 * DE
    WG = KT * GU
    AHEAD = 4
    RING = 8
    MAXB = 2 * TILES + NE
    with ExitStack() as ctx:
        sb = lambda name, shape, dt=F32: ctx.enter_context(nc.sbuf_tensor(name, shape, dt))
        ps = lambda name, shape: ctx.enter_context(nc.psum_tensor(name, shape, F32))
        sem = lambda name: ctx.enter_context(nc.semaphore(name))
        xg = sb("xg", [P, 2, D])
        x_hi = sb("x_hi", [P, KT, P], F32R)
        x_lo = sb("x_lo", [P, KT, P], F32R)
        gsig = sb("gsig", [P, DE])
        gsil = sb("gsil", [P, DE])
        hh = sb("hh", [P, DE])
        hhT = sb("hhT", [P, KD, P])
        y_sb = sb("y_sb", [P, D])
        ids_ring = sb("ids_ring", [P, RING, 4], I32)
        ids_now = sb("ids_now", [P, 4], I32)
        ids_cur = sb("ids_cur", [P, 4], I32)
        ph = ps("ph", [P, 512])
        px = ps("pxe", [P, 1024])
        pht = ps("pht", [P, 512])
        py = ps("py", [P, 1024])
        ids_in, xg_in, y_out = sem("ids_in"), sem("xg_in"), sem("y2_out")
        gu_h, gu_l = sem("gu_h"), sem("gu_l")
        xT_ps, x_h, x_l = sem("xTe_ps"), sem("xe_h"), sem("xe_l")
        gu, sig, h_rdy = sem("gu_done"), sem("sig_done"), sem("h_rdy")
        hT, hT_sb = sem("hT_ps"), sem("hT_sb")
        dn, y_rdy, cur = sem("dn_done"), sem("y_rdy"), sem("cur_rdy")
        kept = sem("kept")
        tick = sem("tick3")

        def slot(buf, s, lo, hi):
            return buf[:, bass.ds(s, 1), lo:hi].rearrange("p a w -> p (a w)")

        def blocks_before(eng, e):
            return eng.value_load(exp_tab[0:1, bass.ds(e, 1)], min_val=0, max_val=MAXB)

        def expert_loop(eng, split_gu, block_work):
            def expert(e, gu_next):
                first = blocks_before(eng, e)
                last = eng.snap(eng.value_load(exp_tab[0:1, bass.ds(e + 1, 1)], min_val=1, max_val=MAXB) - 1)
                with eng.If_lt(eng.to_reg(first), eng.to_reg(last)):
                    with eng.Fori(first, last) as g:
                        block_work(g, None)
                if gu_next is not None:
                    split_gu(gu_next, 0, last)
                block_work(last, gu_next)
            with eng.Fori(0, NE - 2) as e:
                expert(e, e + 2)
            expert(NE - 2, None)
            expert(NE - 1, None)

        with nc.Block() as block:
            @block.sync
            def _(sp):
                def gate_up(e, s):
                    if not (isinstance(e, int) and e < RAW):
                        wait_apart(sp, gu_l, 2 * (e - RAW) + 2, tick)
                    for landed in (wg_in, wu_in):
                        wait_apart(sp, landed, 16 * e, tick)
                    load_gate_up(sp, io, keep, e, s)

                def down(e, s):
                    if not (isinstance(e, int) and e < RAW):
                        wait_apart(sp, dn, blocks_before(sp, e - (RAW - 1)) + 1, tick)
                    wait_apart(sp, wd_in, 16 * e, tick)
                    load_down(sp, io, keep, e, s)

                gate_up(2, 2)
                down(1, 1)
                gate_up(3, 0)
                down(2, 2)
                with sp.Fori(4, NE) as e:
                    gate_up(e, sp.snap(e % RAW))
                    down(e - 1, sp.snap((e - 1) % RAW))
                down(NE - 1, (NE - 1) % RAW)

            @block.gpsimd
            def _(pool):
                total = blocks_before(pool, NE)

                def place(buf, i):
                    return buf[:, bass.ds(i, 1), :].rearrange("p a c -> p (a c)")

                def fetch_ids(b, at_ring):
                    at = pool.value_load(blk_tab[0:1, bass.ds(2 * b + 1, 1)], min_val=0, max_val=(NE + 1) * (CAP // P) - 1)
                    pool.dma_start(place(ids_ring, at_ring), scr["list"][bass.ds(at * P, P), :]).then_inc(ids_in, 16)

                def gather(b, at_ring, half):
                    pool.tensor_copy(ids_now[:, :], place(ids_ring, at_ring)).then_inc(kept, 1)
                    wait_apart(pool, kept, b + 1, tick)
                    pool.indirect_dma_start(xg[:, half, :], None, scr["u2"],
                                            bass.IndirectOffsetOnAxis(ap=ids_now[:, 0:1], axis=0)).then_inc(xg_in, 16)

                fetch_ids(0, 0)
                for b in range(AHEAD):
                    pool.wait_ge(ids_in, 16 * b + 16)
                    fetch_ids(b + 1, b + 1)
                    if b:
                        pool.wait_ge(xg_in, 16 * b)
                    if b >= 2:
                        pool.wait_ge(xT_ps, b - 1)
                    gather(b, b, b % 2)

                def block(g, half):
                    ahead = g + AHEAD
                    wait_apart(pool, ids_in, 16 * ahead + 16, tick)
                    fetch_ids(ahead + 1, (ahead + 1) % RING)
                    wait_apart(pool, xg_in, 16 * ahead, tick)
                    wait_apart(pool, xT_ps, ahead - 1, tick)
                    gather(ahead, ahead % RING, half)
                    if not (isinstance(g, int) and g == 0):
                        wait_apart(pool, y_out, 16 * g, tick)
                    pool.tensor_copy(ids_cur[:, :], place(ids_ring, g % RING)).then_inc(cur, 1)
                    wait_apart(pool, cur, g + 1, tick)
                    wait_apart(pool, y_rdy, g + 2, tick)
                    pool.indirect_dma_start(scr["y2"], bass.IndirectOffsetOnAxis(ap=ids_cur[:, 1:2], axis=0), y_sb[:, :], None).then_inc(y_out, 16)

                block(0, 0)
                block(1, 1)
                with pool.Fori(2, total, 2) as g:
                    block(g, 0)
                    block(pool.snap(g + 1), 1)
                wait_apart(pool, y_out, 16 * total, tick)
                wait_apart(pool, ids_in, 16 * total + 16 * (AHEAD + 1), tick)
                wait_apart(pool, xg_in, 16 * total + 16 * AHEAD, tick)

            @block.scalar
            def _(act):
                def split_gu(e, a, last=None):
                    s, r = (e, e) if isinstance(e, int) else (act.snap(e % 2), act.snap(e % RAW))
                    if a == 0:
                        act.wait_ge(wg_in, 16 * e + 16)
                        act.wait_ge(wu_in, 16 * e + 16)
                    if last is not None:
                        act.wait_ge(gu, last + 1)
                    lo, hi = a * (WG // 2), (a + 1) * (WG // 2)
                    act.activation(slot(gu_hi, s, lo, hi), slot(gu_raw, r, lo, hi), ACT.Copy).then_inc(gu_h, 1)

                def x_evac(b):
                    act.wait_ge(xT_ps, b + 1)
                    act.activation(x_hi[:, :, :], px[:, :].rearrange("p (k t) -> p k t", k=KT), ACT.Copy).then_inc(x_h, 1)

                def sigmoid(b):
                    act.wait_ge(gu, b + 1)
                    act.activation(gsig[:, :], ph[:, 0:DE], ACT.Sigmoid).then_inc(sig, 1)

                def block_work(g, gu_next):
                    act.wait_ge(hT, g + 1)
                    act.activation(hhT[:, :, :], pht[:, 0:KD * P].rearrange("p (k t) -> p k t", k=KD), ACT.Copy).then_inc(hT_sb, 1)
                    sigmoid(g + 1)
                    x_evac(g + 2)
                    if gu_next is not None:
                        split_gu(gu_next, 1)
                    act.wait_ge(dn, g + 2)
                    act.wait_ge(cur, g + 1)
                    act.activation(y_sb[:, :], py[:, :], ACT.Copy, scale=ids_cur[:, 2:3].bitcast(F32)).then_inc(y_rdy, 1)

                act.sem_inc(y_rdy, 1)
                split_gu(0, 0)
                split_gu(0, 1)
                x_evac(0)
                split_gu(1, 0)
                split_gu(1, 1)
                sigmoid(0)
                x_evac(1)
                expert_loop(act, split_gu, block_work)

            @block.vector
            def _(dve):
                def split_gu(e, a, last=None):
                    s, r = (e, e) if isinstance(e, int) else (dve.snap(e % 2), dve.snap(e % RAW))
                    lo, hi = a * (WG // 2), (a + 1) * (WG // 2)
                    dve.wait_ge(gu_h, 2 * e + (a + 1))
                    dve.tensor_tensor(slot(gu_lo, s, lo, hi), slot(gu_raw, r, lo, hi),
                                      slot(gu_hi, s, lo, hi).bitcast(F32), ALU.subtract).then_inc(gu_l, 1)

                def x_evac(b):
                    dve.wait_ge(x_h, b + 1)
                    dve.tensor_tensor(x_lo[:, :, :], px[:, :].rearrange("p (k t) -> p k t", k=KT), x_hi[:, :, :].bitcast(F32), ALU.subtract).then_inc(x_l, 1)

                def gate(b):
                    dve.wait_ge(sig, b + 1)
                    dve.tensor_tensor(gsil[:, :], ph[:, 0:DE], gsig[:, :], ALU.mult)
                    dve.drain()
                    dve.tensor_tensor(hh[:, :], ph[:, DE:GU], gsil[:, :], ALU.mult).then_inc(h_rdy, 1)

                def block_work(g, gu_next):
                    gate(g + 1)
                    x_evac(g + 2)
                    if gu_next is not None:
                        split_gu(gu_next, 1)

                split_gu(0, 0)
                split_gu(0, 1)
                x_evac(0)
                split_gu(1, 0)
                split_gu(1, 1)
                gate(0)
                x_evac(1)
                expert_loop(dve, split_gu, block_work)

            @block.tensor
            def _(pe):
                total = blocks_before(pe, NE)

                def expert_of(b):
                    return pe.value_load(blk_tab[0:1, bass.ds(2 * b, 1)], min_val=0, max_val=NE - 1)

                def transposes(b, half):
                    pe.wait_ge(xg_in, 16 * b + 16)
                    if not (isinstance(b, int) and b == 0):
                        pe.wait_ge(x_l, b)
                    for k in range(KT):
                        last = pe.transpose(px[:, k * P:(k + 1) * P], xg[:, half, k * P:(k + 1) * P], ident[:, :])
                    last.then_inc(xT_ps, 1)

                def gate_up(b, e, s):
                    pe.wait_ge(gu_l, 2 * e + 1)
                    pe.wait_ge(x_l, b + 1)
                    if not (isinstance(b, int) and b == 0):
                        pe.wait_ge(h_rdy, b)
                    for k in range(KT):
                        if k == KT // 2:
                            pe.wait_ge(gu_l, 2 * e + 2)
                        for m, (x, w) in enumerate(((x_hi, gu_hi), (x_hi, gu_lo), (x_lo, gu_hi))):
                            last = pe.matmul(ph[:, :], x[:, k, :], slot(w, s, k * GU, (k + 1) * GU),
                                             start=(k == 0 and m == 0), stop=(k == KT - 1 and m == 2))
                    last.then_inc(gu, 1)

                pe.sem_inc(dn, 1)
                transposes(0, 0)
                gate_up(0, 0, 0)
                transposes(1, 1)
                def block_step(g, half):
                    e_now, e_next = expert_of(g), expert_of(g + 1)
                    s_down, s_next = pe.snap(e_now % RAW), pe.snap(e_next % 2)
                    gate_up(g + 1, e_next, s_next)
                    pe.wait_ge(h_rdy, g + 1)
                    for k in range(KD):
                        last = pe.transpose(pht[:, k * P:(k + 1) * P], hh[:, k * P:(k + 1) * P], ident[:, :])
                    last.then_inc(hT, 1)
                    transposes(g + 2, half)
                    pe.wait_ge(hT_sb, g + 1)
                    pe.wait_ge(wd_in, 16 * e_now + 16)
                    pe.wait_ge(y_rdy, g + 1)
                    for k in range(KD):
                        for hf in range(2):
                            at = k * D + hf * 512
                            last = pe.matmul(py[:, hf * 512:(hf + 1) * 512], hhT[:, k, :], slot(dn_w, s_down, at, at + 512),
                                             start=(k == 0), stop=(k == KD - 1))
                    last.then_inc(dn, 1)

                with pe.Fori(0, total, 2) as g:
                    block_step(g, 0)
                    block_step(pe.snap(g + 1), 1)


def combine_phase(nc, io, keep, scr, outs):
    T = TILES
    LAST = T - 1
    with ExitStack() as ctx:
        sb = lambda name, shape, dt=F32: ctx.enter_context(nc.sbuf_tensor(name, shape, dt))
        ps = lambda name, shape: ctx.enter_context(nc.psum_tensor(name, shape, F32))
        sem = lambda name: ctx.enter_context(nc.semaphore(name))
        mod_rows = sb("mod_rows4", [1 + DEC_B, D])
        gate_p = sb("gate_p", [P, D])
        gate_s = sb("gate_s", [NSAMP, D])
        ln2 = sb("ln2", [P, 2, D])
        x1 = sb("x1_t", [P, 2, D])
        y2 = sb("y2_t", [P, 2, 2, D])
        ysum = sb("ysum", [P, 2, D])
        ga = sb("ga", [P, 2, D])
        z = sb("z4", [P, 2, D])
        zn = sb("zn4", [P, 2, D])
        o1 = sb("o1", [P, 2, D])
        o = sb("o_t", [P, 2, D])
        stats = sb("stats4", [P, 2, 6])
        mv = sb("mv4", [P, 2])
        ve = sb("ve4", [P, 1])
        rstd = sb("rstd4", [P, 1])
        pg = [ps("pg0", [P, 512]), ps("pg1", [P, 512])]
        mod_in, ln_in = sem("mod4_in"), sem("ln4_in")
        x_in = [sem("x4_in0"), sem("x4_in1")]
        y_in = [sem("y4_in0"), sem("y4_in1")]
        bc_ps, bc_ev, ysum_rdy, z_rdy, var_rdy, rs_rdy, o1_rdy, o_rdy = (
            sem(n + "4") for n in ("bc_ps", "bc_ev", "ysum_rdy", "z_rdy", "var_rdy", "rs_rdy", "o1_rdy", "o_rdy"))
        o_out = [sem("o_out0"), sem("o_out1")]
        o_free = sem("o_free")
        tick = sem("tick4")
        op, os_ = outs[0][0], outs[1].rearrange("b l d -> (b l) d")

        def rows_of(t):
            return NSAMP if isinstance(t, int) and t == LAST else P

        def tiles(eng, body):
            with eng.Fori(0, LAST // 2) as i:
                for s in range(2):
                    body(2 * i + s, s, i)
            body(LAST, 0, LAST // 2)

        with nc.Block() as block:
            @block.sync
            def _(sp):
                sp.dma_start(mod_rows[:, :], scr["mod"][:, 5 * D:6 * D]).then_inc(mod_in, 16)

                def load(t, s, i):
                    n = rows_of(t)
                    wait_apart(sp, z_rdy, t + 1, tick)
                    sp.dma_start(x1[0:n, s, :], scr["x1"][bass.ds(t * P, n), :]).then_inc(x_in[s], 16)
                    sp.dma_start(y2[0:n, s, :, :], scr["y2"][bass.ds(t * 2 * P, 2 * n), :].rearrange("(p k) d -> p k d", k=2)).then_inc(y_in[s], 16)
                tiles(sp, load)

            @block.scalar
            def _(act):
                act.dma_start(ln2[:, 0, :], row_bcast(io["ln_g"][0, 1], P)).then_inc(ln_in, 16)
                act.dma_start(ln2[:, 1, :], row_bcast(io["ln_b"][0, 1], P)).then_inc(ln_in, 16)
                act.sem_inc(o_free, 2)
                for n in range(4):
                    p_, hf = n < 2, n % 2
                    act.wait_ge(bc_ps, n + 1)
                    act.activation((gate_p if p_ else gate_s)[:, hf * 512:(hf + 1) * 512],
                                   pg[hf][0:(P if p_ else NSAMP), :], ACT.Copy).then_inc(bc_ev, 1)

                def store(t, s, i):
                    n = rows_of(t)
                    wait_apart(act, o_rdy, t + 3, tick)
                    act.dma_start(os_ if n < P else op[bass.ds(t * P, n), :], o[0:n, s, :]).then_inc(o_out[s], 16)
                    wait_apart(act, o_out[s], 16 * i + 16, tick)
                    act.sem_inc(o_free, 1)
                tiles(act, store)

            @block.gpsimd
            def _(pool):
                pool.wait_ge(ln_in, 32)

                def work(t, s, i):
                    n = rows_of(t)
                    wait_apart(pool, y_in[s], 16 * i + 16, tick)
                    wait_apart(pool, z_rdy, t + 1, tick)
                    pool.tensor_tensor(ysum[0:n, s, :], y2[0:n, s, 0, :], y2[0:n, s, 1, :], ALU.add).then_inc(ysum_rdy, 1)
                    wait_apart(pool, var_rdy, t + 1, tick)
                    pool.tensor_tensor(rstd[0:n, :], ve[0:n, :], keep["neg_half"][0:n, 0:1], ALU.pow).then_inc(rs_rdy, 1)
                    wait_apart(pool, o1_rdy, t + 1, tick)
                    wait_apart(pool, o_free, t + 1, tick)
                    pool.tensor_tensor(o[0:n, s, :], o1[0:n, s, :], ln2[0:n, 1, :], ALU.add).then_inc(o_rdy, 1)
                tiles(pool, work)

            @block.tensor
            def _(pe):
                pe.wait_ge(mod_in, 16)
                for n in range(4):
                    p_, hf = n < 2, n % 2
                    if n >= 2:
                        pe.wait_ge(bc_ev, n - 1)
                    sel = keep["sel_p"] if p_ else keep["sel_s"]
                    pe.matmul(pg[hf][0:(P if p_ else NSAMP), :], sel[:, :], mod_rows[:, hf * 512:(hf + 1) * 512],
                              start=True, stop=True).then_inc(bc_ps, 1)

            @block.vector
            def _(dve):
                dve.sem_inc(z_rdy, 2)
                dve.wait_ge(bc_ev, 4)
                dve.wait_ge(ln_in, 32)

                def work(t, s, i):
                    n = rows_of(t)
                    gate = gate_s if n < P else gate_p
                    dve.wait_ge(ysum_rdy, t + 1)
                    dve.tensor_tensor(ga[0:n, s, :], ysum[0:n, s, :], gate[0:n, :], ALU.mult)
                    dve.drain()
                    dve.wait_ge(x_in[s], 16 * i + 16)
                    dve.scalar_tensor_tensor(z[0:n, s, :], x1[0:n, s, :], ALPHA, ga[0:n, s, :], ALU.mult, ALU.add)
                    dve.drain().then_inc(z_rdy, 1)
                    for a in range(2):
                        dve.bn_stats(stats[0:n, a, :], z[0:n, s, a * 512:(a + 1) * 512])
                    dve.drain()
                    dve.bn_aggr(mv[0:n, :], stats[0:n, :, :])
                    dve.drain()
                    dve.tensor_scalar(ve[0:n, :], mv[0:n, 1:2], LN_EPS, None, ALU.add).then_inc(var_rdy, 1)
                    dve.wait_ge(rs_rdy, t + 1)
                    dve.tensor_scalar(zn[0:n, s, :], z[0:n, s, :], mv[0:n, 0:1], rstd[0:n, :], ALU.subtract, ALU.mult)
                    dve.drain()
                    dve.wait_ge(o_rdy, t + 1)
                    dve.tensor_tensor(o1[0:n, s, :], zn[0:n, s, :], ln2[0:n, 0, :], ALU.mult).then_inc(o1_rdy, 1)
                dve.sem_inc(o_rdy, 2)
                tiles(dve, work)


def build(nc, io, outs):
    scr = {
        "mod": nc.dram_tensor("mod_scratch", [1 + DEC_B, 6 * D], F32).ap(),
        "y": nc.dram_tensor("y_scratch", [2 * HEADS, P, NTOK], F32).ap(),
        "x1": nc.dram_tensor("x1_scratch", [NTOK, D], F32).ap(),
        "u2": nc.dram_tensor("u2_scratch", [NTOK + 1, D], F32).ap(),
        "list": nc.dram_tensor("list_scratch", [(NE + 1) * CAP, 4], I32).ap(),
        "tab": nc.dram_tensor("tab_scratch", [P, 2], I32).ap(),
        "y2": nc.dram_tensor("y2_scratch", [2 * NTOK + P, D], F32).ap(),
    }
    with ExitStack() as ctx:
        sb = lambda name, shape, dt=F32: ctx.enter_context(nc.sbuf_tensor(name, shape, dt))
        keep = {
            "ident": sb("ident", [P, P]),
            "ones": sb("ones", [P, P]),
            "tri": sb("tri", [P, P]),
            "sel_p": sb("sel_p", [1 + DEC_B, P]),
            "sel_s": sb("sel_s", [1 + DEC_B, NSAMP]),
            "neg_half": sb("neg_half", [P, 8]),
        }
        with ExitStack() as mctx:
            mb = lambda name, shape, dt=F32: mctx.enter_context(nc.sbuf_tensor(name, shape, dt))
            keep.update({
                "ident_i": mb("ident_i", [P, P], I32),
                "bmask": mb("bmask", [SS_TOK, SB]),
                "lmask": mb("lmask", [P, LEVELS, NCH * CH // 2], I32),
                "modT": mb("modT", [P, 2 * KT, 1 + DEC_B]),
                "head_par": mb("head_par", [P, HEADS, 6]),
                "A": mb("A", [P, NCH, CH]),
                "A_s": mb("A_s", [SS_TOK, SS_TOK]),
                "state": mb("state", [P, HEADS, P]),
                "conv_carry": mb("conv_carry", [P, HEADS, 2]),
                "conv_state_s": mb("conv_state_s", [P, HEADS, 2 * DEC_B]),
            })
            modulation_phase(nc, io, keep, scr)
            mixer_phase(nc, io, keep, scr, outs)
        keep.update({
            "blk_tab": sb("blk_tab", [1, 2 * P], I32),
            "exp_tab": sb("exp_tab", [1, NE + 1], I32),
            "logits": sb("logits", [P, TILES, NG + NE]),
        })
        output_phase(nc, io, keep, scr)
        with ExitStack() as ectx:
            for name, slots, width, dt in (("gu_raw", RAW, 2 * KT * DE, F32), ("gu_hi", 2, 2 * KT * DE, F32R),
                                           ("gu_lo", 2, 2 * KT * DE, F32R), ("dn_w", RAW, DE // P * D, F32)):
                keep[name] = ectx.enter_context(nc.sbuf_tensor("w_" + name, [P, slots, width], dt))
            for name in ("wg_in", "wu_in", "wd_in"):
                keep[name] = ectx.enter_context(nc.semaphore(name))
            routing_phase(nc, io, keep, scr)
            expert_phase(nc, io, keep, scr)
        combine_phase(nc, io, keep, scr, outs)


def kernel(**inputs):
    import concourse.bacc as bacc
    from concourse.bass_utils import run_bass_kernel_spmd

    nc = bacc.Bacc("TRN2", target_bir_lowering=False, num_devices=1)
    arrays, args = {}, {}
    for name, value in inputs.items():
        a = np.ascontiguousarray(value)
        arrays["in_" + name] = a
        args[name] = nc.dram_tensor("in_" + name, a.shape, mybir.dt.from_np(a.dtype), kind="ExternalInput").ap()
    outs = [nc.dram_tensor("out_%d" % i, shape, mybir.dt.from_np(np.dtype(dtype)), kind="ExternalOutput").ap()
            for i, (shape, dtype) in enumerate(OUTS)]
    build(nc, args, outs)
    r = run_bass_kernel_spmd(nc, [arrays], core_ids=[0])
    return tuple(r.results[0]["out_%d" % i] for i in range(len(OUTS)))
```

```python
from contextlib import ExitStack

import numpy as np

import concourse.bass as bass
from concourse import mybir

P = 128
D = 1024
KT = D // P
SEQ = 2048
DEC_B = 8
DEC_L = 8
NSAMP = DEC_B * DEC_L
NTOK = SEQ + NSAMP
CONV_DIM = 512
HEADS = 4
CONV_W = 3
SEGS = 4
SP_TOK = SEQ // SEGS
SS_TOK = NSAMP // SEGS
SB = DEC_B // SEGS
TS = SP_TOK + SS_TOK
HALF = TS // 2
CH = 128
NCH = SP_TOK // CH
LEVELS = 7
SLEVELS = 3
XT = SP_TOK // P
NE = 32
NG = 4
EPG = NE // NG
DE = 256
TILES = SEQ // P + 1
CAP = (TILES) * P
RAW = 3
LN_EPS = 1e-5
RMS_EPS = 1e-6
ALPHA = 2.0 ** 0.25
QSCALE = float(P) ** -0.5
BIG = 3.0e38
F32 = mybir.dt.float32
F32R = mybir.dt.float32r
I32 = mybir.dt.int32
ALU = mybir.AluOpType
ACT = mybir.ActivationFunctionType
AX = mybir.AxisListType

COL_F, COL_Q, COL_I, COL_G, COL_CB, COL_CC, COL_CV = (
    CONV_DIM * 4, CONV_DIM * 3, CONV_DIM * 5, CONV_DIM * 6, 0, CONV_DIM, 2 * CONV_DIM)
UNIT_COLS = (COL_F, COL_Q, COL_I, COL_G, COL_CB, COL_CC, COL_CV)
NT = len(UNIT_COLS)
WS = 4

OUTS = [((1, SEQ, D), "float32"), ((DEC_B, DEC_L, D), "float32"), ((1, 1, 2, CONV_DIM), "float32"),
        ((1, 1, HEADS, P, P), "float32"), ((1, DEC_B, 2, CONV_DIM), "float32"),
        ((1, DEC_B, HEADS, P, P), "float32")]


def wait_apart(eng, sem, value, tick):
    eng.wait_ge(sem, value)
    eng.sem_inc(tick, 1)


def row_bcast(row, parts):
    return row.partition_broadcast(parts)


def load_segment(eng, io, keep, seg):
    eng.dma_start(keep["x_rows"][:, :, :], io["x_prompt"][0, bass.ds(seg * SP_TOK, SP_TOK), :]
                  .rearrange("(t p) d -> p t d", p=P)).then_inc(keep["x_in"], 16)
    eng.dma_start(keep["xs_rows"][:, :], io["x_sample"].rearrange("b l d -> (b l) d")[bass.ds(seg * SS_TOK, SS_TOK), :]).then_inc(keep["x_in"], 16)


def modulation_phase(nc, io, keep, scr):
    NROW = 1 + DEC_B
    NCHUNK = 5 * D // 512
    ident, modT, sel_p, sel_s = keep["ident"], keep["modT"], keep["sel_p"], keep["sel_s"]
    head_par = keep["head_par"]
    with ExitStack() as ctx:
        sb = lambda name, shape, dt=F32: ctx.enter_context(nc.sbuf_tensor(name, shape, dt))
        ps = lambda name, shape: ctx.enter_context(nc.psum_tensor(name, shape, F32))
        sem = lambda name: ctx.enter_context(nc.semaphore(name))
        c_rows = sb("c_rows", [NROW, D])
        c_sig = sb("c_sig", [NROW, D])
        c_silu = sb("c_silu", [NROW, D])
        cT = keep["cT"]
        b_rows = sb("b_rows", [NROW, 5 * D])
        mod = sb("mod", [NROW, 5 * D])
        w_ring = sb("w_ring", [P, 2, KT, 512])
        conv_rows = sb("conv_rows", [2 * DEC_B, CONV_DIM])
        lbt = sb("lbt", [P, 8, HEADS])
        blk_idx = sb("blk_idx", [P, NCH * CH // 2], I32)
        part_idx = sb("part_idx", [P, 1], I32)
        part_blk = sb("part_blk", [P, LEVELS], I32)
        part_blkf = sb("part_blkf", [P, LEVELS])
        blk_f = sb("blk_f", [P, NCH * CH // 2])
        ps_t = ps("ps_mt", [P, 512])
        ps_m = [ps("ps_m0", [P, 512]), ps("ps_m1", [P, 512])]
        ps_x = ps("ps_mx", [P, 512])
        c_in, b_in, small_in, conv_in = sem("c_in"), sem("b_in"), sem("small_in"), sem("conv_in")
        w_in = [sem("w_mod_in0"), sem("w_mod_in1")]
        c_sigd, c_silud, ident_rdy, cT_ps, cT_rdy = (sem("c_sigd"), sem("c_silud"), sem("ident_rdy"),
                                                     sem("cT_ps"), sem("cT_rdy"))
        prod, evac = sem("mod_prod"), sem("mod_evac")
        modT_ps, lb_d, lb_s, idx_rdy = sem("modT_ps"), sem("lb_d"), sem("lb_s"), sem("idx_rdy")
        mod_out = sem("mod_out")
        wv = io["w_mod"][0].rearrange("(k p) n -> p k n", p=P)

        with nc.Block() as block:
            @block.sync
            def _(sp):
                sp.dma_start(c_rows[0:1, :], io["c_prompt"]).then_inc(c_in, 16)
                sp.dma_start(c_rows[1:NROW, :], io["c_sample"]).then_inc(c_in, 16)
                for s in range(2):
                    sp.dma_start(w_ring[:, s], wv[:, :, bass.ds(s * 512, 512)]).then_inc(w_in[s], 16)
                with sp.Fori(1, NCHUNK // 2) as i:
                    for s in range(2):
                        sp.wait_ge(prod, 2 * i + s - 1)
                        sp.dma_start(w_ring[:, s], wv[:, :, bass.ds(i * 1024 + s * 512, 512)]).then_inc(w_in[s], 16)
                for j in range(2):
                    sp.dma_start(keep["w_raw"][:, j], io["w_in"][0].rearrange("(k p) n -> p k n", p=P)[:, :, UNIT_COLS[j]:UNIT_COLS[j] + P]).then_inc(keep["raw_in"][j], 16)
                sp.wait_ge(evac, NCHUNK + 2)
                sp.dma_start(scr["mod"], mod[:, :]).then_inc(mod_out, 16)
                sp.wait_ge(mod_out, 16)

            @block.scalar
            def _(act):
                act.dma_start(b_rows[:, :], row_bcast(io["b_mod"][0, 0:5 * D], NROW)).then_inc(b_in, 16)
                act.dma_start(conv_rows[:, :], io["state_conv"][0].rearrange("b r c -> (b r) c")).then_inc(conv_in, 16)
                with nc.allow_non_contiguous_dma(reason="a few short parameter vectors"):
                    act.dma_start(lbt[:, 0, :], io["hgrn_lb_logits"][0].rearrange("(h p) -> p h", p=P)).then_inc(small_in, 16)
                    for j in range(CONV_W):
                        act.dma_start(head_par[:, :, 2 + j], io["conv_w"][0, j].rearrange("(h p) -> p h", p=P)).then_inc(small_in, 16)
                    for h in range(HEADS):
                        act.dma_start(head_par[:, h, 5:6], io["gnorm_w"][0].rearrange("(p a) -> p a", a=1)).then_inc(small_in, 16)
                act.wait_ge(c_in, 32)
                act.activation(c_sig[:, :], c_rows[:, :], ACT.Sigmoid).then_inc(c_sigd, 1)
                act.wait_ge(lb_d, 1)
                act.activation(lbt[:, 2, :], lbt[:, 1, :], ACT.Sigmoid)
                act.activation(lbt[:, 3, :], lbt[:, 1, :], ACT.Sigmoid, scale=-1.0).then_inc(lb_s, 1)

            @block.gpsimd
            def _(pool):
                pool.memset(ident[:, :], 0.0)
                pool.memset(sel_p[:, :], 0.0)
                pool.memset(sel_s[:, :], 1.0)
                pool.drain()
                pool.affine_select(out=ident[:, :], in_=ident[:, :], compare_op=ALU.not_equal, fill=1.0,
                                   base=0, pattern=[[-1, P]], channel_multiplier=1)
                pool.affine_select(out=sel_p[:, :], in_=sel_p[:, :], compare_op=ALU.not_equal, fill=1.0,
                                   base=0, pattern=[[0, P]], channel_multiplier=1)
                pool.affine_select(out=sel_s[:, :], in_=sel_s[:, :], compare_op=ALU.is_ge, fill=0.0,
                                   base=DEC_L, pattern=[[1, NSAMP]], channel_multiplier=-DEC_L)
                pool.drain()
                pool.affine_select(out=sel_s[:, :], in_=sel_s[:, :], compare_op=ALU.is_ge, fill=0.0,
                                   base=-1, pattern=[[-1, NSAMP]], channel_multiplier=DEC_L)
                pool.drain()
                pool.tensor_copy(keep["ident_i"][:, :], ident[:, :]).then_inc(ident_rdy, 1)
                pool.memset(keep["bmask"][:, :], 1.0)
                pool.memset(keep["neg_half"][:, :], -0.5)
                pool.memset(keep["ones"][:, :], 1.0)
                pool.memset(keep["tri"][:, :], 1.0)
                pool.drain()
                pool.affine_select(out=keep["bmask"][:, :], in_=keep["bmask"][:, :], compare_op=ALU.is_ge, fill=0.0,
                                   base=0, pattern=[[-DEC_L, SB]], channel_multiplier=1)
                pool.affine_select(out=keep["tri"][:, :], in_=keep["tri"][:, :], compare_op=ALU.is_ge, fill=0.0,
                                   base=-1, pattern=[[1, P]], channel_multiplier=-1)
                pool.iota(part_idx[:, :], pattern=[[0, 1]], base=0, channel_multiplier=1)
                pool.drain()
                pool.affine_select(out=keep["bmask"][:, :], in_=keep["bmask"][:, :], compare_op=ALU.is_ge, fill=0.0,
                                   base=DEC_L - 1, pattern=[[DEC_L, SB]], channel_multiplier=-1).then_inc(idx_rdy, 1)
                for l in range(LEVELS):
                    h, nb = 1 << l, CH >> (l + 1)
                    if l:
                        pool.wait_ge(modT_ps, l + 1)
                    pool.iota(blk_idx[:, :].rearrange("p (c b h) -> p c b h", c=NCH, b=nb),
                              pattern=[[0, NCH], [2, nb], [0, h]], base=0, channel_multiplier=0).then_inc(idx_rdy, 1)
                pool.wait_ge(prod, NCHUNK // 2)
                load_segment(pool, io, keep, 0)

            @block.tensor
            def _(pe):
                pe.wait_ge(ident_rdy, 1)
                pe.wait_ge(c_silud, 1)
                for k in range(KT):
                    last = pe.transpose(ps_t[:, k * NROW:(k + 1) * NROW], c_silu[:, k * P:(k + 1) * P], ident[0:NROW, 0:NROW])
                last.then_inc(cT_ps, 1)
                pe.wait_ge(conv_in, 16)
                for h in range(HEADS):
                    last = pe.transpose(ps_x[:, h * 16:(h + 1) * 16], conv_rows[:, h * P:(h + 1) * P], ident[0:16, 0:16])
                last.then_inc(cT_ps, 1)
                pe.wait_ge(cT_rdy, 1)
                with pe.Fori(0, NCHUNK // 2) as i:
                    for s in range(2):
                        pe.wait_ge(w_in[s], 16 * i + 16)
                        pe.wait_ge(evac, 2 * i + s + 1)
                        for k in range(KT):
                            last = pe.matmul(ps_m[s][0:NROW, :], cT[:, k, :], w_ring[:, s, k, :],
                                             start=(k == 0), stop=(k == KT - 1))
                        last.then_inc(prod, 1)
                pe.wait_ge(evac, NCHUNK + 2)
                pe.wait_ge(cT_rdy, 2)
                for k in range(2 * KT):
                    last = pe.transpose(ps_t[:, k * NROW:(k + 1) * NROW], mod[:, k * P:(k + 1) * P], ident[0:NROW, 0:NROW])
                last.then_inc(cT_ps, 1)

            @block.vector
            def _(dve):
                dve.sem_inc(evac, 2)
                dve.wait_ge(c_sigd, 1)
                dve.tensor_tensor(c_silu[:, :], c_rows[:, :], c_sig[:, :], ALU.mult).then_inc(c_silud, 1)
                dve.wait_ge(cT_ps, 1)
                dve.tensor_copy(cT[:, :, :], ps_t[:, 0:KT * NROW].rearrange("p (k r) -> p k r", k=KT)).then_inc(cT_rdy, 1)
                dve.wait_ge(cT_ps, 2)
                dve.tensor_copy(keep["conv_state_s"][:, :, :], ps_x[:, 0:HEADS * 16].rearrange("p (h r) -> p h r", h=HEADS)).then_inc(cT_rdy, 1)
                dve.wait_ge(small_in, 16 * (1 + CONV_W + HEADS))
                dve.tensor_tensor(lbt[:, 1, :], lbt[:, 0, :], lbt[:, 0, :], ALU.subtract).then_inc(lb_d, 1)
                dve.wait_ge(lb_s, 1)
                dve.reciprocal(lbt[:, 4, :], lbt[:, 3, :])
                dve.drain()
                dve.tensor_tensor(lbt[:, 5, :], lbt[:, 2, :], lbt[:, 4, :], ALU.mult)
                dve.drain()
                dve.reciprocal(lbt[:, 6, :], lbt[:, 5, :])
                dve.drain()
                dve.tensor_tensor(lbt[:, 7, :], lbt[:, 5, :], lbt[:, 6, :], ALU.mult)
                dve.drain()
                dve.tensor_tensor(head_par[:, :, 0], lbt[:, 7, :], lbt[:, 7, :], ALU.subtract)
                dve.drain()
                dve.tensor_scalar(head_par[:, :, 1], head_par[:, :, 0], -1.0, 1.0, ALU.mult, ALU.add)
                dve.wait_ge(idx_rdy, 1)
                for l in range(LEVELS):
                    dve.tensor_scalar(part_blk[:, l:l + 1], part_idx[:, :], l, None, ALU.logical_shift_right)
                dve.drain()
                dve.tensor_copy(part_blkf[:, :], part_blk[:, :]).then_inc(modT_ps, 1)
                for l in range(LEVELS):
                    dve.wait_ge(idx_rdy, l + 2)
                    dve.tensor_copy(blk_f[:, :], blk_idx[:, :])
                    dve.drain()
                    dve.tensor_scalar(keep["lmask"][:, l, :], blk_f[:, :], part_blkf[:, l:l + 1], None, ALU.is_equal)
                    dve.drain().then_inc(modT_ps, 1)
                dve.memset(keep["A"][:, :, :], 0.0)
                dve.memset(keep["A_s"][:, :], 0.0)
                dve.memset(keep["state"][:, :, :], 0.0)
                dve.memset(keep["conv_carry"][:, :, :], 0.0)
                dve.wait_ge(b_in, 16)
                with dve.Fori(0, NCHUNK // 2) as i:
                    for s in range(2):
                        dve.wait_ge(prod, 2 * i + s + 1)
                        dve.tensor_tensor(mod[:, bass.ds(i * 1024 + s * 512, 512)], ps_m[s][0:NROW, :],
                                          b_rows[:, bass.ds(i * 1024 + s * 512, 512)], ALU.add).then_inc(evac, 1)
                dve.wait_ge(cT_ps, 3)
                dve.tensor_copy(modT[:, 0:KT, :], ps_t[:, 0:KT * NROW].rearrange("p (k r) -> p k r", k=KT))
                dve.tensor_scalar(modT[:, KT:2 * KT, :], ps_t[:, KT * NROW:2 * KT * NROW].rearrange("p (k r) -> p k r", k=KT),
                                  1.0, None, ALU.add)


def mixer_phase(nc, io, keep, scr, outs):
    ident, modT, head_par = keep["ident"], keep["modT"], keep["head_par"]
    lmask, ident_i, A, A_s = keep["lmask"], keep["ident_i"], keep["A"], keep["A_s"]
    x_rows, xs_rows, w_raw, x_in, raw_in = (keep[n] for n in ("x_rows", "xs_rows", "w_raw", "x_in", "raw_in"))
    state, conv_carry, conv_state_s, bmask = keep["state"], keep["conv_carry"], keep["conv_state_s"], keep["bmask"]
    with ExitStack() as ctx:
        sb = lambda name, shape, dt=F32: ctx.enter_context(nc.sbuf_tensor(name, shape, dt))
        ps = lambda name, shape: ctx.enter_context(nc.psum_tensor(name, shape, F32))
        sem = lambda name: ctx.enter_context(nc.semaphore(name))
        seg_mod = sb("seg_mod", [P, 2 * KT, SB])
        u_f = sb("u_f", [P, 2, TS])
        u_hi = sb("u_hi", [P, KT, TS], F32R)
        u_lo = sb("u_lo", [P, KT, TS], F32R)
        w_hi = sb("w_hi", [P, WS, KT, P], F32R)
        w_lo = sb("w_lo", [P, WS, KT, P], F32R)
        par = sb("par", [P, 6])
        f_sig = sb("f_sig", [P, TS])
        k_sig = sb("k_sig", [P, TS])
        q_sig = sb("q_sig", [P, TS])
        g_sig = sb("g_sig", [P, TS])
        vT = sb("vT", [P, TS])
        cbs = sb("cbs", [P, TS])
        ccs = sb("ccs", [P, TS])
        q0 = sb("q0", [P, TS])
        ql = sb("ql", [P, LEVELS + 1, TS])
        kl = sb("kl", [P, LEVELS + 1, TS])
        wl0 = sb("wl0", [P, TS])
        wl = sb("wl", [P, TS])
        gg = sb("gg", [P, TS])
        v_tok = sb("v_tok", [P, NCH, P])
        k_tok = sb("k_tok", [P, NCH, P])
        vs_tok = sb("vs_tok", [SS_TOK, P])
        ks_tok = sb("ks_tok", [SS_TOK, P])
        vs_msk = sb("vs_msk", [SS_TOK, SB, P])
        qs_msk = sb("qs_msk", [P, SB * (SS_TOK + DEC_L)])
        s_chain = sb("s_chain", [P, NCH + 1, P])
        s0 = sb("s0", [P, SB, P])
        s1 = sb("s1", [P, SB, P])
        o_tok = sb("o_tok", [P, NCH + 1, P])
        o_sq = sb("o_sq", [P, NCH + 1, P])
        o_n = sb("o_n", [P, NCH + 1, P])
        o_ss = sb("o_ss", [P, NCH + 1])
        o_ms = sb("o_ms", [P, NCH + 1])
        o_r = sb("o_r", [P, NCH + 1])
        cvv = sb("cvv", [P, 2 + SP_TOK + SB * (2 + DEC_L)])
        cy = sb("cy", [P, 2, TS])
        y_conv = sb("y_conv", [P, TS])
        y_rec = sb("y_rec", [P, TS])
        pr = [ps("pr0", [P, 1024]), ps("pr1", [P, 1024])]
        pa = [ps("pa0", [P, 512]), ps("pa1", [P, 512])]
        pt = ps("pt", [P, 512])
        po = ps("po", [P, 512])

        tick = sem("tick")
        s0_in = sem("s0_in")
        hi_done, lo_done, proj_done = sem("hi_done"), sem("lo_done"), sem("proj_done")
        pr_free = [sem("pr_free0"), sem("pr_free1")]
        pa_free = [sem("pa_free0"), sem("pa_free1")]
        pt_free, po_free = sem("pt_free"), sem("po_free")
        xT_ps, u_act, u_rdy = sem("xT_ps"), sem("u_act"), sem("u_rdy")
        ev = sem("act_evac")
        gates = sem("gates")
        q_lev, k_lev = sem("q_lev"), sem("k_lev")
        hg = sem("hg_ps")
        tok_rdy = sem("tok_rdy")
        a_rdy = sem("a_rdy")
        s_rdy = sem("s_rdy")
        smsk = sem("smsk")
        o_evac = sem("o_evac")
        o_mean, o_rs, o_nrm = sem("o_mean"), sem("o_rs"), sem("o_nrm")
        yc_rdy, yr_rdy, s1_rdy = sem("yc_rdy"), sem("yr_rdy"), sem("s1_rdy")
        stored, os_evac = sem("stored"), sem("os_evac")
        yc_out, yr_out, s1_out = sem("yc_out"), sem("yr_out"), sem("s1_out")
        fin, fin_ps, fin_sb, fin_out = sem("fin"), sem("fin_ps"), sem("fin_sb"), sem("fin_out")
        wv = io["w_in"][0].rearrange("(k p) n -> p k n", p=P)
        HG = 13
        (VT_, DIAG, L01, KT_, L23, L45, L6, SA, DS, DSS, O_, OT, OST) = range(1, HG + 1)
        lag = [j - 3 if j >= WS else (j - 2 if j < NT - WS else -3) for j in range(NT)]
        RC = 4

        def raw_count(j, u):
            s = j % WS
            uses = len([t for t in range(NT) if t % WS == s])
            return 16 * uses * u + 16 * (j // WS + 1)

        wl_n = [TS >> l if l <= SLEVELS else SP_TOK >> l for l in range(LEVELS + 1)]
        wl_at = [0, 0]
        for l in range(2, LEVELS + 1):
            wl_at.append(wl_at[-1] + wl_n[l - 1])
        assert wl_at[-1] + wl_n[-1] <= TS

        def decay(l, n):
            return wl0[:, 0:n] if l == 0 else wl[:, wl_at[l]:wl_at[l] + n]

        def blocks(ap, h):
            return ap.rearrange("p (b two h) -> p b two h", two=2, h=h)

        with nc.Block() as block:
            @block.sync
            def _(sp):
                def load_tile(u, h, j):
                    wait_apart(sp, lo_done, NT * u + (lag[j] + RC), tick)
                    sp.dma_start(w_raw[:, j % WS], wv[:, :, bass.ds(h * P + UNIT_COLS[j], P)]).then_inc(raw_in[j % WS], 16)

                with sp.Fori(0, SEGS) as seg:
                    with sp.Fori(0, HEADS) as h:
                        u = sp.snap(seg * HEADS + h)
                        h_next = sp.snap((h + 1) % HEADS)
                        for j in range(2, NT):
                            load_tile(u, h, j)
                        wait_apart(sp, s1_rdy, u + 1, tick)
                        sp.dma_start(s0[:, :, :], io["state_hgrn"][0, bass.ds(seg * SB, SB), bass.ds(h, 1), :, :]
                                     .rearrange("b a k v -> k (b a) v")).then_inc(s0_in, 16)
                        load_tile(u + 1, h_next, 0)
                        load_tile(u + 1, h_next, 1)
                sp.wait_ge(fin_sb, 1)
                sp.dma_start(outs[2][0, 0], cy[0:2, 0, 0:CONV_DIM]).then_inc(fin_out, 16)
                sp.dma_start(outs[4][0].rearrange("b r c -> (b r) c"), cy[0:16, 1, 0:CONV_DIM]).then_inc(fin_out, 16)
                sp.dma_start(outs[3][0, 0].rearrange("h k v -> k h v"), state[:, :, :]).then_inc(fin_out, 16)
                sp.wait_ge(fin_out, 48)

            @block.scalar
            def _(act):
                def split_hi(u, j, j_count):
                    act.wait_ge(raw_in[j % WS], j_count)
                    act.wait_ge(proj_done, NT * u + (lag[j] + RC))
                    act.activation(w_hi[:, j % WS], w_raw[:, j % WS], ACT.Copy).then_inc(hi_done, 1)

                def split_next(u, j):
                    if j + 2 < NT:
                        split_hi(u, j + 2, raw_count(j + 2, u))
                    else:
                        split_hi(u + 1, j + 2 - NT, raw_count(j + 2 - NT, u + 1))

                def proj(j):
                    return pr[j % 2][:, :].rearrange("p (a n) -> p a n", a=2)[:, :, 0:HALF]

                def two(ap):
                    return ap.rearrange("p (a n) -> p a n", a=2)

                act.sem_inc(u_rdy, 2)
                split_hi(0, 0, 16)
                split_hi(0, 1, 16)
                with act.Fori(0, SEGS) as seg:
                    act.activation(seg_mod[:, :, :], modT[:, :, bass.ds(seg * SB + 1, SB)], ACT.Copy)
                    act.drain()
                    for k in range(KT):
                        act.wait_ge(xT_ps, KT * seg + (k + 1))
                        act.wait_ge(u_rdy, KT * seg + (k + 1))
                        act.activation(u_f[:, k % 2, 0:SP_TOK], pr[k % 2][:, 0:SP_TOK], ACT.Identity,
                                       bias=modT[:, k, 0:1], scale=modT[:, KT + k, 0:1])
                        for b in range(SB):
                            last = act.activation(u_f[:, k % 2, SP_TOK + b * DEC_L:SP_TOK + (b + 1) * DEC_L],
                                                  pr[k % 2][:, SP_TOK + b * DEC_L:SP_TOK + (b + 1) * DEC_L], ACT.Identity,
                                                  bias=seg_mod[:, k, b:b + 1], scale=seg_mod[:, KT + k, b:b + 1])
                        act.drain().then_inc(u_act, 1)
                    with act.Fori(0, HEADS) as h:
                        u = act.snap(seg * HEADS + h)
                        split_next(u, 0)
                        act.wait_ge(proj_done, NT * u + (0 + 1 + RC))
                        act.wait_ge(gates, 8 * u + 1)
                        act.activation(two(f_sig[:, :]), proj(0), ACT.Sigmoid)
                        act.activation(two(k_sig[:, :]), proj(0), ACT.Sigmoid, scale=-1.0)
                        act.drain().then_inc(ev, 1)
                        split_next(u, 1)
                        act.wait_ge(proj_done, NT * u + (1 + 1 + RC))
                        act.activation(two(q_sig[:, :]), proj(1), ACT.Sigmoid).then_inc(ev, 1)
                        split_next(u, 2)
                        act.wait_ge(proj_done, NT * u + (2 + 1 + RC))
                        act.activation(two(vT[:, :]), proj(2), ACT.Copy).then_inc(ev, 1)
                        split_next(u, 3)
                        act.wait_ge(hg, HG * u + VT_)
                        act.activation(v_tok[:, :, :], pt[:, :].rearrange("p (c v) -> p c v", c=NCH), ACT.Copy).then_inc(tok_rdy, 1)
                        act.wait_ge(proj_done, NT * u + (3 + 1 + RC))
                        act.activation(two(g_sig[:, :]), proj(3), ACT.Sigmoid).then_inc(ev, 1)
                        split_next(u, 4)
                        act.wait_ge(hg, HG * u + KT_)
                        act.activation(k_tok[:, :, :], pt[:, :].rearrange("p (c v) -> p c v", c=NCH), ACT.Copy).then_inc(tok_rdy, 1)
                        act.wait_ge(proj_done, NT * u + (4 + 1 + RC))
                        act.wait_ge(yc_rdy, u + 1)
                        act.activation(two(cbs[:, :]), proj(4), ACT.Copy).then_inc(ev, 1)
                        split_next(u, 5)
                        act.wait_ge(hg, HG * u + SA)
                        act.activation(vs_tok[:, :], pa[1][0:SS_TOK, 64:64 + P], ACT.Copy)
                        act.activation(ks_tok[:, :], pa[1][0:SS_TOK, 192:192 + P], ACT.Copy)
                        act.drain().then_inc(tok_rdy, 1)
                        act.wait_ge(proj_done, NT * u + (5 + 1 + RC))
                        act.activation(two(ccs[:, :]), proj(5), ACT.Copy).then_inc(ev, 1)
                        split_next(u, 6)
                        act.wait_ge(hg, HG * u + DSS)
                        act.activation(o_tok[0:SS_TOK, NCH, :], pa[0][0:SS_TOK, 2 * P:3 * P], ACT.Copy)
                        act.activation(o_sq[0:SS_TOK, NCH, :], pa[0][0:SS_TOK, 2 * P:3 * P], ACT.Square).then_inc(os_evac, 1)
                        act.wait_ge(hg, HG * u + O_)
                        act.activation(o_tok[:, 0:NCH, :], po[:, :].rearrange("p (c v) -> p c v", c=NCH), ACT.Copy)
                        act.activation(o_sq[:, 0:NCH, :], po[:, :].rearrange("p (c v) -> p c v", c=NCH), ACT.Square)
                        act.drain().then_inc(o_evac, 1)

            @block.gpsimd
            def _(pool):
                pool.sem_inc(yc_rdy, 1)
                pool.sem_inc(s1_rdy, 1)
                pool.sem_inc(yr_rdy, 1)
                pool.sem_inc(stored, 1)
                ss_off = SEQ

                def segment(seg):
                    with pool.Fori(0, HEADS) as h:
                        u = pool.snap(seg * HEADS + h)
                        for l in range(LEVELS):
                            n = TS if l < SLEVELS else SP_TOK
                            hh = 1 << l
                            pool.wait_ge(gates, 8 * u + (l + 2))
                            src, dst = blocks(kl[:, l, 0:n], hh), blocks(kl[:, l + 1, 0:n], hh)
                            wsrc = decay(l, n // hh)
                            wr = wsrc.rearrange("p (b two) -> p b two", two=2)[:, :, 1:2].broadcast_to([P, n // (2 * hh), hh])
                            pool.tensor_tensor(dst[:, :, 0, :], src[:, :, 0, :], wr, ALU.mult)
                            pool.tensor_copy(dst[:, :, 1, :], src[:, :, 1, :])
                            pool.drain().then_inc(k_lev, 1)
                        pool.wait_ge(o_mean, u + 1)
                        pool.tensor_tensor(o_r[:, :], o_ms[:, :], keep["neg_half"][:, 0:NCH + 1], ALU.pow).then_inc(o_rs, 1)
                        pool.wait_ge(yc_rdy, u + 2)
                        pool.dma_start(scr["y"][bass.ds(h, 1), :, bass.ds(seg * SP_TOK, SP_TOK)].rearrange("a p n -> (a p) n"),
                                       y_conv[:, 0:SP_TOK]).then_inc(yc_out, 16)
                        pool.dma_start(scr["y"][bass.ds(h, 1), :, bass.ds(seg * SS_TOK + ss_off, SS_TOK)].rearrange("a p n -> (a p) n"),
                                       y_conv[:, SP_TOK:TS]).then_inc(yc_out, 16)
                        pool.wait_ge(s1_rdy, u + 2)
                        pool.dma_start(outs[5][0, bass.ds(seg * SB, SB), bass.ds(h, 1), :, :].rearrange("b a k v -> k (b a) v"),
                                       s1[:, :, :]).then_inc(s1_out, 16)
                        pool.wait_ge(yr_rdy, u + 2)
                        pool.dma_start(scr["y"][bass.ds(h + HEADS, 1), :, bass.ds(seg * SP_TOK, SP_TOK)].rearrange("a p n -> (a p) n"),
                                       y_rec[:, 0:SP_TOK]).then_inc(yr_out, 16)
                        pool.dma_start(scr["y"][bass.ds(h + HEADS, 1), :, bass.ds(seg * SS_TOK + ss_off, SS_TOK)].rearrange("a p n -> (a p) n"),
                                       y_rec[:, SP_TOK:TS]).then_inc(yr_out, 16)
                        pool.wait_ge(yc_out, 32 * u + 32)
                        pool.wait_ge(s1_out, 16 * u + 16)
                        pool.wait_ge(yr_out, 32 * u + 32)
                        pool.sem_inc(stored, 1)

                with pool.Fori(0, SEGS - 1) as seg:
                    pool.wait_ge(xT_ps, KT * seg + KT)
                    load_segment(pool, io, keep, seg + 1)
                    segment(seg)
                segment(SEGS - 1)

            @block.tensor
            def _(pe):
                for s in range(2):
                    pe.sem_inc(pr_free[s], 1)
                    pe.sem_inc(pa_free[s], 1)
                pe.sem_inc(pt_free, 1)
                pe.sem_inc(po_free, 1)
                pe.sem_inc(proj_done, RC)
                with pe.Fori(0, SEGS) as seg:
                    pe.wait_ge(x_in, 32 * seg + 32)
                    for k in range(KT):
                        uses = 20 if k % 2 == 0 else 16
                        pe.wait_ge(pr_free[k % 2], uses * seg + (k // 2 + 1))
                        for t in range(XT):
                            pe.transpose(pr[k % 2][:, t * P:(t + 1) * P], x_rows[:, t, k * P:(k + 1) * P], ident[:, :])
                        pe.transpose(pr[k % 2][:, SP_TOK:TS], xs_rows[:, k * P:(k + 1) * P],
                                     ident[0:SS_TOK, 0:SS_TOK]).then_inc(xT_ps, 1)
                    wait_apart(pe, u_rdy, KT * seg + (KT + 2), tick)
                    with pe.Fori(0, HEADS) as h:
                        u = pe.snap(seg * HEADS + h)
                        f0 = pe.snap(seg * 20 + h * 4)
                        f1 = pe.snap(seg * 16 + h * 3)

                        def project(j, mid=None):
                            s = j % WS
                            pe.wait_ge(lo_done, NT * u + (j + 1 + RC))
                            if j % 2 == 0:
                                pe.wait_ge(pr_free[0], f0 + (5 + j // 2))
                            else:
                                pe.wait_ge(pr_free[1], f1 + (5 + j // 2))
                            for k in range(KT):
                                for n, (w, x) in enumerate(((w_hi, u_hi), (w_hi, u_lo), (w_lo, u_hi))):
                                    for a in range(2):
                                        last = pe.matmul(pr[j % 2][:, a * 512:a * 512 + HALF], w[:, s, k, :],
                                                         x[:, k, a * HALF:(a + 1) * HALF],
                                                         start=(k == 0 and n == 0), stop=(k == KT - 1 and n == 2))
                                if k == 3 and mid:
                                    mid()
                            last.then_inc(proj_done, 1)

                        def level(l, out, col, tok=P, nch=NCH, base=0):
                            hh = 1 << l
                            for c in range(nch):
                                t0 = base + c * tok
                                right = blocks(ql[:, l, t0:t0 + tok], hh)[:, :, 1, :]
                                last = pe.matmul(out[0:tok, col + c * tok // 2:col + (c + 1) * tok // 2],
                                                 kl[:, l, t0:t0 + tok], right, start=True, stop=True)
                            return last

                        def v_transposes():
                            pe.wait_ge(ev, 6 * u + 3)
                            pe.wait_ge(pt_free, 4 * u + 1)
                            for c in range(NCH):
                                last = pe.transpose(pt[:, c * P:(c + 1) * P], vT[:, c * P:(c + 1) * P], ident[:, :])
                            last.then_inc(hg, 1)

                        def first_scores():
                            pe.wait_ge(q_lev, 9 * u + 1)
                            pe.wait_ge(pa_free[0], 4 * u + 1)
                            for c in range(NCH):
                                last = pe.matmul(pa[0][:, c * P:(c + 1) * P], kl[:, 0, c * P:(c + 1) * P],
                                                 q0[:, c * P:(c + 1) * P], start=True, stop=True)
                            last.then_inc(hg, 1)
                            pe.wait_ge(q_lev, 9 * u + 3)
                            pe.wait_ge(k_lev, 7 * u + 1)
                            pe.wait_ge(pa_free[1], 4 * u + 1)
                            level(0, pa[1], 0)
                            level(1, pa[1], 256).then_inc(hg, 1)
                            pe.wait_ge(k_lev, 7 * u + 7)
                            pe.wait_ge(pt_free, 4 * u + 2)
                            for c in range(NCH):
                                last = pe.transpose(pt[:, c * P:(c + 1) * P], kl[:, LEVELS, c * P:(c + 1) * P], ident[:, :])
                            last.then_inc(hg, 1)

                        def mid_scores():
                            pe.wait_ge(q_lev, 9 * u + 7)
                            pe.wait_ge(pa_free[0], 4 * u + 2)
                            level(2, pa[0], 0)
                            level(3, pa[0], 256).then_inc(hg, 1)
                            pe.wait_ge(pa_free[1], 4 * u + 2)
                            level(4, pa[1], 0)
                            level(5, pa[1], 256).then_inc(hg, 1)

                        def last_scores():
                            pe.wait_ge(q_lev, 9 * u + 9)
                            pe.wait_ge(pa_free[0], 4 * u + 3)
                            level(6, pa[0], 0).then_inc(hg, 1)
                            pe.wait_ge(pa_free[1], 4 * u + 3)
                            pe.matmul(pa[1][0:SS_TOK, 0:SS_TOK], kl[:, 0, SP_TOK:TS], q0[:, SP_TOK:TS], start=True, stop=True)
                            for l in range(SLEVELS):
                                level(l, pa[1], SS_TOK + l * SS_TOK // 2, tok=SS_TOK, nch=1, base=SP_TOK)
                            pe.transpose(pa[1][0:SS_TOK, 64:64 + P], vT[:, SP_TOK:TS], ident[:, :])
                            pe.transpose(pa[1][0:SS_TOK, 192:192 + P], kl[:, SLEVELS, SP_TOK:TS], ident[:, :]).then_inc(hg, 1)
                            pe.wait_ge(tok_rdy, 3 * u + 2)
                            pe.wait_ge(pt_free, 4 * u + 3)
                            for c in range(NCH):
                                last = pe.matmul(pt[:, c * P:(c + 1) * P], k_tok[:, c, :], v_tok[:, c, :], start=True, stop=True)
                            last.then_inc(hg, 1)

                        def outputs():
                            pe.wait_ge(tok_rdy, 3 * u + 3)
                            pe.wait_ge(smsk, 2 * u + 2)
                            pe.wait_ge(a_rdy, 2 * u + 2)
                            pe.wait_ge(s0_in, 16 * u + 16)
                            pe.wait_ge(pa_free[0], 4 * u + 4)
                            pe.matmul(pa[0][:, 0:SB * P], ks_tok[:, :], vs_msk[:, :, :].rearrange("s b v -> s (b v)"), start=True, stop=True)
                            pe.matmul(pa[0][0:SS_TOK, SB * P:(SB + 1) * P], A_s[:, :], vs_tok[:, :], start=True, stop=False)
                            for b in range(SB):
                                last = pe.matmul(pa[0][0:SS_TOK, SB * P:(SB + 1) * P], qs_msk[:, b * SS_TOK:(b + 1) * SS_TOK],
                                                 s0[:, b, :], start=False, stop=(b == SB - 1))
                            last.then_inc(hg, 1)
                            pe.wait_ge(s_rdy, u + 1)
                            pe.wait_ge(po_free, u + 1)
                            for c in range(NCH):
                                pe.matmul(po[:, c * P:(c + 1) * P], A[:, c, :], v_tok[:, c, :], start=True, stop=False)
                                last = pe.matmul(po[:, c * P:(c + 1) * P], ql[:, LEVELS, c * P:(c + 1) * P], s_chain[:, c, :],
                                                 start=False, stop=True)
                            last.then_inc(hg, 1)

                        project(0)
                        project(1)
                        project(2)
                        v_transposes()
                        project(3)
                        first_scores()
                        project(4, mid_scores)
                        last_scores()
                        project(5)
                        outputs()
                        project(6)
                        pe.wait_ge(o_nrm, u + 1)
                        pe.wait_ge(pt_free, 4 * u + 4)
                        for c in range(NCH):
                            last = pe.transpose(pt[:, c * P:(c + 1) * P], o_n[:, c, :], ident[:, :])
                        last.then_inc(hg, 1)
                        wait_apart(pe, pa_free[1], 4 * u + 4, tick)
                        pe.transpose(pa[1][:, 0:SS_TOK], o_n[0:SS_TOK, NCH, :], ident[0:SS_TOK, 0:SS_TOK]).then_inc(hg, 1)
                pe.wait_ge(fin, 1)
                for h in range(HEADS):
                    pe.transpose(pa[0][0:2, h * P:(h + 1) * P], conv_carry[:, h, :], ident[:, :])
                    last = pe.transpose(po[0:16, h * P:(h + 1) * P], conv_state_s[:, h, :], ident[:, :])
                last.then_inc(fin_ps, 1)

            @block.vector
            def _(dve):
                def split_lo(u, j):
                    dve.wait_ge(hi_done, NT * u + (j + 1))
                    dve.tensor_tensor(w_lo[:, j % WS], w_raw[:, j % WS], w_hi[:, j % WS].bitcast(F32), ALU.subtract).then_inc(lo_done, 1)

                def split_next(u, j):
                    if j + 2 < NT:
                        split_lo(u, j + 2)
                    else:
                        split_lo(u + 1, j + 2 - NT)

                def proj(j):
                    return pr[j % 2][:, :].rearrange("p (a n) -> p a n", a=2)[:, :, 0:HALF]

                def two(ap):
                    return ap.rearrange("p (a n) -> p a n", a=2)

                def place(l, src, col):
                    hh = 1 << l
                    out = blocks(A[:, :, :].rearrange("p c t -> p (c t)"), hh)[:, :, 1, :]
                    ins = dve.copy_predicated(out, lmask[:, l, :].rearrange("p (b h) -> p b h", h=hh),
                                              src[:, col:col + NCH * P // 2].rearrange("p (b h) -> p b h", h=hh))
                    return ins

                dve.sem_inc(lo_done, RC)
                dve.sem_inc(gates, 1)
                dve.memset(qs_msk[:, :], 0.0)
                dve.memset(o_tok[:, NCH, :], 0.0)
                dve.memset(o_sq[:, NCH, :], 0.0)
                split_lo(0, 0)
                split_lo(0, 1)
                with dve.Fori(0, SEGS) as seg:
                    for k in range(KT):
                        dve.wait_ge(u_act, KT * seg + (k + 1))
                        dve.wait_ge(proj_done, seg * HEADS * NT + RC)
                        dve.tensor_copy(u_hi[:, k, :], u_f[:, k % 2, :]).then_inc(pr_free[k % 2], 1)
                        dve.drain()
                        dve.tensor_tensor(u_lo[:, k, :], u_f[:, k % 2, :], u_hi[:, k, :].bitcast(F32), ALU.subtract).then_inc(u_rdy, 1)
                    with dve.Fori(0, HEADS) as h:
                        u = dve.snap(seg * HEADS + h)
                        dve.tensor_copy(par[:, :], head_par[:, bass.ds(h, 1), :].rearrange("p a c -> p (a c)"))
                        split_next(u, 0)
                        dve.drain()
                        dve.wait_ge(ev, 6 * u + 1)
                        dve.tensor_scalar(wl0[:, :], f_sig[:, :], par[:, 1:2], par[:, 0:1], ALU.mult, ALU.add).then_inc(pr_free[0], 1)
                        dve.tensor_scalar(kl[:, 0, :], k_sig[:, :], par[:, 1:2], None, ALU.mult)
                        dve.drain().then_inc(gates, 1)
                        for l in range(LEVELS):
                            n = (TS if l < SLEVELS else SP_TOK) >> l
                            src = decay(l, n).rearrange("p (b two) -> p b two", two=2)
                            dve.tensor_tensor(decay(l + 1, n // 2), src[:, :, 0], src[:, :, 1], ALU.mult)
                            dve.drain().then_inc(gates, 1)
                        split_next(u, 1)
                        dve.wait_ge(ev, 6 * u + 2)
                        dve.scalar_tensor_tensor(two(q0[:, :]), proj(1), QSCALE, two(q_sig[:, :]), ALU.mult, ALU.mult)
                        dve.drain().then_inc(q_lev, 1)
                        dve.tensor_tensor(ql[:, 0, :], q0[:, :], wl0[:, :], ALU.mult).then_inc(pr_free[1], 1)
                        dve.drain().then_inc(q_lev, 1)
                        for l in range(LEVELS):
                            n = TS if l < SLEVELS else SP_TOK
                            hh = 1 << l
                            src, dst = blocks(ql[:, l, 0:n], hh), blocks(ql[:, l + 1, 0:n], hh)
                            wsrc = decay(l, n // hh)
                            wleft = wsrc.rearrange("p (b two) -> p b two", two=2)[:, :, 0:1].broadcast_to([P, n // (2 * hh), hh])
                            dve.tensor_tensor(dst[:, :, 1, :], src[:, :, 1, :], wleft, ALU.mult)
                            dve.tensor_copy(dst[:, :, 0, :], src[:, :, 0, :])
                            dve.drain().then_inc(q_lev, 1)
                        dve.tensor_copy(qs_msk[:, :].rearrange("p (b t) -> p b t", b=SB)[:, :, 0:DEC_L],
                                        ql[:, SLEVELS, SP_TOK:TS].rearrange("p (b t) -> p b t", b=SB)).then_inc(smsk, 1)
                        split_next(u, 2)
                        split_next(u, 3)
                        dve.wait_ge(tok_rdy, 3 * u + 1)
                        dve.sem_inc(pt_free, 1)
                        dve.wait_ge(ev, 6 * u + 4)
                        dve.sem_inc(pr_free[0], 1)
                        dve.scalar_tensor_tensor(two(gg[:, :]), proj(3), par[:, 5:6], two(g_sig[:, :]), ALU.mult, ALU.mult).then_inc(pr_free[1], 1)
                        wait_apart(dve, hg, HG * u + DIAG, tick)
                        dve.copy_predicated(A[:, :, :], ident_i[:, :].rearrange("p (a t) -> p a t", a=1).broadcast_to([P, NCH, P]),
                                            pa[0][:, :].rearrange("p (c t) -> p c t", c=NCH)).then_inc(pa_free[0], 1)
                        dve.drain()
                        wait_apart(dve, hg, HG * u + L01, tick)
                        place(0, pa[1], 0)
                        dve.drain()
                        place(1, pa[1], 256).then_inc(pa_free[1], 1)
                        split_next(u, 4)
                        dve.drain()
                        wait_apart(dve, hg, HG * u + L23, tick)
                        place(2, pa[0], 0)
                        dve.drain()
                        place(3, pa[0], 256).then_inc(pa_free[0], 1)
                        dve.drain()
                        wait_apart(dve, hg, HG * u + L45, tick)
                        place(4, pa[1], 0)
                        dve.drain()
                        place(5, pa[1], 256).then_inc(pa_free[1], 1)
                        dve.wait_ge(tok_rdy, 3 * u + 2)
                        dve.sem_inc(pt_free, 1)
                        split_next(u, 5)
                        dve.wait_ge(ev, 6 * u + 5)
                        dve.sem_inc(pr_free[0], 1)
                        dve.drain()
                        wait_apart(dve, hg, HG * u + L6, tick)
                        place(6, pa[0], 0)
                        dve.drain().then_inc(pa_free[0], 1)
                        dve.sem_inc(a_rdy, 1)
                        wait_apart(dve, tok_rdy, 3 * u + 3, tick)
                        dve.copy_predicated(A_s[:, :], ident_i[0:SS_TOK, 0:SS_TOK], pa[1][0:SS_TOK, 0:SS_TOK])
                        for l in range(SLEVELS):
                            hh, n = 1 << l, SS_TOK // 2
                            dve.drain()
                            dve.copy_predicated(blocks(A_s[:, :], hh)[:, :, 1, :],
                                                lmask[0:SS_TOK, l, 0:n].rearrange("p (b h) -> p b h", h=hh),
                                                pa[1][0:SS_TOK, SS_TOK + l * n:SS_TOK + (l + 1) * n].rearrange("p (b h) -> p b h", h=hh))
                        dve.drain().then_inc(a_rdy, 1)
                        dve.sem_inc(pa_free[1], 1)
                        dve.tensor_tensor(vs_msk[:, :, :], vs_tok[:, :].rearrange("s (a v) -> s a v", a=1).broadcast_to([SS_TOK, SB, P]),
                                          bmask[:, :].rearrange("s (b a) -> s b a", a=1).broadcast_to([SS_TOK, SB, P]), ALU.mult).then_inc(smsk, 1)
                        dve.tensor_copy(s_chain[:, 0, :], state[:, bass.ds(h, 1), :].rearrange("p a v -> p (a v)"))
                        dve.drain()
                        dve.wait_ge(hg, HG * u + DS)
                        for c in range(NCH):
                            dve.scalar_tensor_tensor(s_chain[:, c + 1, :], s_chain[:, c, :], decay(LEVELS, NCH)[:, c:c + 1],
                                                     pt[:, c * P:(c + 1) * P], ALU.mult, ALU.add)
                            dve.drain()
                        dve.sem_inc(s_rdy, 1)
                        dve.tensor_copy(state[:, bass.ds(h, 1), :].rearrange("p a v -> p (a v)"), s_chain[:, NCH, :]).then_inc(pt_free, 1)
                        split_next(u, 6)
                        dve.tensor_copy(cvv[:, 0:2], conv_carry[:, bass.ds(h, 1), :].rearrange("p a r -> p (a r)"))
                        samp = cvv[:, 2 + SP_TOK:].rearrange("p (b t) -> p b t", b=SB)
                        cst = conv_state_s[:, bass.ds(h, 1), bass.ds(seg * (2 * SB), 2 * SB)].rearrange("p a (b r) -> p (a b) r", r=2)
                        dve.tensor_copy(samp[:, :, 0:2], cst)
                        dve.wait_ge(os_evac, u + 1)
                        dve.wait_ge(stored, u + 1)
                        for b in range(SB):
                            last = dve.scalar_tensor_tensor(s1[:, b, :], s0[:, b, :], decay(SLEVELS, TS // DEC_L)[:, SP_TOK // DEC_L + b:SP_TOK // DEC_L + b + 1],
                                                            pa[0][:, b * P:(b + 1) * P], ALU.mult, ALU.add)
                        dve.drain().then_inc(s1_rdy, 1)
                        dve.wait_ge(o_evac, u + 1)
                        dve.sem_inc(pa_free[0], 1)
                        dve.sem_inc(po_free, 1)
                        dve.tensor_reduce(o_ss[:, :], o_sq[:, :, :], axis=AX.X, op=ALU.add)
                        dve.drain()
                        dve.tensor_scalar(o_ms[:, :], o_ss[:, :], 1.0 / P, RMS_EPS, ALU.mult, ALU.add).then_inc(o_mean, 1)
                        dve.wait_ge(o_rs, u + 1)
                        dve.tensor_tensor(o_n[:, :, :], o_tok[:, :, :],
                                          o_r[:, :].rearrange("p (c a) -> p c a", a=1).broadcast_to([P, NCH + 1, P]), ALU.mult).then_inc(o_nrm, 1)
                        dve.wait_ge(ev, 6 * u + 6)
                        dve.sem_inc(pr_free[1], 1)
                        dve.wait_ge(proj_done, NT * u + (6 + 1 + RC))
                        dve.tensor_tensor(cvv[:, 2:2 + HALF], pr[0][:, 0:HALF], ccs[:, 0:HALF], ALU.mult)
                        dve.tensor_tensor(cvv[:, 2 + HALF:2 + SP_TOK], pr[0][:, 512:512 + SP_TOK - HALF], ccs[:, HALF:SP_TOK], ALU.mult)
                        dve.tensor_tensor(samp[:, :, 2:2 + DEC_L],
                                          pr[0][:, 512 + SP_TOK - HALF:512 + HALF].rearrange("p (b t) -> p b t", b=SB),
                                          ccs[:, SP_TOK:TS].rearrange("p (b t) -> p b t", b=SB), ALU.mult)
                        dve.drain().then_inc(pr_free[0], 1)
                        cys = [cy[:, n, SP_TOK:TS].rearrange("p (b t) -> p b t", b=SB) for n in range(2)]
                        dve.tensor_scalar(cy[:, 0, 0:SP_TOK], cvv[:, 0:SP_TOK], par[:, 2:3], None, ALU.mult)
                        dve.tensor_scalar(cys[0], samp[:, :, 0:DEC_L], par[:, 2:3], None, ALU.mult)
                        dve.drain()
                        for n in range(1, CONV_W):
                            dve.scalar_tensor_tensor(cy[:, n % 2, 0:SP_TOK], cvv[:, n:n + SP_TOK], par[:, 2 + n:3 + n],
                                                     cy[:, (n + 1) % 2, 0:SP_TOK], ALU.mult, ALU.add)
                            dve.scalar_tensor_tensor(cys[n % 2], samp[:, :, n:n + DEC_L], par[:, 2 + n:3 + n],
                                                     cys[(n + 1) % 2], ALU.mult, ALU.add)
                            dve.drain()
                        dve.tensor_copy(conv_carry[:, bass.ds(h, 1), :].rearrange("p a r -> p (a r)"), cvv[:, SP_TOK:SP_TOK + 2])
                        dve.tensor_copy(cst, samp[:, :, DEC_L:DEC_L + 2])
                        dve.tensor_tensor(y_conv[:, :], cy[:, 0, :], cbs[:, :], ALU.mult).then_inc(yc_rdy, 1)
                        dve.wait_ge(hg, HG * u + OST)
                        dve.tensor_tensor(y_rec[:, 0:SP_TOK], pt[:, :], gg[:, 0:SP_TOK], ALU.mult).then_inc(pt_free, 1)
                        dve.tensor_tensor(y_rec[:, SP_TOK:TS], pa[1][:, 0:SS_TOK], gg[:, SP_TOK:TS], ALU.mult).then_inc(pa_free[1], 1)
                        dve.drain().then_inc(yr_rdy, 1)
                dve.sem_inc(fin, 1)
                dve.wait_ge(fin_ps, 1)
                dve.tensor_copy(cy[0:2, 0, 0:CONV_DIM], pa[0][0:2, :])
                dve.tensor_copy(cy[0:16, 1, 0:CONV_DIM], po[0:16, :])
                dve.drain().then_inc(fin_sb, 1)


def output_phase(nc, io, keep, scr):
    WO_RING = 7
    ident, neg_half, logits = keep["ident"], keep["neg_half"], keep["logits"]
    T = TILES
    LAST = T - 1
    with ExitStack() as ctx:
        sb = lambda name, shape, dt=F32: ctx.enter_context(nc.sbuf_tensor(name, shape, dt))
        ps = lambda name, shape: ctx.enter_context(nc.psum_tensor(name, shape, F32))
        sem = lambda name: ctx.enter_context(nc.semaphore(name))
        mod_p = sb("mod_p", [P, 3, D])
        mod_s = sb("mod_s", [NSAMP, 3, D])
        ln1 = sb("ln1", [P, 2, D])
        wo_raw = sb("wo_raw", [P, WO_RING, D])
        wo_hi = sb("wo_hi", [P, KT, D], F32R)
        wo_lo = sb("wo_lo", [P, KT, D], F32R)
        w_rt = sb("w_rt", [P, KT, NG + NE])
        y_raw = sb("y_raw", [P, 2, KT, P])
        y_hi = sb("y_hi", [P, 2, KT, P], F32R)
        y_lo = sb("y_lo", [P, 2, KT, P], F32R)
        x_t = sb("x_t", [P, 2, D])
        z = sb("z", [P, D])
        z2 = sb("z2", [P, D])
        x1 = sb("x1", [P, 2, D])
        u2 = sb("u2", [P, 2, D])
        u2T = sb("u2T", [P, KT, P])
        stats = sb("stats", [P, 2, 6])
        mv = sb("mv", [P, 2])
        ve = sb("ve", [P, 1])
        rstd = sb("rstd", [P, 1])
        zero_row = sb("zero_row", [1, D])
        NLIST = (NE + 1) * CAP // P
        slot_i = sb("slot_i", [P, NLIST], I32)
        fill = sb("fill", [P, NLIST, 4], I32)
        pm = [ps("pm0", [P, 1024]), ps("pm1", [P, 1024])]
        px = ps("px", [P, 1024])
        pl = ps("pl", [P, 512])

        mod_in, mod_s_in, ln_in, rt_in = sem("mod2_in"), sem("mod2_s_in"), sem("ln_in"), sem("rt_in")
        scale_rdy = sem("scale2_rdy")
        wo_in = [sem("wo_in%d" % k) for k in range(WO_RING)]
        y_in = [sem("y_in0"), sem("y_in1")]
        x_in = [sem("x2_in0"), sem("x2_in1")]
        wo_h, wo_l, y_h, y_l = sem("wo_h"), sem("wo_l"), sem("y_h"), sem("y_l")
        prod, z_rdy, var_rdy, rs_rdy, x1_rdy, u2_rdy = (sem(n) for n in ("prod2", "z_rdy", "var_rdy", "rs_rdy", "x1_rdy", "u2_rdy"))
        uT_ps, uT_sb, lg_ps, lg_sb = sem("uT_ps"), sem("uT_sb"), sem("lg_ps"), sem("lg_sb")
        x1_out, u2_out = [sem("x1_out0"), sem("x1_out1")], [sem("u2_out0"), sem("u2_out1")]
        scaled = sem("u2_scaled")
        consts, fill_rdy, fill_out, zr_rdy, zr_out = (sem(n) for n in ("consts2", "fill_rdy", "fill_out", "zr_rdy", "zr_out"))
        tick = sem("tick2")
        wov = io["w_out"][0].rearrange("(k p) n -> p k n", p=P)
        xp = io["x_prompt"][0]
        xs = io["x_sample"].rearrange("b l d -> (b l) d")
        yv = scr["y"].rearrange("k p t -> p k t")

        def rows_of(t):
            return NSAMP if isinstance(t, int) and t == LAST else P

        with nc.Block() as block:
            @block.sync
            def _(sp):
                for k in range(WO_RING):
                    sp.dma_start(wo_raw[:, k], wov[:, k]).then_inc(wo_in[k], 16)

                def load_y(t, s):
                    n = rows_of(t)
                    sp.dma_start(y_raw[:, s, :, 0:n], yv[:, :, bass.ds(t * P, n)]).then_inc(y_in[s], 16)

                def load_x(t, s):
                    n = rows_of(t)
                    src = xs if n < P else xp[bass.ds(t * P, n), :]
                    sp.dma_start(x_t[0:n, s, :], src).then_inc(x_in[s], 16)

                load_y(0, 0)
                for k in range(WO_RING, KT):
                    sp.wait_ge(wo_l, k - WO_RING + 1)
                    sp.dma_start(wo_raw[:, k % WO_RING], wov[:, k]).then_inc(wo_in[k % WO_RING], 16)
                load_y(1, 1)
                sp.dma_start(mod_p[:, :, :].rearrange("p v d -> p (v d)"), row_bcast(scr["mod"][0, 2 * D:5 * D], P)).then_inc(mod_in, 16)
                load_x(0, 0)
                sp.dma_start(ln1[:, 0, :], row_bcast(io["ln_g"][0, 0], P)).then_inc(ln_in, 16)
                sp.dma_start(ln1[:, 1, :], row_bcast(io["ln_b"][0, 0], P)).then_inc(ln_in, 16)
                load_x(1, 1)
                for b in range(DEC_B):
                    sp.dma_start(mod_s[b * DEC_L:(b + 1) * DEC_L].rearrange("p v d -> p (v d)"),
                                 row_bcast(scr["mod"][b + 1, 2 * D:5 * D], DEC_L)).then_inc(mod_s_in, 16)

                def again(t, s):
                    sp.wait_ge(y_l, t - 1)
                    wait_apart(sp, z_rdy, t - 1, tick)
                    load_y(t, s)
                    load_x(t, s)
                with sp.Fori(1, LAST // 2) as i:
                    for s in range(2):
                        again(i * 2 + s, s)
                again(LAST, 0)

            @block.scalar
            def _(act):
                act.dma_start(w_rt[:, :, 0:NG], io["w_router_group"][0].rearrange("(k p) n -> p k n", p=P)).then_inc(rt_in, 16)
                act.dma_start(w_rt[:, :, NG:NG + NE], io["w_router_expert"][0].rearrange("(k p) n -> p k n", p=P)).then_inc(rt_in, 16)

                def hi(t, s, n_in):
                    n = rows_of(t)
                    act.wait_ge(y_in[s], n_in)
                    act.activation(y_hi[:, s, :, 0:n], y_raw[:, s, :, 0:n], ACT.Copy).then_inc(y_h, 1)

                def to_sb(t):
                    n = rows_of(t)
                    act.wait_ge(uT_ps, t + 1)
                    act.activation(u2T[:, :, 0:n], px[:, :].rearrange("p (k t) -> p k t", k=KT)[:, :, 0:n], ACT.Copy).then_inc(uT_sb, 1)

                for k in range(KT):
                    if k == KT // 2:
                        hi(0, 0, 16)
                    act.wait_ge(wo_in[k % WO_RING], 16 * (k // WO_RING) + 16)
                    act.activation(wo_hi[:, k], wo_raw[:, k % WO_RING], ACT.Copy).then_inc(wo_h, 1)
                hi(1, 1, 16)
                act.wait_ge(mod_in, 16)
                act.activation(mod_p[:, 2, :], mod_p[:, 2, :], ACT.Identity, bias=1.0).then_inc(scale_rdy, 1)
                act.wait_ge(mod_s_in, 16 * DEC_B)
                act.activation(mod_s[:, 2, :], mod_s[:, 2, :], ACT.Identity, bias=1.0).then_inc(scale_rdy, 1)
                act.wait_ge(prod, 1)
                hi(2, 0, 32)
                act.wait_ge(prod, 2)
                hi(3, 1, 32)
                to_sb(0)
                with act.Fori(1, (LAST - 2) // 2) as i:
                    for s in range(2):
                        act.wait_ge(prod, 2 * i + s + 1)
                        hi(2 * i + s + 2, s, 16 * i + 32)
                        to_sb(2 * i + s - 1)
                act.wait_ge(prod, LAST - 1)
                hi(LAST, 0, 16 * (LAST // 2) + 16)
                for t in range(LAST - 3, T):
                    to_sb(t)

            @block.gpsimd
            def _(pool):
                pool.memset(zero_row[:, :], 0.0).then_inc(zr_rdy, 1)
                pool.iota(slot_i[:, :], pattern=[[1, NLIST]], base=0, channel_multiplier=NLIST)
                pool.iota(fill[:, :, 0], pattern=[[0, NLIST]], base=NTOK, channel_multiplier=0)
                pool.memset(fill[:, :, 2:4], 0)
                pool.memset(logits[:, LAST, :], 0.0)
                pool.drain().then_inc(consts, 1)
                pool.wait_ge(zr_rdy, 1)
                pool.dma_start(scr["u2"][NTOK:NTOK + 1, :], zero_row[:, :]).then_inc(zr_out, 16)
                pool.wait_ge(fill_rdy, 1)
                pool.wait_ge(prod, 1)
                pool.dma_start(scr["list"].rearrange("(p s) c -> p (s c)", p=P), fill[:, :, :].rearrange("p s c -> p (s c)")).then_inc(fill_out, 16)
                pool.wait_ge(scale_rdy, 2)

                def tile(t, s, i):
                    n = rows_of(t)
                    m = mod_s if n < P else mod_p
                    pool.wait_ge(var_rdy, t + 1)
                    pool.tensor_tensor(rstd[0:n, :], ve[0:n, :], neg_half[0:n, 0:1], ALU.pow).then_inc(rs_rdy, 1)
                    pool.wait_ge(x1_rdy, t + 1)
                    pool.dma_start(scr["x1"][bass.ds(t * P, n), :], x1[0:n, s, :]).then_inc(x1_out[s], 16)
                    if not (isinstance(t, int) and t < 2):
                        wait_apart(pool, u2_out[s], 16 * i, tick)
                        wait_apart(pool, uT_ps, t - 1, tick)
                    pool.tensor_tensor(u2[0:n, s, :], x1[0:n, s, :], m[0:n, 2, :], ALU.mult).then_inc(scaled, 1)
                    wait_apart(pool, scaled, t + 1, tick)
                    pool.tensor_tensor(u2[0:n, s, :], u2[0:n, s, :], m[0:n, 1, :], ALU.add).then_inc(u2_rdy, 1)
                    wait_apart(pool, u2_rdy, t + 1, tick)
                    pool.dma_start(scr["u2"][bass.ds(t * P, n), :], u2[0:n, s, :]).then_inc(u2_out[s], 16)
                tile(0, 0, 0)
                tile(1, 1, 0)
                with pool.Fori(1, LAST // 2) as i:
                    tile(2 * i, 0, i)
                    tile(2 * i + 1, 1, i)
                tile(LAST, 0, LAST // 2)
                for s in range(2):
                    n_out = 16 * (LAST // 2 + (1 - s))
                    pool.wait_ge(x1_out[s], n_out)
                    pool.wait_ge(u2_out[s], n_out)
                pool.wait_ge(zr_out, 16)
                pool.wait_ge(fill_out, 16)

            @block.tensor
            def _(pe):

                def project(t, s):
                    n = rows_of(t)
                    pe.wait_ge(y_l, t + 1)
                    if not (isinstance(t, int) and t < 2):
                        pe.wait_ge(z_rdy, t - 1)
                    for k in range(KT):
                        if isinstance(t, int) and t == 0:
                            pe.wait_ge(wo_l, k + 1)
                        for m, (a, w) in enumerate(((y_hi, wo_hi), (y_hi, wo_lo), (y_lo, wo_hi))):
                            for hf in range(2):
                                last = pe.matmul(pm[s][0:n, hf * 512:(hf + 1) * 512], a[:, s, k, 0:n],
                                                 w[:, k, hf * 512:(hf + 1) * 512],
                                                 start=(k == 0 and m == 0), stop=(k == KT - 1 and m == 2))
                    last.then_inc(prod, 1)

                def route(t, s):
                    n = rows_of(t)
                    pe.wait_ge(u2_rdy, t + 1)
                    if not (isinstance(t, int) and t < 1):
                        pe.wait_ge(uT_sb, t)
                    for k in range(KT):
                        last = pe.transpose(px[:, k * P:k * P + n], u2[0:n, s, k * P:(k + 1) * P], ident[0:n, 0:n])
                    last.then_inc(uT_ps, 1)
                    if isinstance(t, int) and t == 0:
                        pe.wait_ge(rt_in, 32)
                    pe.wait_ge(uT_sb, t + 1)
                    if not (isinstance(t, int) and t < 1):
                        pe.wait_ge(lg_sb, t)
                    for k in range(KT):
                        last = pe.matmul(pl[0:n, 0:NG + NE], u2T[:, k, 0:n], w_rt[:, k, :], start=(k == 0), stop=(k == KT - 1))
                    last.then_inc(lg_ps, 1)

                project(0, 0)
                project(1, 1)
                for t in (2, 3):
                    project(t, t % 2)
                    route(t - 2, t % 2)
                with pe.Fori(2, LAST // 2) as i:
                    for s in range(2):
                        project(2 * i + s, s)
                        route(2 * i + s - 2, s)
                project(LAST, 0)
                for t in range(LAST - 2, T):
                    route(t, t % 2)

            @block.vector
            def _(dve):
                def lo(t, s):
                    n = rows_of(t)
                    dve.wait_ge(y_h, t + 1)
                    dve.tensor_tensor(y_lo[:, s, :, 0:n], y_raw[:, s, :, 0:n], y_hi[:, s, :, 0:n].bitcast(F32), ALU.subtract).then_inc(y_l, 1)

                def norm(t, s, i):
                    n = rows_of(t)
                    m = mod_s if n < P else mod_p
                    dve.wait_ge(prod, t + 1)
                    dve.tensor_tensor(z[0:n, :], pm[s][0:n, :], m[0:n, 0, :], ALU.mult)
                    dve.drain()
                    dve.wait_ge(x_in[s], 16 * i + 16)
                    dve.scalar_tensor_tensor(z2[0:n, :], x_t[0:n, s, :], ALPHA, z[0:n, :], ALU.mult, ALU.add)
                    dve.drain().then_inc(z_rdy, 1)
                    for a in range(2):
                        dve.bn_stats(stats[0:n, a, :], z2[0:n, a * 512:(a + 1) * 512])
                    dve.drain()
                    dve.bn_aggr(mv[0:n, :], stats[0:n, :, :])
                    dve.drain()
                    dve.tensor_scalar(ve[0:n, :], mv[0:n, 1:2], LN_EPS, None, ALU.add).then_inc(var_rdy, 1)
                    dve.wait_ge(rs_rdy, t + 1)
                    dve.tensor_scalar(z[0:n, :], z2[0:n, :], mv[0:n, 0:1], rstd[0:n, :], ALU.subtract, ALU.mult)
                    dve.drain()
                    dve.tensor_tensor(z2[0:n, :], z[0:n, :], ln1[0:n, 0, :], ALU.mult)
                    dve.drain()
                    if not (isinstance(t, int) and t < 2):
                        wait_apart(dve, x1_out[s], 16 * i, tick)
                        wait_apart(dve, u2_rdy, t - 1, tick)
                    dve.tensor_tensor(x1[0:n, s, :], z2[0:n, :], ln1[0:n, 1, :], ALU.add).then_inc(x1_rdy, 1)

                def keep_logits(t):
                    n = rows_of(t)
                    dve.wait_ge(lg_ps, t + 1)
                    dst = logits[0:n, bass.ds(t, 1), :].rearrange("p a c -> p (a c)")
                    dve.tensor_copy(dst, pl[0:n, 0:NG + NE]).then_inc(lg_sb, 1)

                dve.wait_ge(consts, 1)
                dve.tensor_scalar(slot_i[:, :], slot_i[:, :], P - 1, None, ALU.bitwise_and)
                dve.drain()
                dve.tensor_scalar(fill[:, :, 1], slot_i[:, :], 2 * NTOK, None, ALU.add)
                dve.drain().then_inc(fill_rdy, 1)
                for k in range(KT):
                    if k == KT // 2:
                        lo(0, 0)
                    dve.wait_ge(wo_h, k + 1)
                    dve.tensor_tensor(wo_lo[:, k], wo_raw[:, k % WO_RING], wo_hi[:, k].bitcast(F32), ALU.subtract).then_inc(wo_l, 1)
                lo(1, 1)
                dve.wait_ge(mod_in, 16)
                dve.wait_ge(mod_s_in, 16 * DEC_B)
                dve.wait_ge(ln_in, 32)
                norm(0, 0, 0)
                lo(2, 0)
                norm(1, 1, 0)
                lo(3, 1)
                keep_logits(0)
                with dve.Fori(1, (LAST - 2) // 2) as i:
                    for s in range(2):
                        norm(2 * i + s, s, i)
                        lo(2 * i + s + 2, s)
                        keep_logits(2 * i + s - 1)
                norm(LAST - 2, 0, LAST // 2 - 1)
                lo(LAST, 0)
                keep_logits(LAST - 3)
                norm(LAST - 1, 1, LAST // 2 - 1)
                keep_logits(LAST - 2)
                norm(LAST, 0, LAST // 2)
                keep_logits(LAST - 1)
                keep_logits(LAST)


def gate_up_w(buf, s):
    return buf[:, bass.ds(s, 1), 0:KT * 2 * DE].rearrange("p a (k c f) -> p (a k) c f", k=KT, c=2)


def load_gate_up(eng, io, keep, e, s):
    for c, (w, landed) in enumerate((("w_e_gate", "wg_in"), ("w_e_up", "wu_in"))):
        eng.dma_start(gate_up_w(keep["gu_raw"], s)[:, :, c, :],
                      io[w][0, bass.ds(e, 1)].rearrange("e (k p) f -> p (e k) f", p=P)).then_inc(keep[landed], 16)


def w_slot(buf, s, lo, hi):
    return buf[:, bass.ds(s, 1), lo:hi].rearrange("p a w -> p (a w)")


def split_high(act, keep, e, a, s, r):
    lo, hi = a * KT * DE, (a + 1) * KT * DE
    act.activation(w_slot(keep["gu_hi"], s, lo, hi), w_slot(keep["gu_raw"], r, lo, hi), ACT.Copy).then_inc(keep["gu_h"], 1)


def split_low(dve, keep, e, a, s, r):
    lo, hi = a * KT * DE, (a + 1) * KT * DE
    dve.wait_ge(keep["gu_h"], 2 * e + (a + 1))
    dve.tensor_tensor(w_slot(keep["gu_lo"], s, lo, hi), w_slot(keep["gu_raw"], r, lo, hi),
                      w_slot(keep["gu_hi"], s, lo, hi).bitcast(F32), ALU.subtract).then_inc(keep["gu_l"], 1)


def load_down(eng, io, keep, e, s):
    eng.dma_start(keep["dn_w"][:, bass.ds(s, 1), :].rearrange("p a (k n) -> p (a k) n", k=DE // P),
                  io["w_e_down"][0, bass.ds(e, 1)].rearrange("e (k p) n -> p (e k) n", p=P)).then_inc(keep["wd_in"], 16)


def routing_phase(nc, io, keep, scr):
    ones, tri, logits = keep["ones"], keep["tri"], keep["logits"]
    blk_tab, exp_tab = keep["blk_tab"], keep["exp_tab"]
    T = TILES
    LAST = T - 1
    with ExitStack() as ctx:
        sb = lambda name, shape, dt=F32: ctx.enter_context(nc.sbuf_tensor(name, shape, dt))
        ps = lambda name, shape: ctx.enter_context(nc.psum_tensor(name, shape, F32))
        sem = lambda name: ctx.enter_context(nc.semaphore(name))
        gmax, gsum, psel, gidx = (sb(n, [P, T]) for n in ("gmax", "gsum", "psel", "gidx"))
        gd, gs1, gs2, gr, ge, gq = (sb(n, [P, T, NG]) for n in ("gd", "gs1", "gs2", "gr", "ge", "gq"))
        lem, lem2, eq1, oh1, oh2, posf, tmp = (sb(n, [P, T, NE]) for n in ("lem", "lem2", "eq1", "oh1", "oh2", "posf", "tmp"))
        mm = sb("mm", [P, T, NE])
        m1, m2, e1, dm, w1, w2 = (sb(n, [P, T]) for n in ("m1", "m2", "e1", "dm", "w1", "w2"))
        valid = sb("valid", [P, T])
        base = sb("base", [P, T + 1, NE])
        dest_f = sb("dest_f", [P, T, 2])
        dest = sb("dest", [P, T, 2], I32)
        rows = sb("rows", [P, T, 2, 4], I32)
        cj_g = sb("cj_g", [P, NG])
        cj_e = sb("cj_e", [P, NE])
        ecap = sb("ecap", [P, NE])
        pidx = sb("pidx", [P, 1])
        cnt = sb("cnt", [P, NE])
        cnt_i = sb("cnt_i", [P, NE], I32)
        nb_i = sb("nb_i", [P, NE], I32)
        nb = sb("nb", [P, NE])
        cum = sb("cum", [P, 2, NE])
        cmp_, cmp2 = sb("cmp_", [P, NE]), sb("cmp2", [P, NE])
        eg, gst = sb("eg", [P, 1]), sb("gst", [P, 1])
        odd = sb("odd", [1, 1], I32)
        tab_f = sb("tab_f", [P, 2])
        tab_i = sb("tab_i", [P, 2], I32)
        wm = sb("wm_gate2", [P, 2, KT, 512])
        bm = sb("bm_gate2", [1 + DEC_B, D])
        pm = [ps("pr_rank", [P, 1024]), ps("pr_total", [P, 1024])]
        pg2 = ps("pg2", [P, 1024])
        wm_in, g2_ps = sem("wm_in"), sem("g2_ps")
        wmv = io["w_mod"][0].rearrange("(k p) n -> p k n", p=P)
        consts = sem("consts_r")
        r_dve, r_act, r_pe, rows_rdy = sem("r_dve"), sem("r_act"), sem("r_pe"), sem("rows_rdy")
        sc_out, tab_rdy, tab_out, tab_in = sem("sc_out"), sem("tab_rdy"), sem("tab_out"), sem("tab_in")

        def rows_of(t):
            return NSAMP if t == LAST else P

        with nc.Block() as block:
            @block.sync
            def _(sp):
                for e in range(RAW):
                    if e:
                        for landed in ("wg_in", "wu_in", "wd_in"):
                            sp.wait_ge(keep[landed], 16 * e)
                    load_gate_up(sp, io, keep, e, e)
                    load_down(sp, io, keep, e, e)
                for hf in range(2):
                    sp.dma_start(wm[:, hf], wmv[:, :, 5 * D + hf * 512:5 * D + (hf + 1) * 512]).then_inc(wm_in, 16)
                sp.dma_start(bm[:, :], row_bcast(io["b_mod"][0, 5 * D:6 * D], 1 + DEC_B)).then_inc(wm_in, 16)
                sp.wait_ge(tab_rdy, 1)
                sp.dma_start(scr["tab"], tab_i[:, :]).then_inc(tab_out, 16)
                sp.wait_ge(tab_out, 16)
                sp.dma_start(blk_tab[:, :], scr["tab"].rearrange("(a g) c -> a (g c)", a=1)).then_inc(tab_in, 16)
                sp.wait_ge(tab_in, 16)

            @block.scalar
            def _(act):
                act.wait_ge(r_dve, 1)
                act.activation(gs1[:, :, :], gd[:, :, :], ACT.Sigmoid)
                act.activation(gs2[:, :, :], gd[:, :, :], ACT.Sigmoid, scale=-1.0).then_inc(r_act, 1)
                act.wait_ge(r_dve, 2)
                act.activation(w1[:, :], dm[:, :], ACT.Sigmoid)
                act.activation(w2[:, :], dm[:, :], ACT.Sigmoid, scale=-1.0).then_inc(r_act, 1)
                for e in range(2):
                    act.wait_ge(keep["wg_in"], 16 * e + 16)
                    act.wait_ge(keep["wu_in"], 16 * e + 16)
                    for a in range(2):
                        split_high(act, keep, e, a, e, e)

            @block.gpsimd
            def _(pool):
                pool.iota(rows[:, :, 0, 0], pattern=[[P, T]], base=0, channel_multiplier=1)
                pool.iota(rows[:, :, 1, 0], pattern=[[P, T]], base=0, channel_multiplier=1)
                pool.iota(rows[:, :, 0, 1], pattern=[[2 * P, T]], base=0, channel_multiplier=2)
                pool.iota(rows[:, :, 1, 1], pattern=[[2 * P, T]], base=1, channel_multiplier=2)
                pool.memset(rows[:, :, :, 3], 0)
                pool.iota(cj_g[:, :], pattern=[[1, NG]], base=-NG, channel_multiplier=0, allow_small_or_imprecise_dtypes=True)
                pool.iota(cj_e[:, :], pattern=[[1, NE]], base=-NE, channel_multiplier=0, allow_small_or_imprecise_dtypes=True)
                pool.iota(ecap[:, :], pattern=[[CAP, NE]], base=0, channel_multiplier=0, allow_small_or_imprecise_dtypes=True)
                pool.iota(pidx[:, :], pattern=[[0, 1]], base=0, channel_multiplier=1, allow_small_or_imprecise_dtypes=True)
                pool.memset(valid[:, :], 1.0)
                pool.drain()
                pool.memset(valid[NSAMP:P, LAST:T], 0.0)
                pool.drain().then_inc(consts, 1)
                pool.wait_ge(rows_rdy, 1)
                for t in range(T):
                    n = rows_of(t)
                    for k in range(2):
                        pool.indirect_dma_start(scr["list"], bass.IndirectOffsetOnAxis(ap=dest[0:n, t, k:k + 1], axis=0),
                                                rows[0:n, t, k, :], None).then_inc(sc_out, 16)
                pool.wait_ge(sc_out, 16 * 2 * T)

            @block.tensor
            def _(pe):
                pe.wait_ge(r_dve, 3)
                mf = mm[:, :, :].rearrange("p t e -> p (t e)")
                n1 = 512
                n2 = T * NE - n1
                pe.matmul(pm[0][:, 0:n1], tri[:, :], mf[:, 0:n1], start=True, stop=True)
                pe.matmul(pm[0][:, 512:512 + n2], tri[:, :], mf[:, n1:n1 + n2], start=True, stop=True)
                pe.matmul(pm[1][:, 0:n1], ones[:, :], mf[:, 0:n1], start=True, stop=True)
                pe.matmul(pm[1][:, 512:512 + n2], ones[:, :], mf[:, n1:n1 + n2], start=True, stop=True).then_inc(r_pe, 1)
                pe.wait_ge(wm_in, 48)
                for hf in range(2):
                    for k in range(KT):
                        last = pe.matmul(pg2[0:1 + DEC_B, hf * 512:(hf + 1) * 512], keep["cT"][:, k, :], wm[:, hf, k, :],
                                         start=(k == 0), stop=(k == KT - 1))
                last.then_inc(g2_ps, 1)

            @block.vector
            def _(dve):
                dve.wait_ge(consts, 1)
                def over(ap, n):
                    return ap.rearrange("p (t a) -> p t a", a=1).broadcast_to([P, T, n])

                def const(ap, n):
                    return ap.rearrange("p (a j) -> p a j", a=1).broadcast_to([P, T, n])

                lg, le = logits[:, :, 0:NG], logits[:, :, NG:NG + NE]
                dve.tensor_reduce(gmax[:, :], lg, axis=AX.X, op=ALU.max)
                dve.drain()
                dve.tensor_tensor(gd[:, :, :], lg, over(gmax[:, :], NG), ALU.subtract)
                dve.drain().then_inc(r_dve, 1)
                dve.tensor_scalar(gq[:, :, :], gd[:, :, :], 0.0, None, ALU.is_equal)
                dve.drain()
                dve.tensor_tensor(ge[:, :, :], gq[:, :, :], const(cj_g[:, :], NG), ALU.mult)
                dve.drain()
                dve.tensor_reduce(gidx[:, :], ge[:, :, :], axis=AX.X, op=ALU.min)
                dve.drain()
                dve.tensor_tensor(gq[:, :, :], const(cj_g[:, :], NG), over(gidx[:, :], NG), ALU.is_equal)
                dve.drain()
                dve.tensor_scalar(gq[:, :, :], gq[:, :, :], -1.0, BIG, ALU.add, ALU.mult)
                dve.drain()
                pen = gq[:, :, :].rearrange("p t (g a) -> p (t g) a", a=1).broadcast_to([P, T * NG, EPG])
                dve.tensor_copy(tmp[:, :, :], le)
                dve.drain()
                dve.tensor_tensor(lem[:, :, :].rearrange("p t (g e) -> p (t g) e", e=EPG),
                                  tmp[:, :, :].rearrange("p t (g e) -> p (t g) e", e=EPG), pen, ALU.add)
                dve.wait_ge(r_act, 1)
                dve.reciprocal(gr[:, :, :], gs2[:, :, :])
                dve.drain()
                dve.tensor_tensor(ge[:, :, :], gs1[:, :, :], gr[:, :, :], ALU.mult)
                dve.drain()
                dve.tensor_reduce(gsum[:, :], ge[:, :, :], axis=AX.X, op=ALU.add)
                dve.drain()
                dve.reciprocal(psel[:, :], gsum[:, :])

                def top(src, val, onehot):
                    dve.tensor_reduce(val[:, :], src[:, :, :], axis=AX.X, op=ALU.max)
                    dve.drain()
                    dve.tensor_tensor(eq1[:, :, :], src[:, :, :], over(val[:, :], NE), ALU.is_equal)
                    dve.drain()
                    dve.tensor_tensor(tmp[:, :, :], eq1[:, :, :], const(cj_e[:, :], NE), ALU.mult)
                    dve.drain()
                    dve.tensor_reduce(e1[:, :], tmp[:, :, :], axis=AX.X, op=ALU.min)
                    dve.drain()
                    dve.tensor_tensor(onehot[:, :, :], const(cj_e[:, :], NE), over(e1[:, :], NE), ALU.is_equal)
                    dve.drain()

                top(lem, m1, oh1)
                dve.scalar_tensor_tensor(lem2[:, :, :], oh1[:, :, :], -BIG, lem[:, :, :], ALU.mult, ALU.add)
                dve.drain()
                top(lem2, m2, oh2)
                dve.tensor_tensor(dm[:, :], m1[:, :], m2[:, :], ALU.subtract)
                dve.drain().then_inc(r_dve, 1)
                dve.tensor_tensor(tmp[:, :, :], oh1[:, :, :], oh2[:, :, :], ALU.add)
                dve.drain()
                dve.tensor_tensor(mm[:, :, :], tmp[:, :, :], over(valid[:, :], NE), ALU.mult)
                dve.drain().then_inc(r_dve, 1)
                dve.wait_ge(r_act, 2)
                dve.tensor_tensor(rows[:, :, 0, 2].bitcast(F32), psel[:, :], w1[:, :], ALU.mult)
                dve.tensor_tensor(rows[:, :, 1, 2].bitcast(F32), psel[:, :], w2[:, :], ALU.mult)
                dve.tensor_copy(base[:, 0, :], ecap[:, :])
                dve.drain()
                dve.wait_ge(r_pe, 1)
                for t in range(T):
                    dve.tensor_tensor(base[:, t + 1, :], base[:, t, :], pm[1][:, t * NE:(t + 1) * NE], ALU.add)
                    dve.drain()
                dve.tensor_tensor(posf[:, :, :].rearrange("p t e -> p (t e)"), pm[0][:, 0:T * NE],
                                  base[:, 0:T, :].rearrange("p t e -> p (t e)"), ALU.add)
                dve.drain()
                for k, oh in enumerate((oh1, oh2)):
                    dve.tensor_tensor(tmp[:, :, :], posf[:, :, :], oh[:, :, :], ALU.mult)
                    dve.drain()
                    dve.tensor_reduce(dest_f[:, :, k], tmp[:, :, :], axis=AX.X, op=ALU.add)
                    dve.drain()
                dve.tensor_copy(dest[:, :, :], dest_f[:, :, :])
                dve.drain().then_inc(rows_rdy, 1)
                dve.tensor_tensor(cnt[:, :], base[:, T, :], ecap[:, :], ALU.subtract)
                dve.drain()
                dve.tensor_scalar(cnt[:, :], cnt[:, :], float(P - 1), None, ALU.add)
                dve.drain()
                dve.tensor_copy(cnt_i[:, :], cnt[:, :])
                dve.drain()
                dve.tensor_scalar(nb_i[:, :], cnt_i[:, :], 7, None, ALU.logical_shift_right)
                dve.drain()
                dve.tensor_copy(nb[:, :], nb_i[:, :])
                dve.drain()
                dve.tensor_scalar(nb[:, :], nb[:, :], 1.0, None, ALU.max)
                dve.drain()
                dve.tensor_copy(cum[:, 0, :], nb[:, :])
                dve.drain()
                src = 0
                step = 1
                while step < NE:
                    dve.tensor_copy(cum[:, 1 - src, 0:step], cum[:, src, 0:step])
                    dve.tensor_tensor(cum[:, 1 - src, step:NE], cum[:, src, step:NE], cum[:, src, 0:NE - step], ALU.add)
                    dve.drain()
                    src, step = 1 - src, step * 2
                dve.memset(exp_tab[:, 0:1], 0)
                dve.tensor_copy(exp_tab[:, 1:NE + 1], cum[0:1, src, :])
                dve.drain()
                dve.tensor_scalar(odd[:, :], exp_tab[:, NE:NE + 1], 1, None, ALU.bitwise_and)
                dve.drain()
                dve.tensor_tensor(exp_tab[:, NE:NE + 1], exp_tab[:, NE:NE + 1], odd[:, :], ALU.add)
                dve.tensor_scalar(cmp_[:, :], cum[:, src, :], pidx[:, :], None, ALU.is_le)
                dve.drain()
                dve.tensor_reduce(eg[:, :], cmp_[:, :], axis=AX.X, op=ALU.add)
                dve.tensor_tensor(cmp2[:, :], cmp_[:, :], nb[:, :], ALU.mult)
                dve.drain()
                dve.tensor_reduce(gst[:, :], cmp2[:, :], axis=AX.X, op=ALU.add)
                dve.tensor_scalar(tab_f[:, 0:1], eg[:, :], float(NE - 1), None, ALU.min)
                dve.drain()
                dve.tensor_tensor(gst[:, :], pidx[:, :], gst[:, :], ALU.subtract)
                dve.tensor_scalar(eg[:, :], eg[:, :], float(CAP // P), None, ALU.mult)
                dve.drain()
                dve.tensor_tensor(tab_f[:, 1:2], eg[:, :], gst[:, :], ALU.add)
                dve.drain()
                dve.tensor_copy(tab_i[:, :], tab_f[:, :])
                dve.drain().then_inc(tab_rdy, 1)
                for e in range(2):
                    for a in range(2):
                        split_low(dve, keep, e, a, e, e)
                dve.wait_ge(g2_ps, 1)
                dve.wait_ge(wm_in, 48)
                dve.tensor_tensor(keep["gate2"][:, :], pg2[0:1 + DEC_B, :], bm[:, :], ALU.add)


def expert_phase(nc, io, keep, scr):
    ident, blk_tab, exp_tab = keep["ident"], keep["blk_tab"], keep["exp_tab"]
    gu_hi, gu_lo, dn_w, gu_l = keep["gu_hi"], keep["gu_lo"], keep["dn_w"], keep["gu_l"]
    wg_in, wu_in, wd_in = keep["wg_in"], keep["wu_in"], keep["wd_in"]
    KD = DE // P
    GU = 2 * DE
    WG = KT * GU
    AHEAD = 4
    RING = 8
    MAXB = 2 * TILES + NE
    with ExitStack() as ctx:
        sb = lambda name, shape, dt=F32: ctx.enter_context(nc.sbuf_tensor(name, shape, dt))
        ps = lambda name, shape: ctx.enter_context(nc.psum_tensor(name, shape, F32))
        sem = lambda name: ctx.enter_context(nc.semaphore(name))
        xg = sb("xg", [P, 2, D])
        x_hi = sb("x_hi", [P, KT, P], F32R)
        x_lo = sb("x_lo", [P, KT, P], F32R)
        gsig = sb("gsig", [P, DE])
        gsil = sb("gsil", [P, DE])
        hh = sb("hh", [P, DE])
        hhT = sb("hhT", [P, KD, P])
        y_sb = sb("y_sb", [P, D])
        ids_ring = sb("ids_ring", [P, RING, 4], I32)
        ids_now = sb("ids_now", [P, 4], I32)
        ids_cur = sb("ids_cur", [P, 4], I32)
        ph = ps("ph", [P, 512])
        px = ps("pxe", [P, 1024])
        pht = ps("pht", [P, 512])
        py = ps("py", [P, 1024])
        ids_in, xg_in, y_out = sem("ids_in"), sem("xg_in"), sem("y2_out")
        xT_ps, x_h, x_l = sem("xTe_ps"), sem("xe_h"), sem("xe_l")
        gu, sig, h_rdy = sem("gu_done"), sem("sig_done"), sem("h_rdy")
        hT, hT_sb = sem("hT_ps"), sem("hT_sb")
        dn, y_rdy, cur = sem("dn_done"), sem("y_rdy"), sem("cur_rdy")
        kept = sem("kept")
        tick = sem("tick3")

        def blocks_before(eng, e):
            return eng.value_load(exp_tab[0:1, bass.ds(e, 1)], min_val=0, max_val=MAXB)

        def expert_loop(eng, split_gu, block_work):
            def expert(e, gu_next):
                first = blocks_before(eng, e)
                last = eng.snap(eng.value_load(exp_tab[0:1, bass.ds(e + 1, 1)], min_val=1, max_val=MAXB) - 1)
                with eng.If_lt(eng.to_reg(first), eng.to_reg(last)):
                    with eng.Fori(first, last) as g:
                        block_work(g, None)
                if gu_next is not None:
                    split_gu(gu_next, 0, last)
                block_work(last, gu_next)
            with eng.Fori(0, NE - 2) as e:
                expert(e, e + 2)
            expert(NE - 2, None)
            expert(NE - 1, None)

        with nc.Block() as block:
            @block.sync
            def _(sp):
                def gate_up(e, s):
                    if not (isinstance(e, int) and e < RAW):
                        wait_apart(sp, gu_l, 2 * (e - RAW) + 2, tick)
                    for landed in (wg_in, wu_in):
                        wait_apart(sp, landed, 16 * e, tick)
                    load_gate_up(sp, io, keep, e, s)

                def down(e, s):
                    if not (isinstance(e, int) and e < RAW):
                        wait_apart(sp, dn, blocks_before(sp, e - (RAW - 1)) + 1, tick)
                    wait_apart(sp, wd_in, 16 * e, tick)
                    load_down(sp, io, keep, e, s)

                sp.wait_ge(xg_in, 32)
                gate_up(3, 0)
                with sp.Fori(4, NE) as e:
                    gate_up(e, sp.snap(e % RAW))
                    down(e - 1, sp.snap((e - 1) % RAW))
                down(NE - 1, (NE - 1) % RAW)

            @block.gpsimd
            def _(pool):
                total = blocks_before(pool, NE)

                def place(buf, i):
                    return buf[:, bass.ds(i, 1), :].rearrange("p a c -> p (a c)")

                def fetch_ids(b, at_ring):
                    at = pool.value_load(blk_tab[0:1, bass.ds(2 * b + 1, 1)], min_val=0, max_val=(NE + 1) * (CAP // P) - 1)
                    pool.dma_start(place(ids_ring, at_ring), scr["list"][bass.ds(at * P, P), :]).then_inc(ids_in, 16)

                def gather(b, at_ring, half):
                    pool.tensor_copy(ids_now[:, :], place(ids_ring, at_ring)).then_inc(kept, 1)
                    wait_apart(pool, kept, b + 1, tick)
                    pool.indirect_dma_start(xg[:, half, :], None, scr["u2"],
                                            bass.IndirectOffsetOnAxis(ap=ids_now[:, 0:1], axis=0)).then_inc(xg_in, 16)

                fetch_ids(0, 0)
                for b in range(AHEAD):
                    pool.wait_ge(ids_in, 16 * b + 16)
                    fetch_ids(b + 1, b + 1)
                    if b:
                        pool.wait_ge(xg_in, 16 * b)
                    if b >= 2:
                        pool.wait_ge(xT_ps, b - 1)
                    gather(b, b, b % 2)

                def block(g, half):
                    ahead = g + AHEAD
                    wait_apart(pool, ids_in, 16 * ahead + 16, tick)
                    fetch_ids(ahead + 1, (ahead + 1) % RING)
                    wait_apart(pool, xg_in, 16 * ahead, tick)
                    wait_apart(pool, xT_ps, ahead - 1, tick)
                    gather(ahead, ahead % RING, half)
                    if not (isinstance(g, int) and g == 0):
                        wait_apart(pool, y_out, 16 * g, tick)
                    pool.tensor_copy(ids_cur[:, :], place(ids_ring, g % RING)).then_inc(cur, 1)
                    wait_apart(pool, cur, g + 1, tick)
                    wait_apart(pool, y_rdy, g + 2, tick)
                    pool.indirect_dma_start(scr["y2"], bass.IndirectOffsetOnAxis(ap=ids_cur[:, 1:2], axis=0), y_sb[:, :], None).then_inc(y_out, 16)

                block(0, 0)
                block(1, 1)
                with pool.Fori(2, total, 2) as g:
                    block(g, 0)
                    block(pool.snap(g + 1), 1)
                wait_apart(pool, y_out, 16 * total, tick)
                wait_apart(pool, ids_in, 16 * total + 16 * (AHEAD + 1), tick)
                wait_apart(pool, xg_in, 16 * total + 16 * AHEAD, tick)

            @block.scalar
            def _(act):
                def split_gu(e, a, last=None):
                    if a == 0:
                        act.wait_ge(wg_in, 16 * e + 16)
                        act.wait_ge(wu_in, 16 * e + 16)
                    if last is not None:
                        act.wait_ge(gu, last + 1)
                    split_high(act, keep, e, a, act.snap(e % 2), act.snap(e % RAW))

                def x_evac(b):
                    act.wait_ge(xT_ps, b + 1)
                    act.activation(x_hi[:, :, :], px[:, :].rearrange("p (k t) -> p k t", k=KT), ACT.Copy).then_inc(x_h, 1)

                def sigmoid(b):
                    act.wait_ge(gu, b + 1)
                    act.activation(gsig[:, :], ph[:, 0:DE], ACT.Sigmoid).then_inc(sig, 1)

                def block_work(g, gu_next):
                    act.wait_ge(hT, g + 1)
                    act.activation(hhT[:, :, :], pht[:, 0:KD * P].rearrange("p (k t) -> p k t", k=KD), ACT.Copy).then_inc(hT_sb, 1)
                    sigmoid(g + 1)
                    x_evac(g + 2)
                    if gu_next is not None:
                        split_gu(gu_next, 1)
                    act.wait_ge(dn, g + 2)
                    act.wait_ge(cur, g + 1)
                    act.activation(y_sb[:, :], py[:, :], ACT.Copy, scale=ids_cur[:, 2:3].bitcast(F32)).then_inc(y_rdy, 1)

                act.sem_inc(y_rdy, 1)
                x_evac(0)
                sigmoid(0)
                x_evac(1)
                expert_loop(act, split_gu, block_work)

            @block.vector
            def _(dve):
                def split_gu(e, a, last=None):
                    split_low(dve, keep, e, a, dve.snap(e % 2), dve.snap(e % RAW))

                def x_evac(b):
                    dve.wait_ge(x_h, b + 1)
                    dve.tensor_tensor(x_lo[:, :, :], px[:, :].rearrange("p (k t) -> p k t", k=KT), x_hi[:, :, :].bitcast(F32), ALU.subtract).then_inc(x_l, 1)

                def gate(b):
                    dve.wait_ge(sig, b + 1)
                    dve.tensor_tensor(gsil[:, :], ph[:, 0:DE], gsig[:, :], ALU.mult)
                    dve.drain()
                    dve.tensor_tensor(hh[:, :], ph[:, DE:GU], gsil[:, :], ALU.mult).then_inc(h_rdy, 1)

                def block_work(g, gu_next):
                    gate(g + 1)
                    x_evac(g + 2)
                    if gu_next is not None:
                        split_gu(gu_next, 1)

                x_evac(0)
                gate(0)
                x_evac(1)
                expert_loop(dve, split_gu, block_work)

            @block.tensor
            def _(pe):
                total = blocks_before(pe, NE)

                def expert_of(b):
                    return pe.value_load(blk_tab[0:1, bass.ds(2 * b, 1)], min_val=0, max_val=NE - 1)

                def transposes(b, half):
                    pe.wait_ge(xg_in, 16 * b + 16)
                    if not (isinstance(b, int) and b == 0):
                        pe.wait_ge(x_l, b)
                    for k in range(KT):
                        last = pe.transpose(px[:, k * P:(k + 1) * P], xg[:, half, k * P:(k + 1) * P], ident[:, :])
                    last.then_inc(xT_ps, 1)

                def gate_up(b, e, s):
                    pe.wait_ge(gu_l, 2 * e + 1)
                    pe.wait_ge(x_l, b + 1)
                    if not (isinstance(b, int) and b == 0):
                        pe.wait_ge(h_rdy, b)
                    for k in range(KT):
                        if k == KT // 2:
                            pe.wait_ge(gu_l, 2 * e + 2)
                        for m, (x, w) in enumerate(((x_hi, gu_hi), (x_hi, gu_lo), (x_lo, gu_hi))):
                            last = pe.matmul(ph[:, :], x[:, k, :], w_slot(w, s, k * GU, (k + 1) * GU),
                                             start=(k == 0 and m == 0), stop=(k == KT - 1 and m == 2))
                    last.then_inc(gu, 1)

                pe.sem_inc(dn, 1)
                transposes(0, 0)
                gate_up(0, 0, 0)
                transposes(1, 1)
                def block_step(g, half):
                    e_now, e_next = expert_of(g), expert_of(g + 1)
                    s_down, s_next = pe.snap(e_now % RAW), pe.snap(e_next % 2)
                    gate_up(g + 1, e_next, s_next)
                    pe.wait_ge(h_rdy, g + 1)
                    for k in range(KD):
                        last = pe.transpose(pht[:, k * P:(k + 1) * P], hh[:, k * P:(k + 1) * P], ident[:, :])
                    last.then_inc(hT, 1)
                    transposes(g + 2, half)
                    pe.wait_ge(hT_sb, g + 1)
                    pe.wait_ge(wd_in, 16 * e_now + 16)
                    pe.wait_ge(y_rdy, g + 1)
                    for k in range(KD):
                        for hf in range(2):
                            at = k * D + hf * 512
                            last = pe.matmul(py[:, hf * 512:(hf + 1) * 512], hhT[:, k, :], w_slot(dn_w, s_down, at, at + 512),
                                             start=(k == 0), stop=(k == KD - 1))
                    last.then_inc(dn, 1)

                with pe.Fori(0, total, 2) as g:
                    block_step(g, 0)
                    block_step(pe.snap(g + 1), 1)


def combine_phase(nc, io, keep, scr, outs):
    T = TILES
    LAST = T - 1
    R = 4
    with ExitStack() as ctx:
        sb = lambda name, shape, dt=F32: ctx.enter_context(nc.sbuf_tensor(name, shape, dt))
        ps = lambda name, shape: ctx.enter_context(nc.psum_tensor(name, shape, F32))
        sem = lambda name: ctx.enter_context(nc.semaphore(name))
        gate_p = sb("gate_p", [P, D])
        gate_s = sb("gate_s", [NSAMP, D])
        ln2 = sb("ln2", [P, 2, D])
        x1 = sb("x1_t", [P, R, D])
        y2 = sb("y2_t", [P, R, 2, D])
        ga = sb("ga", [P, R, D])
        z = sb("z4", [P, 2, D])
        zg = sb("zg", [P, 2, D])
        o = sb("o_t", [P, R, D])
        stats = sb("stats4", [P, 2, 6])
        mv = sb("mv4", [P, 2, 2])
        ve = sb("ve4", [P, 2])
        rstd = sb("rstd4", [P, 2])
        pg = [ps("pg0", [P, 512]), ps("pg1", [P, 512])]
        ln_in = sem("ln4_in")
        x_in = [sem("x4_in%d" % s) for s in range(R)]
        y_in = [sem("y4_in%d" % s) for s in range(R)]
        o_out = [sem("o_out%d" % s) for s in range(R)]
        bc_ps, bc_ev, ysum_rdy, ga_rdy, z_rdy, var_rdy, rs_rdy, o_rdy = (
            sem(n + "4") for n in ("bc_ps", "bc_ev", "ysum_rdy", "ga_rdy", "z_rdy", "var_rdy", "rs_rdy", "o_rdy"))
        tick = sem("tick4")
        op, os_ = outs[0][0], outs[1].rearrange("b l d -> (b l) d")

        def rows_of(t):
            return NSAMP if isinstance(t, int) and t == LAST else P

        def tiles(eng, body, ahead=None):
            def both(i, s, t):
                if ahead and not (isinstance(t, int) and t == LAST):
                    ahead(t + 1, (s + 1) % R, i + (s + 1) // R)
                body(t, s, i)
            if ahead:
                ahead(0, 0, 0)
            with eng.Fori(0, LAST // R - 1) as i:
                for s in range(R):
                    both(i, s, i * R + s)
            for t in range(LAST - R, T):
                both(t // R, t % R, t)

        with nc.Block() as block:
            @block.sync
            def _(sp):
                def load(t, s, i):
                    n = rows_of(t)
                    wait_apart(sp, z_rdy, t + 1, tick)
                    sp.dma_start(y2[0:n, s, :, :], scr["y2"][bass.ds(t * 2 * P, 2 * n), :].rearrange("(p k) d -> p k d", k=2)).then_inc(y_in[s], 16)
                    sp.dma_start(x1[0:n, s, :], scr["x1"][bass.ds(t * P, n), :]).then_inc(x_in[s], 16)
                tiles(sp, load)

            @block.scalar
            def _(act):
                act.dma_start(ln2[:, 0, :], row_bcast(io["ln_g"][0, 1], P)).then_inc(ln_in, 16)
                act.dma_start(ln2[:, 1, :], row_bcast(io["ln_b"][0, 1], P)).then_inc(ln_in, 16)
                for n in range(4):
                    p_, hf = n < 2, n % 2
                    act.wait_ge(bc_ps, n + 1)
                    act.activation((gate_p if p_ else gate_s)[:, hf * 512:(hf + 1) * 512],
                                   pg[hf][0:(P if p_ else NSAMP), :], ACT.Copy).then_inc(bc_ev, 1)

                def store(t, s, i):
                    n = rows_of(t)
                    wait_apart(act, o_rdy, t + 1, tick)
                    act.dma_start(os_ if n < P else op[bass.ds(t * P, n), :], o[0:n, s, :]).then_inc(o_out[s], 16)
                tiles(act, store)
                for s in range(R):
                    act.wait_ge(o_out[s], 16 * (LAST // R + (1 if s == 0 else 0)) + 16)

            @block.gpsimd
            def _(pool):
                pool.wait_ge(bc_ev, 4)

                def weigh(t, s, i):
                    n = rows_of(t)
                    gate = gate_s if n < P else gate_p
                    wait_apart(pool, y_in[s], 16 * i + 16, tick)
                    wait_apart(pool, z_rdy, t + 1, tick)
                    pool.tensor_tensor(ga[0:n, s, :], y2[0:n, s, 0, :], y2[0:n, s, 1, :], ALU.add).then_inc(ysum_rdy, 1)
                    wait_apart(pool, ysum_rdy, t + 1, tick)
                    pool.tensor_tensor(ga[0:n, s, :], ga[0:n, s, :], gate[0:n, :], ALU.mult).then_inc(ga_rdy, 1)

                def root(t, s, i):
                    n, h = rows_of(t), s % 2
                    wait_apart(pool, var_rdy, t + 1, tick)
                    pool.tensor_tensor(rstd[0:n, h:h + 1], ve[0:n, h:h + 1], keep["neg_half"][0:n, 0:1], ALU.pow).then_inc(rs_rdy, 1)
                tiles(pool, root, weigh)

            @block.tensor
            def _(pe):
                for n in range(4):
                    p_, hf = n < 2, n % 2
                    if n >= 2:
                        pe.wait_ge(bc_ev, n - 1)
                    sel = keep["sel_p"] if p_ else keep["sel_s"]
                    pe.matmul(pg[hf][0:(P if p_ else NSAMP), :], sel[:, :], keep["gate2"][:, hf * 512:(hf + 1) * 512],
                              start=True, stop=True).then_inc(bc_ps, 1)

            @block.vector
            def _(dve):
                dve.sem_inc(z_rdy, R)
                for s in range(R):
                    dve.sem_inc(o_out[s], 16)
                dve.wait_ge(ln_in, 32)

                def measure(t, s, i):
                    n, h = rows_of(t), s % 2
                    wait_apart(dve, ga_rdy, t + 1, tick)
                    wait_apart(dve, x_in[s], 16 * i + 16, tick)
                    dve.scalar_tensor_tensor(z[0:n, h, :], x1[0:n, s, :], ALPHA, ga[0:n, s, :], ALU.mult, ALU.add)
                    dve.drain().then_inc(z_rdy, 1)
                    for a in range(2):
                        dve.bn_stats(stats[0:n, a, :], z[0:n, h, a * 512:(a + 1) * 512])
                    dve.drain()
                    dve.bn_aggr(mv[0:n, h, :], stats[0:n, :, :])
                    dve.drain()
                    dve.tensor_scalar(ve[0:n, h:h + 1], mv[0:n, h, 1:2], LN_EPS, None, ALU.add).then_inc(var_rdy, 1)

                def normalise(t, s, i):
                    n, h = rows_of(t), s % 2
                    dve.scalar_tensor_tensor(zg[0:n, h, :], z[0:n, h, :], mv[0:n, h, 0:1], ln2[0:n, 0, :], ALU.subtract, ALU.mult)
                    wait_apart(dve, rs_rdy, t + 1, tick)
                    wait_apart(dve, o_out[s], 16 * i + 16, tick)
                    dve.drain()
                    dve.scalar_tensor_tensor(o[0:n, s, :], zg[0:n, h, :], rstd[0:n, h:h + 1], ln2[0:n, 1, :], ALU.mult, ALU.add).then_inc(o_rdy, 1)
                tiles(dve, normalise, measure)


def build(nc, io, outs):
    scr = {
        "mod": nc.dram_tensor("mod_scratch", [1 + DEC_B, 5 * D], F32).ap(),
        "y": nc.dram_tensor("y_scratch", [2 * HEADS, P, NTOK], F32).ap(),
        "x1": nc.dram_tensor("x1_scratch", [NTOK, D], F32).ap(),
        "u2": nc.dram_tensor("u2_scratch", [NTOK + 1, D], F32).ap(),
        "list": nc.dram_tensor("list_scratch", [(NE + 1) * CAP, 4], I32).ap(),
        "tab": nc.dram_tensor("tab_scratch", [P, 2], I32).ap(),
        "y2": nc.dram_tensor("y2_scratch", [2 * NTOK + P, D], F32).ap(),
    }
    with ExitStack() as ctx:
        sb = lambda name, shape, dt=F32: ctx.enter_context(nc.sbuf_tensor(name, shape, dt))
        keep = {
            "ident": sb("ident", [P, P]),
            "ones": sb("ones", [P, P]),
            "tri": sb("tri", [P, P]),
            "sel_p": sb("sel_p", [1 + DEC_B, P]),
            "sel_s": sb("sel_s", [1 + DEC_B, NSAMP]),
            "neg_half": sb("neg_half", [P, 8]),
            "cT": sb("cT", [P, KT, 1 + DEC_B]),
        }
        with ExitStack() as mctx:
            mb = lambda name, shape, dt=F32: mctx.enter_context(nc.sbuf_tensor(name, shape, dt))
            keep.update({
                "ident_i": mb("ident_i", [P, P], I32),
                "bmask": mb("bmask", [SS_TOK, SB]),
                "lmask": mb("lmask", [P, LEVELS, NCH * CH // 2], I32),
                "modT": mb("modT", [P, 2 * KT, 1 + DEC_B]),
                "head_par": mb("head_par", [P, HEADS, 6]),
                "A": mb("A", [P, NCH, CH]),
                "A_s": mb("A_s", [SS_TOK, SS_TOK]),
                "state": mb("state", [P, HEADS, P]),
                "conv_carry": mb("conv_carry", [P, HEADS, 2]),
                "conv_state_s": mb("conv_state_s", [P, HEADS, 2 * DEC_B]),
                "x_rows": mb("x_rows", [P, XT, D]),
                "xs_rows": mb("xs_rows", [SS_TOK, D]),
                "w_raw": mb("w_raw", [P, WS, KT, P]),
                "x_in": mctx.enter_context(nc.semaphore("x_in")),
                "raw_in": [mctx.enter_context(nc.semaphore("raw_in%d" % s)) for s in range(WS)],
            })
            modulation_phase(nc, io, keep, scr)
            mixer_phase(nc, io, keep, scr, outs)
        keep.update({
            "blk_tab": sb("blk_tab", [1, 2 * P], I32),
            "exp_tab": sb("exp_tab", [1, NE + 1], I32),
            "logits": sb("logits", [P, TILES, NG + NE]),
        })
        output_phase(nc, io, keep, scr)
        keep["gate2"] = sb("gate2", [1 + DEC_B, D])
        with ExitStack() as ectx:
            for name, slots, width, dt in (("gu_raw", RAW, 2 * KT * DE, F32), ("gu_hi", 2, 2 * KT * DE, F32R),
                                           ("gu_lo", 2, 2 * KT * DE, F32R), ("dn_w", RAW, DE // P * D, F32)):
                keep[name] = ectx.enter_context(nc.sbuf_tensor("w_" + name, [P, slots, width], dt))
            for name in ("wg_in", "wu_in", "wd_in", "gu_h", "gu_l"):
                keep[name] = ectx.enter_context(nc.semaphore(name))
            routing_phase(nc, io, keep, scr)
            expert_phase(nc, io, keep, scr)
        combine_phase(nc, io, keep, scr, outs)


def kernel(**inputs):
    import concourse.bacc as bacc
    from concourse.bass_utils import run_bass_kernel_spmd

    nc = bacc.Bacc("TRN2", target_bir_lowering=False, num_devices=1)
    arrays, args = {}, {}
    for name, value in inputs.items():
        a = np.ascontiguousarray(value)
        arrays["in_" + name] = a
        args[name] = nc.dram_tensor("in_" + name, a.shape, mybir.dt.from_np(a.dtype), kind="ExternalInput").ap()
    outs = [nc.dram_tensor("out_%d" % i, shape, mybir.dt.from_np(np.dtype(dtype)), kind="ExternalOutput").ap()
            for i, (shape, dtype) in enumerate(OUTS)]
    build(nc, args, outs)
    r = run_bass_kernel_spmd(nc, [arrays], core_ids=[0])
    return tuple(r.results[0]["out_%d" % i] for i in range(len(OUTS)))
```
